# Optimizing a Trainium2 kernel written in Bass

```python
import jax
import jax.numpy as jnp
from jax import lax
import numpy as np
import jax, jax.numpy as jnp

D_MODEL = 1024
BATCH = 1
SEQ = 512
DEPTH = 1

GRID_W = 64
CTX_LEN = 256
EPS = 1e-6
MLA_HEADS = 8
MLA_NOPE = 64
MLA_ROPE = 32
MLA_V_HEAD = 64
MLA_Q_LORA = 384
MLA_KV_LORA = 256
MLA_WIDTH = MLA_HEADS * MLA_V_HEAD
MLA_SCALE = (MLA_NOPE + MLA_ROPE) ** -0.5
ROPE_AXIS_DIM = MLA_ROPE // 2
ROPE_THETA = 10000.0
Q_BLOCK = 128
GLA_HEADS = 4
GLA_HEAD_K = 128
GLA_HEAD_V = 128
GLA_KEY = GLA_HEADS * GLA_HEAD_K
GLA_VALUE = GLA_HEADS * GLA_HEAD_V
GLA_QSCALE = GLA_HEAD_K ** -0.5
GATE_RANK = 16
GATE_NORM = 16.0
GLA_CHUNK = 64
D_FF = 2816
CONV_W = 3
IN_SPLITS = (MLA_Q_LORA, MLA_KV_LORA, MLA_ROPE, GLA_KEY, GLA_KEY, GLA_VALUE, GLA_VALUE, 2 * GATE_RANK, 2 * D_MODEL)
IN_COLS = sum(IN_SPLITS)


def rms_norm(x, g):
    xf = x.astype(jnp.float32)
    y = xf * lax.rsqrt(jnp.mean(xf * xf, axis=-1, keepdims=True) + EPS)
    return (y * g.astype(jnp.float32)).astype(x.dtype)

def modulate(h, shift, scale):
    return h * (1 + scale) + shift

def split_columns(z):
    offsets = [int(o) for o in np.cumsum(IN_SPLITS)[:-1]]
    return jnp.split(z, offsets, axis=-1)

def heads(z, n_heads):
    return z.reshape(z.shape[:-1] + (n_heads, z.shape[-1] // n_heads))

def axial_angles(length):
    t = jnp.arange(length, dtype=jnp.int32)
    row = (t // GRID_W).astype(jnp.float32)
    col = (t % GRID_W).astype(jnp.float32)
    inv_freq = ROPE_THETA ** (-jnp.arange(0, ROPE_AXIS_DIM, 2, dtype=jnp.float32) / ROPE_AXIS_DIM)
    return row[:, None] * inv_freq, col[:, None] * inv_freq

def rotate_axis(x, ang):
    x1, x2 = jnp.split(x, 2, axis=-1)
    cos, sin = jnp.cos(ang), jnp.sin(ang)
    return jnp.concatenate([x1 * cos - x2 * sin, x2 * cos + x1 * sin], axis=-1)

def rope_2d(x, ang_row, ang_col):
    xf = x.astype(jnp.float32)
    xr, xc = xf[..., :ROPE_AXIS_DIM], xf[..., ROPE_AXIS_DIM:]
    return jnp.concatenate([rotate_axis(xr, ang_row), rotate_axis(xc, ang_col)], axis=-1).astype(x.dtype)

def mla_queries(q_c, q_norm_g, w_uq):
    q = heads(rms_norm(q_c, q_norm_g) @ w_uq, MLA_HEADS)
    return q[..., :MLA_NOPE], q[..., MLA_NOPE:]

def mla_keys_values(kv_c, kv_norm_g, w_ukv):
    kv = heads(rms_norm(kv_c, kv_norm_g) @ w_ukv, MLA_HEADS)
    return kv[..., :MLA_NOPE], kv[..., MLA_NOPE:]

def attention(q_nope, q_rope, k_nope, k_rope, v):
    b, lq = q_nope.shape[:2]
    nb = lq // Q_BLOCK

    def blocks(z):
        return jnp.moveaxis(z.reshape((b, nb, Q_BLOCK) + z.shape[2:]), 1, 0)

    def one_block(qs):
        qn, qr = qs
        s = jnp.einsum('bqhd,bkhd->bhqk', qn, k_nope) + jnp.einsum('bqhr,bkr->bhqk', qr, k_rope)
        p = jax.nn.softmax(s.astype(jnp.float32) * MLA_SCALE, axis=-1).astype(v.dtype)
        return jnp.einsum('bhqk,bkhd->bqhd', p, v)

    o = lax.map(one_block, (blocks(q_nope), blocks(q_rope)))
    return jnp.moveaxis(o, 0, 1).reshape(b, lq, MLA_WIDTH)

def to_chunks(z):
    b, l, h, d = z.shape
    return z.reshape(b, l // GLA_CHUNK, GLA_CHUNK, h, d).transpose(0, 3, 1, 2, 4)

def from_chunks(z):
    b, h, n, c, d = z.shape
    return z.transpose(0, 2, 3, 1, 4).reshape(b, n * c, h, d)

def chunk_state_terms(kc, vc, b_cum):
    b_last = b_cum[..., -1:, :]
    u = jnp.einsum('bhncd,bhncv->bhndv', kc * jnp.exp(b_last - b_cum), vc)
    decay = jnp.exp(b_last[..., 0, :])
    return decay, u

def scan_states(decay, u, s0):
    def step(s, inp):
        d, du = inp
        return d[..., None] * s + du, s

    s_final, s_in = lax.scan(step, s0, (jnp.moveaxis(decay, 2, 0), jnp.moveaxis(u, 2, 0)))
    return s_final, jnp.moveaxis(s_in, 0, 2)

def gla_direction(q, k, v, g, s0):
    qc, kc, vc = (to_chunks(z.astype(jnp.float32)) for z in (q, k, v))
    b_cum = jnp.cumsum(to_chunks(g), axis=3)
    decay, u = chunk_state_terms(kc, vc, b_cum)
    s_final, s_in = scan_states(decay, u, s0)
    qe = qc * jnp.exp(b_cum)
    mask = jnp.tril(jnp.ones((GLA_CHUNK, GLA_CHUNK), jnp.float32))
    a = jnp.einsum('bhncd,bhnsd->bhncs', qe, kc * jnp.exp(-b_cum)) * mask
    o = jnp.einsum('bhncs,bhnsv->bhncv', a, vc) + jnp.einsum('bhncd,bhndv->bhncv', qe, s_in)
    return from_chunks(o), s_final

def gla_final_state(k, v, g, s0):
    kc, vc = to_chunks(k.astype(jnp.float32)), to_chunks(v.astype(jnp.float32))
    decay, u = chunk_state_terms(kc, vc, jnp.cumsum(to_chunks(g), axis=3))
    s_final, _ = scan_states(decay, u, s0)
    return s_final

def flip(z):
    return jnp.flip(z, axis=1)

def gla_bidirectional(q, k, v, g_f, g_b, s_f, s_b):
    o_f, s_f_out = gla_direction(q, k, v, g_f, s_f)
    o_b, s_b_out = gla_direction(flip(q), flip(k), flip(v), flip(g_b), s_b)
    return o_f + flip(o_b), s_f_out, s_b_out

def gla_inputs(gq, gk, gv, glow, w_decay, b_decay):
    lf, lb = glow[..., :GATE_RANK], glow[..., GATE_RANK:]
    g_f = jax.nn.log_sigmoid((lf @ w_decay[0] + b_decay[0]).astype(jnp.float32)) / GATE_NORM
    g_b = jax.nn.log_sigmoid((lb @ w_decay[1] + b_decay[1]).astype(jnp.float32)) / GATE_NORM
    return (heads(gq, GLA_HEADS) * GLA_QSCALE, heads(gk, GLA_HEADS), heads(gv, GLA_HEADS),
            heads(g_f, GLA_HEADS), heads(g_b, GLA_HEADS))

def gla_branch(o, r, norm_g, w_br):
    y = rms_norm(o, norm_g).reshape(o.shape[0], o.shape[1], GLA_VALUE).astype(r.dtype) * jax.nn.silu(r)
    return y @ w_br

def merge_branches(br_mla, br_gla, gate_logits, w_out):
    g = jax.nn.sigmoid(gate_logits.astype(jnp.float32)).astype(br_mla.dtype)
    g_mla, g_gla = jnp.split(g, 2, axis=-1)
    return (g_mla * br_mla + g_gla * br_gla) @ w_out

def token_mixer(h, hc, w_in, q_norm_g, w_uq, kv_norm_g, w_ukv, w_decay, b_decay, gla_norm_g,
                w_br_mla, w_br_gla, w_out, ang_row, ang_col, update_ctx):
    q_c, kv_c, k_rope, gq, gk, gv, gr, glow, gate_logits = split_columns(h @ w_in)
    q_cc, kv_cc, k_rope_c, gq_c, gk_c, gv_c, gr_c, glow_c, gate_logits_c = split_columns(hc @ w_in)

    k_nope_c, v_c = mla_keys_values(kv_cc, kv_norm_g, w_ukv)
    k_nope, v = mla_keys_values(kv_c, kv_norm_g, w_ukv)
    q_nope, q_rope = mla_queries(q_c, q_norm_g, w_uq)
    q_rope = rope_2d(q_rope, ang_row[:, None, :], ang_col[:, None, :])
    k_rope = rope_2d(k_rope, ang_row, ang_col)
    o_mla = attention(q_nope, q_rope,
                      jnp.concatenate([k_nope, k_nope_c], axis=1),
                      jnp.concatenate([k_rope, k_rope_c], axis=1),
                      jnp.concatenate([v, v_c], axis=1))

    b = h.shape[0]
    s0 = jnp.zeros((b, GLA_HEADS, GLA_HEAD_K, GLA_HEAD_V), jnp.float32)
    qg_c, kg_c, vg_c, gf_c, gb_c = gla_inputs(gq_c, gk_c, gv_c, glow_c, w_decay, b_decay)
    qg, kg, vg, gf, gb = gla_inputs(gq, gk, gv, glow, w_decay, b_decay)
    if update_ctx:
        o_gla_c, s_f, s_b = gla_bidirectional(qg_c, kg_c, vg_c, gf_c, gb_c, s0, s0)
    else:
        s_f = gla_final_state(kg_c, vg_c, gf_c, s0)
        s_b = gla_final_state(flip(kg_c), flip(vg_c), flip(gb_c), s0)
    o_gla, _, _ = gla_bidirectional(qg, kg, vg, gf, gb, s_f, s_b)

    out_lat = merge_branches(o_mla @ w_br_mla, gla_branch(o_gla, gr, gla_norm_g, w_br_gla), gate_logits, w_out)
    out_ctx = None
    if update_ctx:
        q_nope_c, q_rope_c = mla_queries(q_cc, q_norm_g, w_uq)
        o_mla_c = attention(q_nope_c, q_rope_c, k_nope_c, k_rope_c, v_c)
        out_ctx = merge_branches(o_mla_c @ w_br_mla, gla_branch(o_gla_c, gr_c, gla_norm_g, w_br_gla),
                                 gate_logits_c, w_out)
    return out_lat, out_ctx

def depthwise_conv_grid(u, w, bias, rows, cols):
    b, l, ch = u.shape
    grid = u.reshape(b, rows, cols, ch)
    y = lax.conv_general_dilated(grid, w[:, :, None, :].astype(u.dtype), (1, 1), 'SAME',
                                 dimension_numbers=('NHWC', 'HWIO', 'NHWC'), feature_group_count=ch)
    return y.reshape(b, l, ch) + bias

def conv_ffn(h, w_up, conv_w, conv_b, w_down, rows, cols):
    val, gate = jnp.split(h @ w_up, 2, axis=-1)
    gate = depthwise_conv_grid(gate, conv_w, conv_b, rows, cols)
    return (jax.nn.gelu(gate, approximate=False) * val) @ w_down

def first_inputs(seed: int = 0) -> dict:
    key = jax.random.key(seed)
    ks = jax.random.split(key, 24)
    f32 = jnp.float32

    def normal(k, shape, s=1.0):
        return s * jax.random.normal(k, shape, f32)

    def dense(k, shape, fan_in, gain=1.0):
        return normal(k, shape, gain * fan_in ** -0.5)

    def norm_gain(k, shape):
        return 1.0 + normal(k, shape, 0.05)

    return {
        "x": normal(ks[0], (BATCH, SEQ, D_MODEL)),
        "c": normal(ks[1], (BATCH, D_MODEL)),
        "ctx": normal(ks[2], (BATCH, CTX_LEN, D_MODEL)),
        "c_ctx": normal(ks[3], (D_MODEL,)),
        "w_ada": dense(ks[4], (DEPTH, D_MODEL, 6 * D_MODEL), D_MODEL, 0.5),
        "b_ada": normal(ks[5], (DEPTH, 6 * D_MODEL), 0.01),
        "norm1_g": norm_gain(ks[6], (DEPTH, D_MODEL)),
        "w_in": dense(ks[7], (DEPTH, D_MODEL, IN_COLS), D_MODEL),
        "q_norm_g": norm_gain(ks[8], (DEPTH, MLA_Q_LORA)),
        "w_uq": dense(ks[9], (DEPTH, MLA_Q_LORA, MLA_HEADS * (MLA_NOPE + MLA_ROPE)), MLA_Q_LORA),
        "kv_norm_g": norm_gain(ks[10], (DEPTH, MLA_KV_LORA)),
        "w_ukv": dense(ks[11], (DEPTH, MLA_KV_LORA, MLA_HEADS * (MLA_NOPE + MLA_V_HEAD)), MLA_KV_LORA),
        "gla_w_decay": dense(ks[12], (DEPTH, 2, GATE_RANK, GLA_KEY), GATE_RANK),
        "gla_b_decay": normal(ks[13], (DEPTH, 2, GLA_KEY), 0.1),
        "gla_norm_g": norm_gain(ks[14], (DEPTH, GLA_HEAD_V)),
        "w_br_mla": dense(ks[15], (DEPTH, MLA_WIDTH, D_MODEL), MLA_WIDTH),
        "w_br_gla": dense(ks[16], (DEPTH, GLA_VALUE, D_MODEL), GLA_VALUE),
        "w_out": dense(ks[17], (DEPTH, D_MODEL, D_MODEL), D_MODEL),
        "norm2_g": norm_gain(ks[18], (DEPTH, D_MODEL)),
        "w_up": dense(ks[19], (DEPTH, D_MODEL, 2 * D_FF), D_MODEL),
        "conv_w": dense(ks[20], (DEPTH, CONV_W, CONV_W, D_FF), CONV_W * CONV_W),
        "conv_b": normal(ks[21], (DEPTH, D_FF), 0.01),
        "w_down": dense(ks[22], (DEPTH, D_FF, D_MODEL), D_FF),
        "final_g": norm_gain(ks[23], (D_MODEL,)),
    }

def first_block(x, c, ctx, c_ctx, w_ada, b_ada, norm1_g, w_in, q_norm_g, w_uq, kv_norm_g, w_ukv,
              gla_w_decay, gla_b_decay, gla_norm_g, w_br_mla, w_br_gla, w_out, norm2_g, w_up,
              conv_w, conv_b, w_down, final_g):
    length = x.shape[1]
    rows = length // GRID_W
    ang_row, ang_col = axial_angles(length)
    x_lat, x_ctx = x, ctx
    for layer in range(DEPTH):
        update_ctx = layer + 1 < DEPTH
        mod = jax.nn.silu(c) @ w_ada[layer] + b_ada[layer]
        mod_c = jax.nn.silu(c_ctx) @ w_ada[layer] + b_ada[layer]
        sh1, sc1, gt1, sh2, sc2, gt2 = jnp.split(mod[:, None, :], 6, axis=-1)
        sh1c, sc1c, gt1c, sh2c, sc2c, gt2c = jnp.split(mod_c, 6, axis=-1)

        h = modulate(rms_norm(x_lat, norm1_g[layer]), sh1, sc1)
        hc = modulate(rms_norm(x_ctx, norm1_g[layer]), sh1c, sc1c)
        mix, mix_c = token_mixer(h, hc, w_in[layer], q_norm_g[layer], w_uq[layer], kv_norm_g[layer],
                                 w_ukv[layer], gla_w_decay[layer], gla_b_decay[layer], gla_norm_g[layer],
                                 w_br_mla[layer], w_br_gla[layer], w_out[layer], ang_row, ang_col, update_ctx)
        x_lat = x_lat + gt1 * mix
        h = modulate(rms_norm(x_lat, norm2_g[layer]), sh2, sc2)
        x_lat = x_lat + gt2 * conv_ffn(h, w_up[layer], conv_w[layer], conv_b[layer], w_down[layer], rows, GRID_W)
        if update_ctx:
            x_ctx = x_ctx + gt1c * mix_c
            hc = modulate(rms_norm(x_ctx, norm2_g[layer]), sh2c, sc2c)
            x_ctx = x_ctx + gt2c * conv_ffn(hc, w_up[layer], conv_w[layer], conv_b[layer], w_down[layer],
                                            1, x_ctx.shape[1])
    return rms_norm(x_lat, final_g)


DEPTH_2 = 4

N_MIXERS = 3
N_A = (DEPTH_2 + 2) // 3
N_B = (DEPTH_2 + 1) // 3
N_C = DEPTH_2 // 3
D_RNN = 1280
A_HEADS = 16
A_HEAD_DIM = D_RNN // A_HEADS
A_CONV = 4
LRU_C = 8.0
D_SGU = D_MODEL
SGU_CHUNK = 128
SGU_GROUPS = 8
SGU_GROUP_DIM = D_SGU // SGU_GROUPS
D_CONV = D_MODEL
C_CONV = 3
D_FF_2 = 4 * D_MODEL


def _rmsnorm(x, g):
    x32 = x.astype(jnp.float32)
    y = x32 * lax.rsqrt(jnp.mean(x32 * x32, axis=-1, keepdims=True) + EPS)
    return y.astype(x.dtype) * g

def _causal_dwconv(x, w):
    k = w.shape[0]
    return lax.conv_general_dilated(
        x, w[:, None, :].astype(x.dtype), window_strides=(1,),
        padding=[(k - 1, 0)], dimension_numbers=("NWC", "WIO", "NWC"),
        feature_group_count=x.shape[-1])

def _lru_combine(left, right):
    a_l, b_l = left
    a_r, b_r = right
    return a_l * a_r, a_r * b_l + b_r

def _rglru_mixer(h, w_in, conv_w, conv_b, gate_a_w, gate_a_b, gate_x_w, gate_x_b, lam, w_out):
    b, s, _ = h.shape
    gate, xr = jnp.split(h @ w_in, 2, axis=-1)
    gate = jax.nn.gelu(gate)
    xr = _causal_dwconv(xr, conv_w) + conv_b
    xh = xr.reshape(b, s, A_HEADS, A_HEAD_DIM)
    r = jax.nn.sigmoid(jnp.einsum("bshi,hij->bshj", xh, gate_a_w).reshape(b, s, D_RNN) + gate_a_b)
    ig = jax.nn.sigmoid(jnp.einsum("bshi,hij->bshj", xh, gate_x_w).reshape(b, s, D_RNN) + gate_x_b)
    log_a = -LRU_C * r.astype(jnp.float32) * jax.nn.softplus(-lam.astype(jnp.float32))
    a = jnp.exp(log_a)
    u = jnp.sqrt(-jnp.expm1(2.0 * log_a)) * (ig * xr).astype(jnp.float32)
    _, hs = lax.associative_scan(_lru_combine, (a, u), axis=1)
    return (hs.astype(h.dtype) * gate) @ w_out

def _sgu_mixer(h, w_in, norm_g, w_s, s_bias, w_out):
    b, s, _ = h.shape
    z = jax.nn.gelu(h @ w_in)
    u, v = jnp.split(z, 2, axis=-1)
    v = _rmsnorm(v, norm_g)
    n_chunks = s // SGU_CHUNK
    v = v.reshape(b, n_chunks, SGU_CHUNK, SGU_GROUPS, SGU_GROUP_DIM)
    causal = jnp.tril(jnp.ones((SGU_CHUNK, SGU_CHUNK), dtype=bool))
    w_causal = jnp.where(causal[None], w_s, jnp.zeros((), w_s.dtype))
    mixed = jnp.einsum("gts,bnsgc->bntgc", w_causal, v) + s_bias.T[None, None, :, :, None]
    y = u * mixed.reshape(b, s, D_SGU)
    return y @ w_out

def _shortconv_mixer(h, w_in, conv_w, w_out):
    gb, gc, xv = jnp.split(h @ w_in, 3, axis=-1)
    y = gb * _causal_dwconv(gc * xv, conv_w)
    return y @ w_out

def _sqrelu_mlp(h, w1, w2):
    return jnp.square(jax.nn.relu(h @ w1)) @ w2

def second_inputs(seed: int = 0) -> dict:
    key = jax.random.key(seed)
    ks = jax.random.split(key, 24)
    f32 = jnp.float32

    def w(k, shape, fan_in):
        return jax.random.normal(k, shape, f32) * (fan_in ** -0.5)

    def gain(k, shape):
        return 1.0 + 0.1 * jax.random.normal(k, shape, f32)

    def bias(k, shape, scale=0.1):
        return scale * jax.random.normal(k, shape, f32)

    a_c = jax.random.uniform(ks[11], (N_A, D_RNN), f32, minval=0.9, maxval=0.999)
    a0 = a_c ** (1.0 / LRU_C)
    a_lambda = jnp.log(a0) - jnp.log1p(-a0)

    return {
        "x": jax.random.normal(ks[0], (BATCH, SEQ, D_MODEL), f32),
        "norm_mix_g": gain(ks[1], (DEPTH_2, D_MODEL)),
        "norm_mlp_g": gain(ks[2], (DEPTH_2, D_MODEL)),
        "final_norm_g": gain(ks[3], (D_MODEL,)),
        "a_w_in": w(ks[4], (N_A, D_MODEL, 2 * D_RNN), D_MODEL),
        "a_conv_w": w(ks[5], (N_A, A_CONV, D_RNN), A_CONV),
        "a_conv_b": bias(ks[6], (N_A, D_RNN)),
        "a_gate_a_w": w(ks[7], (N_A, A_HEADS, A_HEAD_DIM, A_HEAD_DIM), A_HEAD_DIM),
        "a_gate_a_b": bias(ks[8], (N_A, D_RNN)),
        "a_gate_x_w": w(ks[9], (N_A, A_HEADS, A_HEAD_DIM, A_HEAD_DIM), A_HEAD_DIM),
        "a_gate_x_b": bias(ks[10], (N_A, D_RNN)),
        "a_lambda": a_lambda,
        "a_w_out": w(ks[12], (N_A, D_RNN, D_MODEL), D_RNN),
        "b_w_in": w(ks[13], (N_B, D_MODEL, 2 * D_SGU), D_MODEL),
        "b_norm_g": gain(ks[14], (N_B, D_SGU)),
        "b_w_s": w(ks[15], (N_B, SGU_GROUPS, SGU_CHUNK, SGU_CHUNK), SGU_CHUNK),
        "b_s_bias": gain(ks[16], (N_B, SGU_GROUPS, SGU_CHUNK)),
        "b_w_out": w(ks[17], (N_B, D_SGU, D_MODEL), D_SGU),
        "c_w_in": w(ks[18], (N_C, D_MODEL, 3 * D_CONV), D_MODEL),
        "c_conv_w": w(ks[19], (N_C, C_CONV, D_CONV), C_CONV),
        "c_w_out": w(ks[20], (N_C, D_CONV, D_MODEL), D_CONV),
        "mlp_w1": w(ks[21], (DEPTH_2, D_MODEL, D_FF_2), D_MODEL),
        "mlp_w2": w(ks[22], (DEPTH_2, D_FF_2, D_MODEL), D_FF_2),
    }

def second_block(x, norm_mix_g, norm_mlp_g, final_norm_g,
              a_w_in, a_conv_w, a_conv_b, a_gate_a_w, a_gate_a_b, a_gate_x_w, a_gate_x_b, a_lambda, a_w_out,
              b_w_in, b_norm_g, b_w_s, b_s_bias, b_w_out,
              c_w_in, c_conv_w, c_w_out,
              mlp_w1, mlp_w2):
    for i in range(DEPTH_2):
        kind, j = i % N_MIXERS, i // N_MIXERS
        h = _rmsnorm(x, norm_mix_g[i])
        if kind == 0:
            mix = _rglru_mixer(h, a_w_in[j], a_conv_w[j], a_conv_b[j], a_gate_a_w[j], a_gate_a_b[j],
                               a_gate_x_w[j], a_gate_x_b[j], a_lambda[j], a_w_out[j])
        elif kind == 1:
            mix = _sgu_mixer(h, b_w_in[j], b_norm_g[j], b_w_s[j], b_s_bias[j], b_w_out[j])
        else:
            mix = _shortconv_mixer(h, c_w_in[j], c_conv_w[j], c_w_out[j])
        x = x + mix
        x = x + _sqrelu_mlp(_rmsnorm(x, norm_mlp_g[i]), mlp_w1[i], mlp_w2[i])
    return _rmsnorm(x, final_norm_g)


def setup_inputs(seed=0):
    out = dict(first_inputs(seed))
    for name, value in second_inputs(seed + 1).items():
        if name != "x":
            out[name + "_2"] = value
    return out


def reference(
    x, c, ctx, c_ctx, w_ada, b_ada, norm1_g, w_in, q_norm_g, w_uq, kv_norm_g, w_ukv,
    gla_w_decay, gla_b_decay, gla_norm_g, w_br_mla, w_br_gla, w_out, norm2_g, w_up, conv_w,
    conv_b, w_down, final_g, norm_mix_g_2, norm_mlp_g_2, final_norm_g_2, a_w_in_2, a_conv_w_2,
    a_conv_b_2, a_gate_a_w_2, a_gate_a_b_2, a_gate_x_w_2, a_gate_x_b_2, a_lambda_2, a_w_out_2,
    b_w_in_2, b_norm_g_2, b_w_s_2, b_s_bias_2, b_w_out_2, c_w_in_2, c_conv_w_2, c_w_out_2,
    mlp_w1_2, mlp_w2_2,
):
    x = first_block(
        x, c, ctx, c_ctx, w_ada, b_ada, norm1_g, w_in, q_norm_g, w_uq, kv_norm_g, w_ukv,
        gla_w_decay, gla_b_decay, gla_norm_g, w_br_mla, w_br_gla, w_out, norm2_g, w_up, conv_w,
        conv_b, w_down, final_g,
    )
    return second_block(
        x, norm_mix_g_2, norm_mlp_g_2, final_norm_g_2, a_w_in_2, a_conv_w_2, a_conv_b_2,
        a_gate_a_w_2, a_gate_a_b_2, a_gate_x_w_2, a_gate_x_b_2, a_lambda_2, a_w_out_2, b_w_in_2,
        b_norm_g_2, b_w_s_2, b_s_bias_2, b_w_out_2, c_w_in_2, c_conv_w_2, c_w_out_2, mlp_w1_2,
        mlp_w2_2,
    )


_drawn_inputs = setup_inputs


def setup_inputs(seed=0):
    import zlib

    import numpy as np

    out = dict(_drawn_inputs(seed))
    spreads = {}
    factors = {'b_ada': 2.752,
     'norm1_g': 3.047,
     'q_norm_g': 8.0,
     'kv_norm_g': 7.597,
     'gla_b_decay': 6.361,
     'gla_norm_g': 6.332,
     'conv_b': 39.556,
     'a_gate_a_b_2': 3.757,
     'norm2_g': 7.045}
    for name, (base, spread) in spreads.items():
        noise = np.random.default_rng([zlib.crc32(name.encode()), seed]).standard_normal(out[name].shape)
        drawn = base * np.exp(spread * noise) if base else spread * noise
        out[name] = jnp.asarray(drawn.astype(out[name].dtype))
    for name, factor in factors.items():
        out[name] = (out[name] * factor).astype(out[name].dtype)
    return out
```

```python
from contextlib import ExitStack

import numpy as np

import concourse.bass as bass
from concourse import mybir

F32 = mybir.dt.float32
F32R = mybir.dt.float32r
ALU = mybir.AluOpType
ACT = mybir.ActivationFunctionType
AX = mybir.AxisListType

P = 128
D = 1024
KT = D // P
T = 512
C = 256
TC = T + C
EPS = 1e-6
SLOTS = 4
BANKS = 4
TP = 8

LAYERS = 4
RT = 1280 // P
HALF = RT // 2
FF2 = 4 * D // P
UG = FF2 // 8
A_TAPS = 4
C_TAPS = 3
SG = 8


def block_diagonal_inputs(m):
    first = (P * m // 80) * 80
    last = ((P * m + P - 1) // 80 + 1) * 80 - 1
    return list(range(first // P, last // P + 1))


BD = [block_diagonal_inputs(m) for m in range(RT)]
BD_HALF_PANELS = -(-2 * sum(len(BD[m]) for m in range(HALF)) // TP)

QL, KVL = 384 // P, 256 // P
HEADS, NOPE, ROPE = 8, 64, 32
QK = NOPE + ROPE
MLA_SCALE = float(QK) ** -0.5
GH = 4
GLA_SCALE = float(P) ** -0.5
GATE_NORM = 16.0
CHUNK = 64
NCH = TC // CHUNK
FF1 = 2816 // P
FF1_GROUPS = [range(0, 8), range(8, 16), range(16, FF1)]
GRID_W, GRID_H = 64, T // 64
ADA_SLOTS = 16
KB = TC // P

OUT_MISC = 0
OUT_KV = OUT_MISC + 2
OUT_Q = OUT_KV + 2 * KVL
OUT_GV = OUT_Q + QL
OUT_GLA = OUT_GV + 4
GLA_OUTS = 19


def out_gla_project(h):
    return OUT_GLA + 4 * h + GLA_OUTS * max(h - 1, 0)


def out_gla(h):
    return OUT_GLA + 4 * min(h + 2, GH) + GLA_OUTS * h


OUT_QNORM = out_gla(GH - 1) + GLA_OUTS
OUT_QH = OUT_QNORM + 1
OUT_KVNORM = OUT_QH + HEADS
OUT_KH = OUT_KVNORM + 2
OUT_V = OUT_KH + HEADS
OUT_ATT = OUT_V + KB
OUT_ATT += OUT_ATT % 2
UNITS = 4 * HEADS


def out_scores(u):
    return OUT_ATT + (0 if u == 0 else 2 + 4 * (u - 1))


def out_turned(u):
    return OUT_ATT + (4 + 4 * u if u < UNITS - 1 else 2 + 4 * u)


OUT_MERGE = OUT_ATT + 4 * UNITS
OUT_MIX = OUT_MERGE + 4 * KT
OUT_FF = OUT_MIX + KT


def out_ff_up(group):
    return OUT_FF + sum(2 * len(FF1_GROUPS[g]) for g in range(group)) + KT * max(group - 1, 0)


def out_ff_down(group):
    return OUT_FF + sum(2 * len(FF1_GROUPS[g]) for g in range(min(group + 2, 3))) + KT * group


FIRST_OUTS = out_ff_down(2) + KT
FIRST_NORMS = 4


class Turn:

    def __init__(self):
        self.out = 0
        self.it = None
        self.rate = 0

    def value(self, count, per_turn=None):
        if self.it is None:
            return count
        return self.it * (self.rate if per_turn is None else per_turn) + count


def build(nc, io, names, upto=None, start_x=False):
    n_panels = io["weights"].shape[0]
    with ExitStack() as whole:
        def sem(name):
            return whole.enter_context(nc.semaphore(name))

        def sb(name, shape, dt=F32):
            return whole.enter_context(nc.sbuf_tensor(name, shape, dt))

        x = sb("x", [P, KT, T])
        h_hi = sb("h_hi", [P, KT, T], F32R)
        h_lo = sb("h_lo", [P, KT, T], F32R)
        w_raw = sb("w_raw", [P, SLOTS, TP * P])
        w_hi = sb("w_hi", [P, SLOTS, TP * P], F32R)
        w_lo = sb("w_lo", [P, SLOTS, TP * P], F32R)
        table = sb("table", [P, names["width"]])
        ones = sb("ones", [P, P])
        sgu_mask = sb("sgu_mask", [P, P])
        square = sb("square", [P, 2, T])
        square_sum = sb("square_sum", [P, T])
        root = sb("root", [P, T])
        rstd = sb("rstd", [P, T])

        def col(name, i=0):
            return table[:, names[name] + i:names[name] + i + 1]

        memory = {}
        def overlay(part, **tensors):
            with ExitStack() as stage:
                for name, (shape, dt) in tensors.items():
                    memory[name] = stage.enter_context(nc.sbuf_tensor(f"{part}_{name}", shape, dt))

        overlay("rec", rec_in=([P, 3, A_TAPS - 1 + T], F32), rec_x=([P, RT, T], F32),
                rec_hi=([P, RT, T], F32R), rec_lo=([P, RT, T], F32R),
                rec_a=([P, HALF, T], F32), rec_u=([P, HALF, T], F32), rec_gate=([P, HALF, T], F32),
                rec_cl=([P, 4, RT], F32))
        overlay("mlp", hid_hi=([P, 2, 8, T], F32R), hid_lo=([P, 2, 8, T], F32R),
                relu=([P, 4, T], F32), hidden=([P, 4, T], F32))
        overlay("sgu", sgu_v=([P, 4, D], F32), sgu_u=([P, KT, T], F32), sgu_w=([P, SG, P], F32),
                sgu_bias=([P, SG, P], F32), sgu_hi=([P, KT, T], F32R), sgu_lo=([P, KT, T], F32R),
                sgu_stat=([P, 4, 4], F32), sgu_sq=([P, D], F32), sgu_y=([P, 2, T], F32))
        overlay("conv", cnv_g=([P, 2, T], F32), cnv_x=([P, 2, T], F32), cnv_p=([P, 2, C_TAPS - 1 + T], F32),
                cnv_c=([P, 2, T], F32), cnv_b=([P, 2, T], F32),
                cnv_hi=([P, KT, T], F32R), cnv_lo=([P, KT, T], F32R))
        M = memory

        acc = whole.enter_context(nc.psum_tensor("acc", [P, BANKS, T], F32))
        stat = whole.enter_context(nc.psum_tensor("stat", [P, T], F32))
        side = whole.enter_context(nc.psum_tensor("side", [P, 3, T], F32))

        raw_in = [sem(f"raw_in{s}") for s in range(SLOTS)]
        hi_made = sem("hi_made")
        panel_made = sem("panel_made")
        panel_used = sem("panel_used")
        out_made = sem("out_made")
        out_taken = [sem(f"out_taken{b}") for b in range(BANKS)]
        const_in = sem("const_in")
        x_in = sem("x_in")
        squared = sem("squared")
        h_hi_made = sem("h_hi_made")
        summed = sem("summed")
        h_lo_made = sem("h_lo_made")
        stat_made = sem("stat_made")
        root_made = sem("root_made")
        rstd_made = sem("rstd_made")
        hid_hi_made = sem("hid_hi_made")
        hid_lo_made = sem("hid_lo_made")
        rec_zeroed = sem("rec_zeroed")
        rec_cl_exp = sem("rec_cl_exp")
        rec_cl_ln = sem("rec_cl_ln")
        rec_cl_made = sem("rec_cl_made")
        rec_conv = sem("rec_conv")
        rec_hi_made = sem("rec_hi_made")
        rec_lo_made = sem("rec_lo_made")
        rec_xi_made = sem("rec_xi_made")
        rec_tanh = sem("rec_tanh")
        rec_decay = sem("rec_decay")
        rec_ratio = sem("rec_ratio")
        rec_sqrt = sem("rec_sqrt")
        rec_scan = sem("rec_scan")
        rec_gelu = sem("rec_gelu")
        rec_y = sem("rec_y")
        sgu_in = sem("sgu_in")
        sgu_masked = sem("sgu_masked")
        sgu_col = sem("sgu_col")
        sgu_col_taken = sem("sgu_col_taken")
        sgu_v_made = sem("sgu_v_made")
        sgu_sq_made = sem("sgu_sq_made")
        sgu_root = sem("sgu_root")
        sgu_norm = sem("sgu_norm")
        sgu_v_norm = sem("sgu_v_norm")
        sgu_u_made = sem("sgu_u_made")
        sgu_biased = sem("sgu_biased")
        sgu_y_made = sem("sgu_y_made")
        sgu_hi_made = sem("sgu_hi_made")
        sgu_lo_made = sem("sgu_lo_made")
        cnv_zeroed = sem("cnv_zeroed")
        cnv_step = sem("cnv_step")
        cnv_y = sem("cnv_y")
        cnv_hi_made = sem("cnv_hi_made")
        cnv_lo_made = sem("cnv_lo_made")
        scaled = sem("scaled")
        result_out = sem("result_out")

        A_OUTS = 2 * (HALF + 2 * HALF + HALF) + KT
        B_OUTS = 8 + KT + KT + KT
        C_OUTS = 3 * KT + KT
        M_OUTS = FF2 + UG * KT
        first_out = {}
        n = 0
        if not start_x:
            n = FIRST_OUTS
        for layer in range(LAYERS):
            first_out["mix", layer] = n
            n += (A_OUTS, B_OUTS, C_OUTS)[layer % 3]
            first_out["mlp", layer] = n
            n += M_OUTS
        last_norm = n
        CONSTS = 48
        NORM0 = 0 if start_x else FIRST_NORMS
        H_SKIP = 0 if start_x else KT

        def bank(o):
            return acc[:, o % BANKS, :]

        def wait_made(eng, o, turn=None):
            eng.wait_ge(out_made, turn.value(o + 1) if turn else o + 1)

        def wait_taken(eng, o, turn=None):
            v = o // BANKS + 1
            eng.wait_ge(out_taken[o % BANKS], turn.value(v, turn.rate // BANKS) if turn else v)

        def mix_down(layer):
            return first_out["mlp", layer] - KT

        def mlp_down(layer):
            return first_out["mlp", layer] + M_OUTS - KT

        def rec_x_lo(inst, k):
            half = k // HALF
            return 2 * RT * inst + k + HALF * half + 1

        def rec_y_lo(inst, k):
            return 2 * RT * inst + k + HALF * (1 + k // HALF) + 1


        with ExitStack() as first:
            def fb(name, shape, dt=F32):
                return first.enter_context(nc.sbuf_tensor(name, shape, dt))

            mod = fb("mod", [P, 6 * KT, 2])
            gain1 = fb("gain1", [P, 2, KT])
            gain2 = fb("gain2", [P, KT])
            cvec = fb("cvec", [P, KT, 2])
            identity = fb("identity", [P, P])
            rope = fb("rope", [P, T])
            main = ExitStack()
            og_hi = main.enter_context(nc.sbuf_tensor("og_hi", [P, GH, T], F32R))
            og_lo = main.enter_context(nc.sbuf_tensor("og_lo", [P, GH, T], F32R))
            with ExitStack() as part:
                def fa(name, shape, dt=F32):
                    return part.enter_context(nc.sbuf_tensor(name, shape, dt))
                ada = fa("ada", [P, ADA_SLOTS, TP * P])
            with ExitStack() as part:
                hc_hi = fa("hc_hi", [P, KT, C], F32R)
                hc_lo = fa("hc_lo", [P, KT, C], F32R)
                glow = fa("glow", [64, TC])
                v_tok = fa("v_tok", [P, KB, GH * P])
                gk = fa("gk", [P, 2, TC])
                gq = fa("gq", [P, 2, T])
                gr = fa("gr", [P, 2, T])
                decay_w = fa("decay_w", [48, GH * P])
                intra_mask = fa("intra_mask", [P, 2, P])
                reset = fa("reset", [P, TC + 1])
                with ExitStack() as norm_part:
                    xc = norm_part.enter_context(nc.sbuf_tensor("xc", [P, KT, C], F32))
                    n_full = norm_part.enter_context(nc.sbuf_tensor("n_full", [P, 2, T], F32))
                    n_scaled = norm_part.enter_context(nc.sbuf_tensor("n_scaled", [P, 2, T], F32))
                zb = fa("zb", [P, TC])
                ln = fa("ln", [P, TC])
                b_cum = fa("b_cum", [P, TC])
                kd = fa("kd", [P, TC])
                qe = fa("qe", [P, T])
                ke = fa("ke", [P, T])
                kd_tok = fa("kd_tok", [P, KB, P])
                a_t = fa("a_t", [P, 4, P])
                state = fa("state", [P, T // CHUNK, P])
                state_c = fa("state_c", [P, 4, P])
                chunk_decay = fa("chunk_decay", [P, NCH])
            with ExitStack() as part:
                om_hi = fa("om_hi", [P, 4, T], F32R)
                om_lo = fa("om_lo", [P, 4, T], F32R)
                with ExitStack() as att:
                    def ft(name, shape, dt=F32):
                        return att.enter_context(nc.sbuf_tensor(name, shape, dt))
                    q_t = ft("q_t", [P, HEADS, T])
                    k_t = ft("k_t", [P, HEADS, TC])
                    v_mla = ft("v_mla", [P, KB, T])
                    prob = ft("prob", [P, 2, TC])
                    att_stat = ft("att_stat", [P, 2, 8])
                with ExitStack() as att:
                    mg_hi = ft("mg_hi", [P, KT, T], F32R)
                    mg_lo = ft("mg_lo", [P, KT, T], F32R)
                    gate_m = ft("gate_m", [P, 2, T])
                    gate_g = ft("gate_g", [P, 2, T])
            main.close()
            with ExitStack() as part:
                f2_full = fa("f2_full", [P, 2, T])
                f2_scaled = fa("f2_scaled", [P, 2, T])
                ff_hi = fa("ff_hi", [P, 2, 8, T], F32R)
                ff_lo = fa("ff_lo", [P, 2, 8, T], F32R)
                ff_pad = fa("ff_pad", [P, 2, GRID_H + 2, GRID_W + 2])
                ff_conv = fa("ff_conv", [P, 2, T])
                ff_hid = fa("ff_hid", [P, 2, T])
        x_flat = x[:, :, :].rearrange("p k t -> p (k t)")
        z_kv = x_flat[:, 0:KVL * TC].rearrange("p (k t) -> p k t", k=KVL)
        z_q = x_flat[:, KVL * TC:KVL * TC + QL * T].rearrange("p (k t) -> p k t", k=QL)
        k_rope = x_flat[64:96, KVL * TC + QL * T:KVL * TC + QL * T + TC]
        p_t = x_flat[:, 0:KB * T].rearrange("p (b q) -> p b q", b=KB)
        o_norm = zb[:, 0:T]
        spread = [prob[:, :, :].rearrange("p a t -> p (a t)")]

        ada_in = [sem(f"ada_in{s}") for s in range(ADA_SLOTS)]
        ada_used = sem("ada_used")
        small_in = sem("small_in")
        mix_in = sem("mix_in")
        silu_made = sem("silu_made")
        mod_made = sem("mod_made")
        dve_chain = sem("dve_chain")
        act_chain = sem("act_chain")
        gains_made = sem("gains_made")
        n_scaled_made = sem("n_scaled_made")
        side_made = sem("side_made")
        side_taken = sem("side_taken")
        gla_ln = sem("gla_ln")
        gla_b = sem("gla_b")
        gla_e = sem("gla_e")
        gla_d = sem("gla_d")
        gla_ed = sem("gla_ed")
        gla_qk = sem("gla_qk")
        gla_kd = sem("gla_kd")
        gla_s = sem("gla_s")
        gla_o = sem("gla_o")
        gla_sq = sem("gla_sq")
        gla_y = sem("gla_y")
        og_hi_made = sem("og_hi_made")
        og_lo_made = sem("og_lo_made")
        lr_sq = sem("lr_sq")
        lr_scaled = sem("lr_scaled")
        lr_hi = sem("lr_hi")
        lr_lo = sem("lr_lo")
        k_spread = sem("k_spread")
        att_max = sem("att_max")
        att_exp = sem("att_exp")
        att_prob = sem("att_prob")
        att_o = sem("att_o")
        om_hi_made = sem("om_hi_made")
        om_lo_made = sem("om_lo_made")
        mg_made = sem("mg_made")
        mg_hi_made = sem("mg_hi_made")
        mg_lo_made = sem("mg_lo_made")
        pads_made = sem("pads_made")
        ff_conved = sem("ff_conved")
        ff_gelu = sem("ff_gelu")
        ff_hi_made = sem("ff_hi_made")
        ff_lo_made = sem("ff_lo_made")
        x_normed = sem("x_normed")

        def sums(norm):
            return C if norm == 1 else T

        def lin(n):
            return n // 2, n % 2

        def rev(ap, d, a, b):
            return ap[:, a:b] if d == 0 else ap[:, a:b][:, ::-1]

        def chunk_cols(d, i):
            if i < 4:
                n = 8 + (i if d == 0 else 3 - i)
            else:
                n = i - 4 if d == 0 else 11 - i
            return n

        def first_block_sp(sp):
            for m in range(6 * KT):
                if m >= ADA_SLOTS:
                    sp.wait_ge(ada_used, m - ADA_SLOTS + 1)
                sp.dma_start(ada[:, m % ADA_SLOTS, :], io["ada"][m].rearrange("p t c -> p (t c)")).then_inc(ada_in[m % ADA_SLOTS], 16)

        def first_block_pe(pe, turn, next_tile, mm, begin_out, project, tile, norm_sum, skip_to_panel):
            def both(parts_a, parts_b, wa, wb, ready=None):
                a, b = begin_out(), begin_out()
                n = len(parts_a)
                for k in range(n):
                    slot, cols = next_tile()
                    if ready:
                        ready(k)
                    (ah, al), (bh, bl) = parts_a[k], parts_b[k]
                    mm(a[:, 0:wa], w_hi[:, slot, cols], ah, k == 0, False)
                    mm(a[:, 0:wa], w_hi[:, slot, cols], al, False, False)
                    mm(b[:, 0:wb], w_hi[:, slot, cols], bh, k == 0, False)
                    mm(b[:, 0:wb], w_hi[:, slot, cols], bl, False, False)
                    ia = mm(a[:, 0:wa], w_lo[:, slot, cols], ah, False, k == n - 1)
                    if k == n - 1:
                        ia.then_inc(out_made, 1)
                    ib = mm(b[:, 0:wb], w_lo[:, slot, cols], bh, False, k == n - 1)
                ib.then_inc(out_made, 1)

            h_parts = [(h_hi[:, k, :], h_lo[:, k, :]) for k in range(KT)]
            hc_parts = [(hc_hi[:, k, :], hc_lo[:, k, :]) for k in range(KT)]
            pe.wait_ge(small_in, 32)
            pe.wait_ge(silu_made, 1)
            for m in range(6 * KT):
                pe.wait_ge(ada_in[m % ADA_SLOTS], 16 * (m // ADA_SLOTS + 1))
                for k in range(KT):
                    ins = pe.matmul(side[:, 0, 2 * m:2 * m + 2], ada[:, m % ADA_SLOTS, P * k:P * k + P], cvec[:, k, :],
                                    start=(k == 0), stop=(k == KT - 1))
                ins.then_inc(ada_used, 1)
            norm_sum(0)
            norm_sum(1)
            pe.wait_ge(h_lo_made, 2 * KT)
            both(h_parts, hc_parts, T, C)
            for m in range(KVL):
                both(h_parts, hc_parts, T, C)
            for m in range(QL):
                project(h_parts)
            outs = [begin_out() for _ in range(4)] + [side[:, 1, :], side[:, 2, :]]
            for k in range(KT):
                if k % 2 == 0:
                    slot, _ = next_tile()
                    tile[0] += TP - 1
                cols = slice(T * (k % 2), T * (k % 2) + T)
                for tb in range(KB):
                    hi, lo = (h_hi, h_lo) if tb < 4 else (hc_hi, hc_lo)
                    tok = slice(P * (tb % 4), P * (tb % 4) + P)
                    mm(outs[tb], hi[:, k, tok], w_hi[:, slot, cols], k == 0, False)
                    mm(outs[tb], hi[:, k, tok], w_lo[:, slot, cols], False, False)
                    ins = mm(outs[tb], lo[:, k, tok], w_hi[:, slot, cols], False, k == KT - 1)
                    if k == KT - 1 and tb < 4:
                        ins.then_inc(out_made, 1)
            ins.then_inc(side_made, 1)

            def gla_project(h):
                assert turn.out == out_gla_project(h)
                both(h_parts, hc_parts, T, C)
                project(h_parts)
                project(h_parts)

            def gla(h):
                assert turn.out == out_gla(h)
                hs = slice(P * h, P * h + P)
                o = side[:, h % 2, :]
                if h == 0:
                    wait_taken(pe, OUT_MISC + 1)
                    pe.wait_ge(mix_in, 64)
                for d in range(2):
                    u = 2 * h + d
                    rows = slice(32 * d, 32 * d + 16)
                    for c0, c1 in ((0, T), (T, TC)):
                        out = begin_out()
                        pe.matmul(out[:, 0:c1 - c0], decay_w[rows, hs], glow[rows, c0:c1], start=True,
                                  stop=True).then_inc(out_made, 1)
                    pe.wait_ge(gla_kd, u + 1)
                    for b0, b1 in ((0, 4), (4, KB)):
                        out = begin_out()
                        for b in range(b0, b1):
                            ins = pe.transpose(out[:, P * (b - b0):P * (b - b0) + P], kd[:, P * b:P * b + P], identity[:, :])
                        ins.then_inc(out_made, 1)
                    pe.wait_ge(gla_qk, u + 1)
                    out = begin_out()
                    for b in range(4):
                        ins = pe.matmul(out[:, P * b:P * b + P], ke[:, P * b:P * b + P], qe[:, P * b:P * b + P],
                                        start=True, stop=True)
                    ins.then_inc(out_made, 1)
                    wait_taken(pe, out_gla(h) + 9 * d + 3)
                    if u == 0:
                        pe.wait_ge(gains_made, 1)
                        wait_taken(pe, OUT_GV + 3)
                        pe.wait_ge(side_taken, 2)
                    for i0 in (0, 8):
                        pair = [begin_out(), begin_out()]
                        for i in range(i0, min(i0 + 8, NCH - 1)):
                            n = chunk_cols(d, i)
                            r = slice(CHUNK * (n % 2), CHUNK * (n % 2) + CHUNK)
                            j = (i - i0) // 2
                            ins = pe.matmul(pair[i % 2][:, P * j:P * j + P], kd_tok[r, n // 2, :], v_tok[r, n // 2, hs],
                                            start=True, stop=True)
                            if i + 2 >= min(i0 + 8, NCH - 1):
                                ins.then_inc(out_made, 1)
                    wait_taken(pe, out_gla(h) + 9 * d + 4)
                    if d == 0 and h >= 1:
                        pe.wait_ge(side_taken, 2)
                        if h >= 2:
                            pe.wait_ge(gla_y, h - 1)
                    for b in range(4):
                        pe.matmul(o[:, P * b:P * b + P], v_tok[:, b, hs], a_t[:, b, :], start=(d == 0 and b == 0),
                                  stop=False, skip_group_check=True)
                    pe.wait_ge(gla_s, u + 1)
                    for i in range(T // CHUNK):
                        n = chunk_cols(d, i + 4)
                        cs = slice(CHUNK * n, CHUNK * n + CHUNK)
                        ins = pe.matmul(o[:, cs], state[:, i, :], qe[:, cs], start=False,
                                        stop=(d == 1 and i == T // CHUNK - 1), skip_group_check=True)
                    ins.then_inc(gla_o, 1)
                out = begin_out()
                pe.wait_ge(gla_sq, h + 1)
                pe.matmul(out[:, :], ones[:, :], square[:, h % 2, :], start=True, stop=True).then_inc(out_made, 1)

            gla_project(0)
            for h in range(GH):
                if h + 1 < GH:
                    gla_project(h + 1)
                gla(h)

            assert turn.out == OUT_QNORM
            out = begin_out()
            pe.wait_ge(lr_sq, 1)
            for k in range(QL):
                ins = pe.matmul(out[:, :], ones[:, :], spread[0][:, T * k:T * k + T], start=(k == 0), stop=(k == QL - 1))
            ins.then_inc(out_made, 1)
            om = [t[:, :, :].rearrange("p k t -> p (k t)") for t in (om_hi, om_lo)]
            for h in range(HEADS):
                project([(om[0][:, T * k:T * k + T], om[1][:, T * k:T * k + T]) for k in range(QL)],
                        (lambda k: pe.wait_ge(lr_lo, k + 1)) if h == 0 else None)
            out_a, out_b = begin_out(), begin_out()
            pe.wait_ge(lr_sq, 2)
            for out, c0, c1 in ((out_a, 0, T), (out_b, T, TC)):
                for k in range(KVL):
                    ins = pe.matmul(out[:, 0:c1 - c0], ones[:, :], spread[0][:, TC * k + c0:TC * k + c1], start=(k == 0),
                                    stop=(k == KVL - 1))
                ins.then_inc(out_made, 1)
            for pair in range(HEADS // 2):
                both([(om[0][:, TC * k:TC * k + T], om[1][:, TC * k:TC * k + T]) for k in range(KVL)],
                     [(om[0][:, TC * k + T:TC * k + TC], om[1][:, TC * k + T:TC * k + TC]) for k in range(KVL)], T, C,
                     (lambda k: pe.wait_ge(lr_lo, QL + k + 1)) if pair == 0 else None)
            slot, _ = next_tile()
            tile[0] += TP - 1
            for tb in range(KB):
                out = begin_out()
                for k in range(KVL):
                    tok = slice(TC * k + P * tb, TC * k + P * tb + P)
                    cols = slice(T * k, T * k + T)
                    mm(out, om[0][:, tok], w_hi[:, slot, cols], k == 0, False)
                    mm(out, om[0][:, tok], w_lo[:, slot, cols], False, False)
                    ins = mm(out, om[1][:, tok], w_hi[:, slot, cols], False, k == KVL - 1)
                ins.then_inc(out_made, 1)

            def scores(u):
                assert turn.out == out_scores(u)
                h, qb = u // 4, u % 4
                for c0, c1 in ((0, T), (T, TC)):
                    out = begin_out()
                    pe.matmul(out[:, 0:c1 - c0], q_t[0:QK, h, P * qb:P * qb + P], k_t[0:QK, h, c0:c1],
                              start=True, stop=True).then_inc(out_made, 1)

            def turn_probs(u):
                assert turn.out == out_turned(u)
                pe.wait_ge(att_prob, u + 1)
                for b0, b1 in ((0, 4), (4, KB)):
                    out = begin_out()
                    for b in range(b0, b1):
                        ins = pe.transpose(out[:, P * (b - b0):P * (b - b0) + P], prob[:, u % 2, P * b:P * b + P],
                                           identity[:, :])
                    ins.then_inc(out_made, 1)

            assert turn.out == OUT_ATT
            wait_taken(pe, OUT_KVNORM - 1)
            pe.wait_ge(k_spread, 1)
            wait_taken(pe, OUT_V - 1)
            scores(0)
            for u in range(UNITS):
                if u + 1 < UNITS:
                    scores(u + 1)
                turn_probs(u)
                if u % 4 == 3:
                    h = u // 4
                    wait_taken(pe, out_turned(u) + 1)
                    wait_taken(pe, out_turned(u))
                    if h == 0:
                        wait_taken(pe, OUT_ATT - 1)
                    if h >= 2:
                        pe.wait_ge(om_lo_made, h - 1)
                    rows = slice(64 * (h % 2), 64 * (h % 2) + 64)
                    for b in range(KB):
                        ins = pe.matmul(side[rows, h % 2, :], v_mla[:, b, 64 * h:64 * h + 64], p_t[:, b, :],
                                        start=(b == 0), stop=(b == KB - 1))
                    ins.then_inc(att_o, 1)

            assert turn.out == OUT_MERGE
            for m in range(KT):
                project(h_parts)
                project(h_parts)
                project([(om_hi[:, k, :], om_lo[:, k, :]) for k in range(4)],
                        (lambda k: pe.wait_ge(om_lo_made, 2 * k + 2)) if m == 0 else None)
                project([(og_hi[:, k, :], og_lo[:, k, :]) for k in range(4)],
                        (lambda k: pe.wait_ge(og_lo_made, k + 1)) if m == 0 else None)
            for m in range(KT):
                project([(mg_hi[:, k, :], mg_lo[:, k, :]) for k in range(KT)],
                        (lambda k: pe.wait_ge(mg_lo_made, k + 1)) if m == 0 else None)

            norm_sum(2)
            def up(group):
                for j in FF1_GROUPS[group]:
                    for part in range(2):
                        project(h_parts, (lambda k: pe.wait_ge(h_lo_made, 2 * KT + k + 1)) if j == 0 and part == 0 else None)

            def down(group):
                n = len(FF1_GROUPS[group])
                for m in range(KT):
                    project([(ff_hi[:, group % 2, k, :], ff_lo[:, group % 2, k, :]) for k in range(n)],
                            (lambda k: pe.wait_ge(ff_lo_made, FF1_GROUPS[group][k] + 1)) if m == 0 else None)
            up(0)
            up(1)
            down(0)
            up(2)
            down(1)
            down(2)
            norm_sum(3)
            assert turn.out == FIRST_OUTS and tile[0] % TP == 0

        def first_block_act(act, feed):
            steps = [0]

            def link(ins):
                steps[0] += 1
                ins.then_inc(act_chain, 1)
                act.wait_ge(act_chain, steps[0])

            act.dma_start(cvec[:, :, :], io["cvec"]).then_inc(small_in, 16)
            act.dma_start(identity[:, :], io["identity"]).then_inc(small_in, 16)
            act.wait_ge(small_in, 32)
            act.activation(cvec[:, :, :], cvec[:, :, :], ACT.Silu).then_inc(silu_made, 1)
            for k in range(KT):
                act.dma_start(x[:, k, :], io["x"][:, k, :]).then_inc(x_in, 16)
            act.wait_ge(ada_used, 6 * KT)
            act.dma_start(xc[:, :, :], io["ctx"]).then_inc(x_in, 16)
            act.dma_start(rope[:, :], io["rope"]).then_inc(mix_in, 16)
            act.dma_start(decay_w[:, :], io["decay_w"]).then_inc(mix_in, 16)
            act.dma_start(intra_mask[:, :, :], io["intra_mask"]).then_inc(mix_in, 16)
            act.dma_start(reset[:, :], io["reset"]).then_inc(mix_in, 16)
            act.wait_ge(const_in, CONSTS)
            act.wait_ge(x_in, 16 * (KT + 1))

            def sq(k, norm, src):
                if KT * norm + k >= 2:
                    act.wait_ge(summed, KT * norm + k - 1)
                w = sums(norm)
                act.activation(square[:, k % 2, 0:w], src[:, k, 0:w], ACT.Square).then_inc(squared, 1)

            def root_of(norm):
                act.wait_ge(stat_made, norm + 1)
                if norm:
                    act.wait_ge(rstd_made, norm)
                w = sums(norm)
                act.activation(root[:, 0:w], stat[:, 0:w], ACT.Sqrt, bias=col("eps"), scale=1.0 / D).then_inc(root_made, 1)

            def modulated(norm, n0, hi, scaled_, full, gain, shift):
                w = sums(norm)
                for k in range(KT):
                    act.wait_ge(n_scaled_made, n0 + k + 1)
                    if n0 + k >= 2:
                        act.wait_ge(h_lo_made, n0 + k - 1)
                    act.activation(full[:, k % 2, 0:w], scaled_[:, k % 2, 0:w], ACT.Identity, bias=shift(k), scale=gain(k))
                    act.activation(hi[:, k, :], scaled_[:, k % 2, 0:w], ACT.Identity, bias=shift(k),
                                   scale=gain(k)).then_inc(h_hi_made, 1)

            for k in range(KT):
                sq(k, 0, x)
            for k in range(KT):
                sq(k, 1, xc)
            root_of(0)
            act.wait_ge(gains_made, 1)
            modulated(0, 0, h_hi, n_scaled, n_full, lambda k: gain1[:, 0, k:k + 1], lambda k: mod[:, k, 0:1])
            root_of(1)
            modulated(1, KT, hc_hi, n_scaled, n_full, lambda k: gain1[:, 1, k:k + 1], lambda k: mod[:, k, 1:2])

            def take(o, out, func=ACT.Copy, width=T, **kw):
                wait_made(act, o)
                act.activation(out, bank(o)[:, 0:width], func, **kw).then_inc(out_taken[o % BANKS], 1)

            act.wait_ge(h_lo_made, 2 * KT)
            for m in range(KVL):
                take(OUT_KV + 2 * m, z_kv[:, m, 0:T])
                take(OUT_KV + 2 * m + 1, z_kv[:, m, T:TC], width=C)
            for m in range(QL):
                take(OUT_Q + m, z_q[:, m, :])
            for tb in range(4):
                take(OUT_GV + tb, v_tok[:, tb, :])

            def gla_take(h):
                o = out_gla_project(h)
                if h >= 2:
                    act.wait_ge(og_hi_made, h - 1)
                    act.wait_ge(gla_y, h - 1)
                take(o, gk[:, h % 2, 0:T])
                take(o + 1, gk[:, h % 2, T:TC], width=C)
                take(o + 2, gq[:, h % 2, :], scale=GLA_SCALE)
                take(o + 3, gr[:, h % 2, :], func=ACT.Silu)

            def gla(h):
                for d in range(2):
                    u, o = 2 * h + d, out_gla(h) + 9 * d
                    last = slice(CHUNK - 1, TC, CHUNK) if d == 0 else slice(0, TC, CHUNK)
                    wait_taken(act, o + 1)
                    if u:
                        act.wait_ge(gla_b, u)
                    link(act.activation(ln[:, :], zb[:, :], ACT.Abs))
                    link(act.activation(ln[:, :], ln[:, :], ACT.Exp, scale=-1.0))
                    act.activation(ln[:, :], ln[:, :], ACT.Ln, bias=col("one")).then_inc(gla_ln, 1)
                    act.wait_ge(gla_b, u + 1)
                    if u:
                        act.wait_ge(gla_o, u)
                    act.activation(chunk_decay[:, :], b_cum[:, last], ACT.Exp, scale=1.0 / GATE_NORM)
                    act.activation(qe[:, :], b_cum[:, 0:T], ACT.Exp, scale=1.0 / GATE_NORM)
                    act.activation(ke[:, :], b_cum[:, 0:T], ACT.Exp, scale=-1.0 / GATE_NORM).then_inc(gla_e, 1)
                    act.wait_ge(gla_d, u + 1)
                    act.activation(kd[:, :], kd[:, :], ACT.Exp, scale=1.0 / GATE_NORM).then_inc(gla_ed, 1)
                    take(o + 2, kd_tok[:, 0:4, :].rearrange("p b d -> p (b d)"))
                    take(o + 3, kd_tok[:, 4:KB, :].rearrange("p b d -> p (b d)"), width=2 * P)
                act.wait_ge(gla_o, 2 * h + 2)
                act.activation(square[:, h % 2, :], side[:, h % 2, :], ACT.Square).then_inc(gla_sq, 1)
                take(out_gla(h) + 18, root[:, :], func=ACT.Sqrt, bias=col("eps"), scale=1.0 / P)
                act.wait_ge(gla_y, h + 1)
                act.activation(og_hi[:, h, :], o_norm, ACT.Copy).then_inc(og_hi_made, 1)

            gla_take(0)
            for h in range(GH):
                if h + 1 < GH:
                    gla_take(h + 1)
                gla(h)
            act.wait_ge(og_lo_made, GH)
            for k in range(QL):
                ins = act.activation(spread[0][:, T * k:T * k + T], z_q[:, k, :], ACT.Square)
            ins.then_inc(lr_sq, 1)
            take(OUT_QNORM, root[:, :], func=ACT.Sqrt, bias=col("eps"), scale=1.0 / (QL * P))
            om = om_hi[:, :, :].rearrange("p k t -> p (k t)")
            for k in range(QL):
                act.wait_ge(lr_scaled, k + 1)
                act.activation(om[:, T * k:T * k + T], z_q[:, k, :], ACT.Copy).then_inc(lr_hi, 1)
            wait_made(act, OUT_QNORM)
            for k in range(KVL):
                ins = act.activation(spread[0][:, TC * k:TC * k + TC], z_kv[:, k, :], ACT.Square)
            ins.then_inc(lr_sq, 1)
            take(OUT_KVNORM, root[:, :], func=ACT.Sqrt, bias=col("eps"), scale=1.0 / (KVL * P))
            take(OUT_KVNORM + 1, square[:, 0, 0:C], func=ACT.Sqrt, bias=col("eps"), scale=1.0 / (KVL * P), width=C)
            for k in range(KVL):
                act.wait_ge(lr_scaled, QL + k + 1)
                act.activation(om[:, TC * k:TC * k + TC], z_kv[:, k, :], ACT.Copy).then_inc(lr_hi, 1)
            for pair in range(HEADS // 2):
                for o, c0, c1 in ((OUT_KH + 2 * pair, 0, T), (OUT_KH + 2 * pair + 1, T, TC)):
                    wait_made(act, o)
                    act.activation(k_t[0:64, 2 * pair, c0:c1], bank(o)[0:64, 0:c1 - c0], ACT.Copy)
                    act.activation(k_t[0:64, 2 * pair + 1, c0:c1], bank(o)[64:P, 0:c1 - c0], ACT.Copy)\
                       .then_inc(out_taken[o % BANKS], 1)
            for tb in range(KB):
                take(OUT_V + tb, v_mla[:, tb, :])

            def exps(u):
                o = out_scores(u)
                act.wait_ge(att_max, u + 1)
                if u >= 2:
                    wait_made(act, out_turned(u - 2) + 1)
                for i, (c0, c1) in enumerate(((0, T), (T, TC))):
                    act.activation(prob[:, u % 2, c0:c1], bank(o + i)[:, 0:c1 - c0], ACT.Exp, scale=MLA_SCALE,
                                   bias=att_stat[:, u % 2, 1:2], accum_out=att_stat[:, u % 2, 2 + i:3 + i])\
                       .then_inc(out_taken[(o + i) % BANKS], 1)

            exps(0)
            for u in range(UNITS):
                if u + 1 < UNITS:
                    exps(u + 1)
                h, qb = u // 4, u % 4
                if qb == 0 and h:
                    act.wait_ge(att_o, h)
                wait_made(act, out_turned(u))
                act.activation(p_t[:, 0:4, P * qb:P * qb + P], bank(out_turned(u)).rearrange("p (b q) -> p b q", b=4),
                               ACT.Copy).then_inc(out_taken[out_turned(u) % BANKS], 1)
                if u % 4 == 3:
                    rows = slice(64 * (h % 2), 64 * (h % 2) + 64)
                    act.wait_ge(att_o, h + 1)
                    act.activation(om_hi[rows, h // 2, :], side[rows, h % 2, :], ACT.Copy).then_inc(om_hi_made, 1)
            for k in range(KT):
                act.dma_start(x[:, k, :], io["x"][:, k, :]).then_inc(x_in, 16)
            for m in range(KT):
                o = OUT_MERGE + 4 * m
                if m >= 2:
                    act.wait_ge(mg_lo_made, m - 1)
                take(o, gate_m[:, m % 2, :], func=ACT.Sigmoid)
                take(o + 1, gate_g[:, m % 2, :], func=ACT.Sigmoid)
                act.wait_ge(mg_made, m + 1)
                act.activation(mg_hi[:, m, :], gate_m[:, m % 2, :], ACT.Copy).then_inc(mg_hi_made, 1)
            for k in range(KT):
                wait_taken(act, OUT_MIX + k)
                sq(k, 2, x)
            root_of(2)
            modulated(2, 2 * KT, h_hi, f2_scaled, f2_full, lambda k: gain2[:, k:k + 1], lambda k: mod[:, 3 * KT + k, 0:1])

            def up(group):
                for i, j in enumerate(FF1_GROUPS[group]):
                    o = out_ff_up(group) + 2 * i
                    wait_made(act, o)
                    if j >= 2:
                        act.wait_ge(ff_conved, j - 1)
                    else:
                        act.wait_ge(pads_made, 1)
                    act.activation(ff_pad[:, j % 2, 1:GRID_H + 1, 1:GRID_W + 1],
                                   bank(o).rearrange("p (r c) -> p r c", r=GRID_H), ACT.Copy).then_inc(out_taken[o % BANKS], 1)
                    act.wait_ge(ff_conved, j + 1)
                    act.activation(ff_conv[:, j % 2, :], ff_conv[:, j % 2, :], ACT.Gelu).then_inc(ff_gelu, 1)
                    wait_taken(act, o + 1)
                    act.activation(ff_hi[:, group % 2, i, :], ff_hid[:, j % 2, :], ACT.Copy).then_inc(ff_hi_made, 1)
            for g in range(3):
                up(g)
            o = out_ff_down(2)
            for k in range(KT):
                wait_taken(act, o + k)
                sq(k, 3, x)
            root_of(3)
            for k in range(KT):
                feed(k, NORM0, ("norm_mix", 0), lambda k: act.wait_ge(x_normed, k + 1), o)

        last_of = [slice(CHUNK - 1, CHUNK), slice(0, 1)]

        def first_block_dve(dve, feed, feed_low):
            steps = [0]

            def link(ins):
                steps[0] += 1
                ins.then_inc(dve_chain, 1)
                dve.wait_ge(dve_chain, steps[0])

            def take(ins, o):
                ins.then_inc(out_taken[o % BANKS], 1)
                wait_taken(dve, o)

            def own(ins, s, count):
                ins.then_inc(s, 1)
                dve.wait_ge(s, count)

            def add_up(k, norm):
                w = sums(norm)
                dve.wait_ge(squared, KT * norm + k + 1)
                if k == 0:
                    if norm:
                        dve.wait_ge(stat_made, norm)
                    dve.tensor_copy(square_sum[:, 0:w], square[:, 0, 0:w]).then_inc(summed, 1)
                else:
                    dve.wait_ge(summed, KT * norm + k)
                    dve.tensor_tensor(square_sum[:, 0:w], square_sum[:, 0:w], square[:, k % 2, 0:w], ALU.add)\
                       .then_inc(summed, 1)

            def rstd_of(norm):
                w = sums(norm)
                dve.wait_ge(root_made, norm + 1)
                own(dve.reciprocal(rstd[:, 0:w], root[:, 0:w]), rstd_made, norm + 1)

            def modulated(norm, n0, src, hi, lo, scaled_, full):
                w = sums(norm)
                for k in range(KT + 1):
                    if k < KT:
                        dve.tensor_tensor(scaled_[:, k % 2, 0:w], src[:, k, 0:w], rstd[:, 0:w], ALU.mult)\
                           .then_inc(n_scaled_made, 1)
                    if k:
                        dve.wait_ge(h_hi_made, n0 + k)
                        dve.tensor_tensor(lo[:, k - 1, :], full[:, (k - 1) % 2, 0:w], hi[:, k - 1, :].bitcast(F32),
                                          ALU.subtract).then_inc(h_lo_made, 1)

            for k in range(KT):
                add_up(k, 0)
            dve.wait_ge(ada_used, 6 * KT)
            products = side[:, 0, 0:12 * KT].rearrange("p (m s) -> p m s", s=2)
            for s in range(2):
                link(dve.tensor_tensor(mod[:, :, s], products[:, :, s], table[:, names["b_ada"]:names["b_ada"] + 6 * KT], ALU.add))
            norm1 = table[:, names["norm1"]:names["norm1"] + KT]
            for s in range(2):
                link(dve.scalar_tensor_tensor(out=gain1[:, s, :], in0=mod[:, KT:2 * KT, s], scalar=1.0, in1=norm1,
                                              op0=ALU.add, op1=ALU.mult))
            own(dve.scalar_tensor_tensor(out=gain2[:, :], in0=mod[:, 4 * KT:5 * KT, 0], scalar=1.0,
                                         in1=table[:, names["norm2"]:names["norm2"] + KT], op0=ALU.add, op1=ALU.mult),
                gains_made, 1)
            for k in range(KT):
                add_up(k, 1)
            rstd_of(0)
            modulated(0, 0, x, h_hi, h_lo, n_scaled, n_full)
            rstd_of(1)
            modulated(1, KT, xc, hc_hi, hc_lo, n_scaled, n_full)
            dve.wait_ge(h_lo_made, 2 * KT)

            dve.wait_ge(mix_in, 64)
            wait_made(dve, OUT_MISC)
            lat, con = bank(OUT_MISC), bank(OUT_MISC + 1)
            link(dve.tensor_copy(glow[:, 0:T], lat[0:64, :]))
            link(dve.tensor_tensor(square[64:96, 1, :], lat[96:P, :], rope[96:P, :], ALU.mult))
            take(dve.tensor_tensor(k_rope[:, 0:T], lat[64:96, :], rope[64:96, :], ALU.mult), OUT_MISC)
            link(dve.tensor_tensor(k_rope[:, 0:T], k_rope[:, 0:T], square[64:96, 1, :], ALU.add))
            wait_made(dve, OUT_MISC + 1)
            link(dve.tensor_copy(k_rope[:, T:TC], con[64:96, 0:C]))
            own(dve.tensor_copy(glow[:, T:TC], con[0:64, 0:C]), out_taken[(OUT_MISC + 1) % BANKS], 1)
            dve.wait_ge(side_made, 1)
            dve.tensor_copy(v_tok[:, 4, :], side[:, 1, :]).then_inc(side_taken, 1)
            dve.tensor_copy(v_tok[:, 5, :], side[:, 2, :]).then_inc(side_taken, 1)
            dve.wait_ge(side_taken, 2)

            def gla(h):
                for d in range(2):
                    u, o = 2 * h + d, out_gla(h) + 9 * d
                    last = slice(CHUNK - 1, TC, CHUNK) if d == 0 else slice(0, TC, CHUNK)
                    bias = col("b_decay", GH * d + h)
                    wait_made(dve, o)
                    take(dve.tensor_scalar(zb[:, 0:T], bank(o), bias, None, ALU.add), o)
                    wait_made(dve, o + 1)
                    take(dve.tensor_scalar(zb[:, T:TC], bank(o + 1)[:, 0:C], bias, None, ALU.add), o + 1)
                    dve.wait_ge(gla_ln, u + 1)
                    link(dve.scalar_tensor_tensor(out=zb[:, :], in0=zb[:, :], scalar=0.0, in1=ln[:, :], op0=ALU.min,
                                                  op1=ALU.subtract))
                    own(dve.tensor_tensor_scan(rev(b_cum, d, 0, TC), rev(reset, d, d, TC + d), rev(zb, d, 0, TC), 0.0,
                                               ALU.mult, ALU.add), gla_b, u + 1)
                    chunks = lambda t: t.rearrange("p (n c) -> p n c", c=CHUNK)
                    own(dve.tensor_tensor(chunks(kd[:, :]), chunks(b_cum[:, :])[:, :, last_of[d]].to_broadcast([P, NCH, CHUNK]),
                                          chunks(b_cum[:, :]), ALU.subtract), gla_d, u + 1)
                    dve.wait_ge(gla_e, u + 1)
                    wait_taken(dve, out_gla_project(h) + 2)
                    link(dve.tensor_tensor(qe[:, :], qe[:, :], gq[:, h % 2, :], ALU.mult))
                    own(dve.tensor_tensor(ke[:, :], ke[:, :], gk[:, h % 2, 0:T], ALU.mult), gla_qk, u + 1)
                    dve.wait_ge(gla_ed, u + 1)
                    own(dve.tensor_tensor(kd[:, :], kd[:, :], gk[:, h % 2, :], ALU.mult), gla_kd, u + 1)
                    wait_made(dve, o + 4)
                    take(dve.tensor_tensor(a_t[:, :, :], bank(o + 4).rearrange("p (b c) -> p b c", b=4),
                                           intra_mask[:, d:d + 1, :].to_broadcast([P, 4, P]), ALU.mult), o + 4)
                    for i in range(NCH - 1):
                        n = chunk_cols(d, i)
                        source = o + 5 + i % 2 + 2 * (i // 8)
                        if i % 8 < 2:
                            wait_made(dve, o + 6 + 2 * (i // 8))
                        out = state_c[:, i, :] if i < 3 else state[:, i - 3, :]
                        new = bank(source)[:, P * (i % 8 // 2):P * (i % 8 // 2) + P]
                        if i == 0:
                            link(dve.tensor_copy(out, new))
                            continue
                        before = state_c[:, i - 1, :] if i < 4 else state[:, i - 4, :]
                        ins = dve.scalar_tensor_tensor(out=out, in0=before, scalar=chunk_decay[:, n:n + 1], in1=new,
                                                       op0=ALU.mult, op1=ALU.add)
                        if i % 8 >= 6 or i >= NCH - 3:
                            take(ins, source)
                        else:
                            link(ins)
                    own(dve.tensor_copy(state_c[:, 3, 0:1], state[:, 7, 0:1]), gla_s, u + 1)
                o = out_gla(h) + 18
                wait_taken(dve, o)
                link(dve.reciprocal(rstd[:, :], root[:, :]))
                dve.wait_ge(gla_o, 2 * h + 2)
                link(dve.scalar_tensor_tensor(out=o_norm, in0=side[:, h % 2, :], scalar=col("gla_norm"),
                                              in1=rstd[:, :], op0=ALU.mult, op1=ALU.mult))
                own(dve.tensor_tensor(o_norm, o_norm, gr[:, h % 2, :], ALU.mult), gla_y, h + 1)
                dve.wait_ge(og_hi_made, h + 1)
                own(dve.tensor_tensor(og_lo[:, h, :], o_norm, og_hi[:, h, :].bitcast(F32), ALU.subtract),
                    og_lo_made, h + 1)

            for h in range(GH):
                gla(h)

            om = [t[:, :, :].rearrange("p k t -> p (k t)") for t in (om_hi, om_lo)]
            wait_taken(dve, OUT_QNORM)
            link(dve.reciprocal(rstd[:, :], root[:, :]))
            for k in range(QL):
                own(dve.scalar_tensor_tensor(out=z_q[:, k, :], in0=z_q[:, k, :], scalar=col("q_norm", k), in1=rstd[:, :],
                                             op0=ALU.mult, op1=ALU.mult), lr_scaled, k + 1)
                dve.wait_ge(lr_hi, k + 1)
                own(dve.tensor_tensor(om[1][:, T * k:T * k + T], z_q[:, k, :], om[0][:, T * k:T * k + T].bitcast(F32),
                                      ALU.subtract), lr_lo, k + 1)
            for h in range(HEADS):
                o = OUT_QH + h
                wait_made(dve, o)
                b = bank(o)
                link(dve.tensor_tensor(square[64:96, 1, :], b[96:P, :], rope[96:P, :], ALU.mult))
                link(dve.tensor_copy(q_t[0:64, h, :], b[0:64, :]))
                link(dve.tensor_tensor(q_t[64:96, h, :], b[64:96, :], rope[64:96, :], ALU.mult))
                take(dve.tensor_tensor(q_t[64:96, h, :], q_t[64:96, h, :], square[64:96, 1, :], ALU.add), o)
            wait_taken(dve, OUT_KVNORM)
            wait_taken(dve, OUT_KVNORM + 1)
            link(dve.reciprocal(rstd[:, :], root[:, :]))
            link(dve.reciprocal(square[:, 1, 0:C], square[:, 0, 0:C]))
            wait_made(dve, OUT_KVNORM - 1)
            for k in range(KVL):
                link(dve.scalar_tensor_tensor(out=z_kv[:, k, 0:T], in0=z_kv[:, k, 0:T], scalar=col("kv_norm", k),
                                              in1=rstd[:, :], op0=ALU.mult, op1=ALU.mult))
                own(dve.scalar_tensor_tensor(out=z_kv[:, k, T:TC], in0=z_kv[:, k, T:TC], scalar=col("kv_norm", k),
                                             in1=square[:, 1, 0:C], op0=ALU.mult, op1=ALU.mult), lr_scaled, QL + k + 1)
                dve.wait_ge(lr_hi, QL + k + 1)
                own(dve.tensor_tensor(om[1][:, TC * k:TC * k + TC], z_kv[:, k, :], om[0][:, TC * k:TC * k + TC].bitcast(F32),
                                      ALU.subtract), lr_lo, QL + k + 1)
            for h in range(HEADS):
                ins = dve.tensor_copy(k_t[64:96, h, :], k_rope)
            own(ins, k_spread, 1)

            def probs(u):
                o, st = out_scores(u), att_stat[:, u % 2, :]
                wait_made(dve, o + 1)
                both_banks = acc[:, o % BANKS:o % BANKS + 2, :].rearrange("p b t -> p (b t)")[:, 0:TC]
                link(dve.tensor_reduce(st[:, 0:1], both_banks, AX.X, ALU.max))
                own(dve.tensor_scalar(st[:, 1:2], st[:, 0:1], -MLA_SCALE, None, ALU.mult), att_max, u + 1)

            def normalised(u):
                o, st = out_scores(u), att_stat[:, u % 2, :]
                wait_taken(dve, o)
                wait_taken(dve, o + 1)
                link(dve.tensor_tensor(st[:, 4:5], st[:, 2:3], st[:, 3:4], ALU.add))
                link(dve.reciprocal(st[:, 5:6], st[:, 4:5]))
                own(dve.tensor_scalar(prob[:, u % 2, :], prob[:, u % 2, :], st[:, 5:6], None, ALU.mult), att_prob, u + 1)

            wait_taken(dve, OUT_V - 1)
            probs(0)
            for u in range(UNITS):
                h, qb = u // 4, u % 4
                normalised(u)
                if u + 1 < UNITS:
                    probs(u + 1)
                o = out_turned(u) + 1
                wait_made(dve, o)
                if qb == 0 and h:
                    dve.wait_ge(att_o, h)
                take(dve.tensor_copy(p_t[:, 4:KB, P * qb:P * qb + P],
                                     bank(o)[:, 0:2 * P].rearrange("p (b q) -> p b q", b=2)), o)
                if qb == 3:
                    rows = slice(64 * (h % 2), 64 * (h % 2) + 64)
                    dve.wait_ge(om_hi_made, h + 1)
                    own(dve.tensor_tensor(om_lo[rows, h // 2, :], side[rows, h % 2, :], om_hi[rows, h // 2, :].bitcast(F32),
                                          ALU.subtract), om_lo_made, h + 1)
            for m in range(KT):
                o = OUT_MERGE + 4 * m
                gm, gg = gate_m[:, m % 2, :], gate_g[:, m % 2, :]
                wait_taken(dve, o + 1)
                wait_made(dve, o + 2)
                take(dve.tensor_tensor(gm, gm, bank(o + 2), ALU.mult), o + 2)
                wait_made(dve, o + 3)
                take(dve.tensor_tensor(gg, gg, bank(o + 3), ALU.mult), o + 3)
                own(dve.tensor_tensor(gm, gm, gg, ALU.add), mg_made, m + 1)
                dve.wait_ge(mg_hi_made, m + 1)
                own(dve.tensor_tensor(mg_lo[:, m, :], gm, mg_hi[:, m, :].bitcast(F32), ALU.subtract), mg_lo_made, m + 1)
            dve.wait_ge(x_in, 16 * (2 * KT + 1))

            def gated_add(o, k, gate):
                wait_made(dve, o)
                take(dve.scalar_tensor_tensor(out=x[:, k, :], in0=bank(o), scalar=mod[:, gate * KT + k, 0:1], in1=x[:, k, :],
                                              op0=ALU.mult, op1=ALU.add), o)

            for k in range(KT + 1):
                if k < KT:
                    gated_add(OUT_MIX + k, k, 2)
                if k:
                    add_up(k - 1, 2)
            rstd_of(2)
            modulated(2, 2 * KT, x, h_hi, h_lo, f2_scaled, f2_full)
            dve.memset(ff_pad[:, :, :, :], 0.0).then_inc(pads_made, 1)

            def up(group):
                for i, j in enumerate(FF1_GROUPS[group]):
                    o = out_ff_up(group) + 2 * i
                    pad, conv = ff_pad[:, j % 2, :, :], ff_conv[:, j % 2, :].rearrange("p (r c) -> p r c", r=GRID_H)
                    wait_taken(dve, o)
                    for tap in range(9):
                        r, c = tap // 3, tap % 3
                        src = pad[:, r:r + GRID_H, c:c + GRID_W]
                        w = col("conv_w", FF1 * tap + j)
                        if tap == 0:
                            ins = dve.tensor_scalar(conv, src, w, col("conv_b", j), ALU.mult, ALU.add)
                        else:
                            ins = dve.scalar_tensor_tensor(out=conv, in0=src, scalar=w, in1=conv, op0=ALU.mult, op1=ALU.add)
                        if tap < 8:
                            link(ins)
                    own(ins, ff_conved, j + 1)
                    dve.wait_ge(ff_gelu, j + 1)
                    wait_made(dve, o + 1)
                    ins = dve.tensor_tensor(ff_hid[:, j % 2, :], bank(o + 1), ff_conv[:, j % 2, :], ALU.mult)
                    take(ins, o + 1)
                    dve.wait_ge(ff_hi_made, j + 1)
                    own(dve.tensor_tensor(ff_lo[:, group % 2, i, :], ff_hid[:, j % 2, :], ff_hi[:, group % 2, i, :].bitcast(F32),
                                          ALU.subtract), ff_lo_made, j + 1)

            up(0)
            up(1)
            for k in range(KT):
                gated_add(out_ff_down(0) + k, k, 5)
            up(2)
            for k in range(KT):
                gated_add(out_ff_down(1) + k, k, 5)
            for k in range(KT + 1):
                if k < KT:
                    gated_add(out_ff_down(2) + k, k, 5)
                if k:
                    add_up(k - 1, 3)
            rstd_of(3)
            for k in range(KT + 1):
                if k < KT:
                    dve.scalar_tensor_tensor(out=x[:, k, :], in0=x[:, k, :], scalar=col("final1", k), in1=rstd[:, :],
                                             op0=ALU.mult, op1=ALU.mult).then_inc(x_normed, 1)
                if k:
                    dve.wait_ge(x_normed, k)
                    feed(k - 1, NORM0)
                    feed_low(k - 1, NORM0, ("norm_mix", 0))

        def load_panel(eng, slot, panel):
            eng.dma_start(w_raw[:, slot, :], io["weights"][panel].rearrange("p t c -> p (t c)")).then_inc(raw_in[slot], 16)

        block = whole.enter_context(nc.Block())

        @block.sync
        def _(sp):
            sp.dma_start(table[:, :], io["table"]).then_inc(const_in, 16)
            sp.dma_start(ones[:, :], io["ones"]).then_inc(const_in, 16)
            sp.dma_start(sgu_mask[:, :], io["sgu_mask"]).then_inc(const_in, 16)
            if start_x:
                for k in range(KT):
                    sp.dma_start(x[:, k, :], io["x"][:, k, :]).then_inc(x_in, 16)
            for slot in range(SLOTS):
                load_panel(sp, slot, slot)
            if not start_x:
                first_block_sp(sp)
            turns = n_panels // SLOTS - 1
            with sp.Fori(0, turns) as it:
                for slot in range(SLOTS):
                    sp.wait_ge(panel_made, it * SLOTS + (slot + 1))
                    load_panel(sp, slot, it * SLOTS + (SLOTS + slot))
            for slot in range(n_panels % SLOTS):
                sp.wait_ge(panel_made, SLOTS * turns + slot + 1)
                load_panel(sp, slot, SLOTS * (turns + 1) + slot)
            for k in range(KT):
                sp.wait_ge(scaled, k + 1)
                sp.dma_start(io["out"][:, k, :], x[:, k, :]).then_inc(result_out, 16)
            sp.wait_ge(result_out, 16 * KT)

        @block.gpsimd
        def _(pool):
            def high(slot):
                pool.tensor_scalar(w_hi[:, slot, :], w_raw[:, slot, :], 1.0, 1.0, ALU.mult, ALU.mult).then_inc(hi_made, 1)

            def low_then_high(slot, made, landed, used):
                after = (slot + 1) % SLOTS
                if landed is not None:
                    pool.wait_ge(raw_in[after], landed)
                if used is not None:
                    pool.wait_ge(panel_used, used)
                pool.wait_ge(hi_made, made)
                pool.tensor_tensor(w_lo[:, slot, :], w_raw[:, slot, :], w_hi[:, slot, :].bitcast(F32),
                                   ALU.subtract).then_inc(panel_made, 1)
                if landed is not None:
                    high(after)

            pool.wait_ge(raw_in[0], 16)
            high(0)
            for n in range(SLOTS - 1):
                low_then_high(n, n + 1, 16, None)
            first = SLOTS - 1
            turns = (n_panels - 1 - first) // SLOTS
            with pool.Fori(0, turns) as it:
                for j in range(SLOTS):
                    low_then_high((first + j) % SLOTS, it * SLOTS + (first + j + 1), it * 16 + 32, it * SLOTS + (j + 1))
            for n in range(first + SLOTS * turns, n_panels):
                last = n == n_panels - 1
                low_then_high(n % SLOTS, n + 1, None if last else 16 * ((n + 1) // SLOTS + 1), None if last else n + 2 - SLOTS)

        @block.tensor
        def _(pe):
            turn = Turn()
            turn.out = first_out["mix", 0] if start_x else 0
            tile = [0]
            pending = [False]

            def next_tile():
                t = tile[0]
                tile[0] += 1
                slot = t // TP % SLOTS
                if t % TP == 0:
                    pe.wait_ge(panel_made, turn.value(t // TP + 1))
                    pending[0] = t >= TP
                return slot, slice(P * (t % TP), P * (t % TP) + P)

            def mm(out, lhs, rhs, start, stop, group=False):
                ins = pe.matmul(out, lhs, rhs, start=start, stop=stop, skip_group_check=group)
                if pending[0]:
                    ins.then_inc(panel_used, 1)
                    pending[0] = False
                return ins

            def skip_to_panel():
                while tile[0] % TP:
                    tile[0] += 1

            def begin_out():
                o = turn.out
                turn.out += 1
                if o >= BANKS:
                    v = o // BANKS
                    pe.wait_ge(out_taken[o % BANKS], turn.value(v, turn.rate // BANKS))
                return bank(o)

            def project(parts, ready=None):
                out = begin_out()
                for k, (hi, lo) in enumerate(parts):
                    slot, cols = next_tile()
                    if ready:
                        ready(k)
                    last = k == len(parts) - 1
                    mm(out, w_hi[:, slot, cols], hi, k == 0, False)
                    mm(out, w_hi[:, slot, cols], lo, False, False)
                    ins = mm(out, w_lo[:, slot, cols], hi, False, last)
                ins.then_inc(out_made, 1)

            h_parts = [(h_hi[:, k, :], h_lo[:, k, :]) for k in range(KT)]

            def norm_sum(norm):
                pe.wait_ge(summed, KT * (norm + 1))
                if norm:
                    pe.wait_ge(root_made, norm)
                pe.matmul(stat[:, :], ones[:, :], square_sum[:, :], start=True, stop=True).then_inc(stat_made, 1)

            def ready_h(norm):
                return lambda k: pe.wait_ge(h_lo_made, KT * norm + k + 1 - H_SKIP)

            def recurrent(inst, norm):
                for half in range(2):
                    for m in range(HALF):
                        project(h_parts, ready_h(norm) if half == 0 and m == 0 else None)
                        if half == 0 and m == 0:
                            norm_sum(norm)
                    for m in range(HALF * half, HALF * half + HALF):
                        for gate in range(2):
                            project([(M["rec_hi"][:, k, :], M["rec_lo"][:, k, :]) for k in BD[m]],
                                    lambda i, m=m: pe.wait_ge(rec_lo_made, rec_x_lo(inst, BD[m][i])))
                    skip_to_panel()
                    for m in range(HALF):
                        project(h_parts)
                for m in range(KT):
                    project([(M["rec_hi"][:, k, :], M["rec_lo"][:, k, :]) for k in range(RT)],
                            (lambda k: pe.wait_ge(rec_lo_made, rec_y_lo(inst, k))) if m == 0 else None)

            def spatial(norm):
                for half in range(2):
                    outs = [begin_out() for _ in range(4)]
                    for k in range(KT):
                        if k % 2 == 0:
                            slot, _ = next_tile()
                            tile[0] += TP - 1
                        if half == 0:
                            pe.wait_ge(h_lo_made, KT * norm + k + 1 - H_SKIP)
                        cols = slice(512 * (k % 2), 512 * (k % 2) + 512)
                        for tb in range(4):
                            tok = slice(P * tb, P * tb + P)
                            mm(outs[tb], h_hi[:, k, tok], w_hi[:, slot, cols], k == 0, False)
                            mm(outs[tb], h_hi[:, k, tok], w_lo[:, slot, cols], False, False)
                            ins = mm(outs[tb], h_lo[:, k, tok], w_hi[:, slot, cols], False, k == KT - 1)
                            if k == KT - 1:
                                ins.then_inc(out_made, 1)
                    if half == 0:
                        norm_sum(norm)
                        pe.wait_ge(rstd_made, norm + 1)
                        for tb in range(4):
                            ins = pe.matmul(side[:, 0, tb:tb + 1], rstd[0:1, P * tb:P * tb + P], ones[0:1, 0:1],
                                            start=True, stop=True)
                        ins.then_inc(sgu_col, 1)
                for m in range(KT):
                    project(h_parts)
                pe.wait_ge(sgu_masked, 1)
                for g in range(SG):
                    out = begin_out()
                    if g == 0:
                        pe.wait_ge(sgu_v_norm, 4)
                    for tb in range(4):
                        ins = pe.matmul(out[:, P * tb:P * tb + P], M["sgu_v"][:, tb, P * g:P * g + P],
                                        M["sgu_w"][:, g, :], start=True, stop=True)
                    ins.then_inc(out_made, 1)
                for m in range(KT):
                    project([(M["sgu_hi"][:, k, :], M["sgu_lo"][:, k, :]) for k in range(KT)],
                            (lambda k: pe.wait_ge(sgu_lo_made, k + 1)) if m == 0 else None)

            def short_conv(norm):
                for m in range(KT):
                    for part in range(3):
                        project(h_parts, ready_h(norm) if m == 0 and part == 0 else None)
                        if m == 0 and part == 0:
                            norm_sum(norm)
                for m in range(KT):
                    project([(M["cnv_hi"][:, k, :], M["cnv_lo"][:, k, :]) for k in range(KT)],
                            (lambda k: pe.wait_ge(cnv_lo_made, k + 1)) if m == 0 else None)

            def looped(parts):
                assert tile[0] % TP == 0
                with pe.Fori(0, 2) as it:
                    turn.it, turn.rate = it, SLOTS
                    for _ in range(SLOTS):
                        project(parts)
                turn.it = None
                turn.out += SLOTS
                tile[0] += SLOTS * TP

            def mlp(layer, norm):
                for j in range(8):
                    project(h_parts, ready_h(norm) if j == 0 else None)
                    if j == 0:
                        norm_sum(norm)
                for group in range(1, UG + 1):
                    if group < UG:
                        looped(h_parts)
                    pe.wait_ge(hid_lo_made, FF2 * layer + 8 * group)
                    half = (group - 1) % 2
                    looped([(M["hid_hi"][:, half, k, :], M["hid_lo"][:, half, k, :]) for k in range(8)])

            pe.wait_ge(const_in, CONSTS)
            if not start_x:
                first_block_pe(pe, turn, next_tile, mm, begin_out, project, tile, norm_sum, skip_to_panel)
            norm = NORM0
            for layer in range(LAYERS)[:upto]:
                assert turn.out == first_out["mix", layer]
                (lambda n: recurrent(layer // 3, n), spatial, short_conv)[layer % 3](norm)
                assert turn.out == first_out["mlp", layer]
                mlp(layer, norm + 1)
                norm += 2
            norm_sum(norm)

        @block.scalar
        def _(act):
            def feed(k, norm, gain, x_ready, h_free):
                x_ready(k)
                if KT * norm + k >= 2:
                    act.wait_ge(summed, KT * norm + k - 1)
                act.activation(square[:, k % 2, :], x[:, k, :], ACT.Square).then_inc(squared, 1)
                if gain is not None:
                    if k == 0 and h_free:
                        wait_made(act, h_free - 1)
                    act.activation(h_hi[:, k, :], x[:, k, :], ACT.Copy, scale=col(*gain_at(gain, k))).then_inc(h_hi_made, 1)

            def norm_root(norm):
                act.wait_ge(stat_made, norm + 1)
                if norm:
                    act.wait_ge(rstd_made, norm)
                act.activation(root[:, :], stat[:, :], ACT.Sqrt, bias=col("eps"), scale=1.0 / D).then_inc(root_made, 1)

            def recurrent(inst, layer, norm):
                o = first_out["mix", layer]
                act.activation(M["rec_cl"][:, 0, :], table[:, names["a_lambda"] + RT * inst:names["a_lambda"] + RT * inst + RT],
                               ACT.Exp, scale=-1.0).then_inc(rec_cl_exp, 1)
                act.wait_ge(rec_cl_exp, inst + 1)
                act.activation(M["rec_cl"][:, 1, :], M["rec_cl"][:, 0, :], ACT.Ln, bias=col("one")).then_inc(rec_cl_ln, 1)
                norm_root(norm)
                for half in range(2):
                    ms = range(HALF * half, HALF * half + HALF)
                    for m in ms:
                        act.wait_ge(rec_conv, A_TAPS * (RT * inst + m + 1))
                        act.activation(M["rec_hi"][:, m, :], M["rec_x"][:, m, :], ACT.Copy).then_inc(rec_hi_made, 1)
                    o += HALF
                    for i, m in enumerate(ms):
                        if half == 1 or inst == 1:
                            act.wait_ge(rec_y, RT * inst + HALF * half)
                        wait_made(act, o)
                        act.activation(M["rec_a"][:, i, :], bank(o), ACT.Sigmoid,
                                       bias=col("a_gate_a_b", RT * inst + m)).then_inc(out_taken[o % BANKS], 1)
                        wait_made(act, o + 1)
                        act.activation(M["rec_u"][:, i, :], bank(o + 1), ACT.Sigmoid,
                                       bias=col("a_gate_x_b", RT * inst + m)).then_inc(out_taken[(o + 1) % BANKS], 1)
                        o += 2
                    act.wait_ge(rec_cl_made, 2 * inst + 2)
                    done = RT * inst + HALF * half
                    for i, m in enumerate(ms):
                        act.wait_ge(rec_xi_made, done + i + 1)
                        wait_taken(act, o - 2)
                        act.activation(M["rec_u"][:, i, :], M["rec_a"][:, i, :], ACT.Tanh,
                                       scale=M["rec_cl"][:, 2, m:m + 1]).then_inc(rec_tanh, 1)
                        act.wait_ge(rec_tanh, done + i + 1)
                        act.activation(M["rec_a"][:, i, :], M["rec_a"][:, i, :], ACT.Exp,
                                       scale=M["rec_cl"][:, 3, m:m + 1]).then_inc(rec_decay, 1)
                    for i, m in enumerate(ms):
                        act.wait_ge(rec_ratio, 3 * (done + i + 1))
                        act.activation(M["rec_u"][:, i, :], M["rec_u"][:, i, :], ACT.Sqrt, scale=2.0).then_inc(rec_sqrt, 1)
                    for i, m in enumerate(ms):
                        wait_taken(act, o + i)
                        act.activation(M["rec_gate"][:, i, :], M["rec_gate"][:, i, :], ACT.Gelu_apprx_tanh).then_inc(rec_gelu, 1)
                    o += HALF
                    for i, m in enumerate(ms):
                        act.wait_ge(rec_y, done + i + 1)
                        if i == 0:
                            wait_made(act, o - HALF - 1)
                        act.activation(M["rec_hi"][:, m, :], M["rec_u"][:, i, :], ACT.Copy).then_inc(rec_hi_made, 1)

            def spatial(layer, norm):
                o = first_out["mix", layer]
                act.dma_start(M["sgu_w"][:, :, :], io["sgu_w"]).then_inc(sgu_in, 16)
                act.dma_start(M["sgu_bias"][:, :, :], io["sgu_bias"]).then_inc(sgu_in, 16)
                norm_root(norm)
                act.wait_ge(sgu_col_taken, 1)
                for half in range(2):
                    for tb in range(4):
                        wait_made(act, o)
                        act.activation(M["sgu_v"][:, tb, 512 * half:512 * half + 512], bank(o), ACT.Gelu_apprx_tanh,
                                       scale=M["sgu_stat"][:, 0, tb:tb + 1]).then_inc(out_taken[o % BANKS], 1)
                        o += 1
                for tb in range(4):
                    wait_taken(act, o - 4 + tb)
                    if tb:
                        act.wait_ge(sgu_sq_made, tb)
                    act.activation(M["sgu_sq"][:, :], M["sgu_v"][:, tb, :], ACT.Square,
                                   accum_out=M["sgu_stat"][:, 1, tb:tb + 1]).then_inc(sgu_sq_made, 1)
                act.wait_ge(sgu_sq_made, 4)
                act.activation(M["sgu_stat"][:, 2, :], M["sgu_stat"][:, 1, :], ACT.Sqrt, bias=col("eps"),
                               scale=1.0 / D).then_inc(sgu_root, 1)
                for m in range(KT):
                    wait_taken(act, o)
                    act.activation(M["sgu_u"][:, m, :], M["sgu_u"][:, m, :], ACT.Gelu_apprx_tanh).then_inc(sgu_u_made, 1)
                    o += 1
                for m in range(KT):
                    act.wait_ge(sgu_y_made, m + 1)
                    act.activation(M["sgu_hi"][:, m, :], M["sgu_y"][:, m % 2, :], ACT.Copy).then_inc(sgu_hi_made, 1)

            def short_conv(layer, norm):
                norm_root(norm)
                for m in range(KT):
                    act.wait_ge(cnv_y, m + 1)
                    act.activation(M["cnv_hi"][:, m, :], M["cnv_c"][:, m % 2, :], ACT.Copy).then_inc(cnv_hi_made, 1)

            def hidden(o, j, half, made, turn=None):
                wait_taken(act, o, turn)
                if made >= 4:
                    act.wait_ge(hid_lo_made, turn.value(made - 3) if turn else made - 3)
                act.activation(M["hidden"][:, o % 4, :], M["relu"][:, o % 4, :], ACT.Square)
                act.activation(M["hid_hi"][:, half, j, :] if turn is None else
                               M["hid_hi"][:, half, bass.ds(turn.it * SLOTS + j, 1), :].rearrange("p a t -> p (a t)"),
                               M["relu"][:, o % 4, :], ACT.Square).then_inc(hid_hi_made, 1)

            def mlp(layer, norm):
                o = first_out["mlp", layer]
                norm_root(norm)
                for j in range(8):
                    hidden(o + j, j, 0, FF2 * layer + j)
                o += 8
                turn = Turn()
                for group in range(1, UG):
                    with act.Fori(0, 2) as it:
                        turn.it, turn.rate = it, SLOTS
                        for j in range(SLOTS):
                            hidden(o + j, j, group % 2, FF2 * layer + 8 * group + j, turn)
                    o += 16

            def gain_at(gain, k):
                name, layer = gain
                return name, KT * layer + k

            if start_x:
                act.wait_ge(const_in, CONSTS)
                for k in range(KT):
                    feed(k, NORM0, ("norm_mix", 0), lambda k: act.wait_ge(x_in, 16 * KT), None)
            else:
                first_block_act(act, feed)
            norm = NORM0
            for layer in range(LAYERS)[:upto]:
                (lambda l, n: recurrent(l // 3, l, n), spatial, short_conv)[layer % 3](layer, norm)
                o = mix_down(layer)
                for k in range(KT):
                    feed(k, norm + 1, ("norm_mlp", layer), lambda k: wait_taken(act, o + k), o)
                mlp(layer, norm + 1)
                norm += 2
                o = mlp_down(layer)
                last = layer == len(range(LAYERS)[:upto]) - 1
                for k in range(KT):
                    feed(k, norm, None if last else ("norm_mix", layer + 1), lambda k: wait_taken(act, o + k), o)
            norm_root(norm)

        @block.vector
        def _(dve):
            def feed(k, norm, h=True):
                dve.wait_ge(squared, KT * norm + k + 1)
                if k == 0:
                    if norm:
                        dve.wait_ge(stat_made, norm)
                    dve.tensor_copy(square_sum[:, :], square[:, 0, :]).then_inc(summed, 1)
                else:
                    dve.wait_ge(summed, KT * norm + k)
                    dve.tensor_tensor(square_sum[:, :], square_sum[:, :], square[:, k % 2, :], ALU.add).then_inc(summed, 1)
                return h

            def feed_low(k, norm, gain):
                name, layer = gain
                dve.wait_ge(h_hi_made, KT * norm + k + 1 - H_SKIP)
                dve.scalar_tensor_tensor(out=h_lo[:, k, :], in0=x[:, k, :], scalar=col(name, KT * layer + k),
                                         in1=h_hi[:, k, :].bitcast(F32), op0=ALU.mult, op1=ALU.subtract).then_inc(h_lo_made, 1)

            def norm_rstd(norm):
                dve.wait_ge(root_made, norm + 1)
                dve.reciprocal(rstd[:, :], root[:, :]).then_inc(rstd_made, 1)
                dve.wait_ge(rstd_made, norm + 1)

            def add_to_x(o, k, turn=None):
                wait_made(dve, o, turn)
                tile = x[:, k, :] if turn is None else x[:, bass.ds(turn.it * SLOTS + k, 1), :].rearrange("p a t -> p (a t)")
                dve.tensor_tensor(tile, bank(o), tile, ALU.add).then_inc(out_taken[o % BANKS], 1)

            def taken(o, turn=None):
                wait_taken(dve, o, turn)

            def split_low(lo, whole_, hi, made_sem):
                dve.tensor_tensor(lo, whole_, hi.bitcast(F32), ALU.subtract).then_inc(made_sem, 1)

            def recurrent(inst, layer, norm):
                o = first_out["mix", layer]
                dve.memset(M["rec_in"][:, :, 0:A_TAPS - 1], 0.0).then_inc(rec_zeroed, 1)
                dve.wait_ge(rec_cl_ln, inst + 1)
                dve.tensor_scalar(M["rec_cl"][:, 2, :], M["rec_cl"][:, 1, :], 8.0, None, ALU.mult).then_inc(rec_cl_made, 1)
                dve.tensor_scalar(M["rec_cl"][:, 3, :], M["rec_cl"][:, 1, :], -8.0, None, ALU.mult).then_inc(rec_cl_made, 1)
                dve.wait_ge(rec_zeroed, inst + 1)
                norm_rstd(norm)
                steps = A_TAPS * RT * inst

                def low_x(m):
                    dve.wait_ge(rec_hi_made, rec_x_lo(inst, m))
                    split_low(M["rec_lo"][:, m, :], M["rec_x"][:, m, :], M["rec_hi"][:, m, :], rec_lo_made)

                for half in range(2):
                    ms = range(HALF * half, HALF * half + HALF)
                    done = RT * inst + HALF * half
                    for m in ms:
                        wait_made(dve, o)
                        if m >= 1:
                            dve.wait_ge(rec_conv, A_TAPS * (RT * inst + m))
                        xin = M["rec_in"][:, m % 3, :]
                        dve.tensor_tensor(xin[:, A_TAPS - 1:], bank(o), rstd[:, :], ALU.mult).then_inc(out_taken[o % BANKS], 1)
                        taken(o)
                        w = [col("a_conv_w", (A_TAPS * inst + j) * RT + m) for j in range(A_TAPS)]
                        dve.tensor_scalar(M["rec_x"][:, m, :], xin[:, 0:T], w[0], col("a_conv_b", RT * inst + m),
                                          ALU.mult, ALU.add).then_inc(rec_conv, 1)
                        for j in range(1, A_TAPS):
                            dve.wait_ge(rec_conv, A_TAPS * (RT * inst + m) + j)
                            dve.scalar_tensor_tensor(out=M["rec_x"][:, m, :], in0=xin[:, j:j + T], scalar=w[j],
                                                     in1=M["rec_x"][:, m, :], op0=ALU.mult, op1=ALU.add).then_inc(rec_conv, 1)
                        o += 1
                        if m > ms[0]:
                            low_x(m - 1)
                    low_x(ms[-1])
                    for i, m in enumerate(ms):
                        taken(o + 1)
                        dve.tensor_tensor(M["rec_x"][:, m, :], M["rec_x"][:, m, :], M["rec_u"][:, i, :],
                                          ALU.mult).then_inc(rec_xi_made, 1)
                        o += 2

                    def take_gate(i):
                        wait_made(dve, o + i)
                        if i == 0 and done:
                            dve.wait_ge(rec_y, done)
                        dve.tensor_tensor(M["rec_gate"][:, i, :], bank(o + i), rstd[:, :], ALU.mult)\
                           .then_inc(out_taken[(o + i) % BANKS], 1)

                    for i in range(HALF):
                        u, spare = M["rec_u"][:, i, :], M["rec_in"][:, i % 2, A_TAPS - 1:]
                        base = 3 * (done + i)
                        dve.wait_ge(rec_decay, done + i + 1)
                        if base:
                            dve.wait_ge(rec_ratio, base)
                        dve.tensor_scalar(spare, u, 1.0, None, ALU.add).then_inc(rec_ratio, 1)
                        dve.wait_ge(rec_ratio, base + 1)
                        dve.reciprocal(spare, spare).then_inc(rec_ratio, 1)
                        dve.wait_ge(rec_ratio, base + 2)
                        dve.tensor_tensor(u, u, spare, ALU.mult).then_inc(rec_ratio, 1)
                        if i >= 1:
                            take_gate(i - 1)
                    take_gate(HALF - 1)
                    for i, m in enumerate(ms):
                        u, a = M["rec_u"][:, i, :], M["rec_a"][:, i, :]
                        base = 2 * (done + i)
                        dve.wait_ge(rec_sqrt, done + i + 1)
                        dve.wait_ge(rec_xi_made, done + i + 1)
                        dve.tensor_tensor(M["rec_x"][:, m, :], u, M["rec_x"][:, m, :], ALU.mult).then_inc(rec_scan, 1)
                        dve.wait_ge(rec_scan, base + 1)
                        dve.tensor_tensor_scan(u, a, M["rec_x"][:, m, :], 0.0, ALU.mult, ALU.add).then_inc(rec_scan, 1)
                        dve.wait_ge(rec_scan, base + 2)
                        dve.wait_ge(rec_gelu, done + i + 1)
                        dve.tensor_tensor(u, u, M["rec_gate"][:, i, :], ALU.mult).then_inc(rec_y, 1)
                    o += HALF
                    for i, m in enumerate(ms):
                        dve.wait_ge(rec_y, done + i + 1)
                        dve.wait_ge(rec_hi_made, hi_count(inst, half, i))
                        split_low(M["rec_lo"][:, m, :], M["rec_u"][:, i, :], M["rec_hi"][:, m, :], rec_lo_made)
                return o

            def hi_count(inst, half, i):
                return 2 * RT * inst + 2 * HALF * half + HALF + i + 1

            def spatial(layer, norm):
                o = first_out["mix", layer]
                dve.wait_ge(sgu_in, 32)
                for g in range(SG):
                    dve.tensor_tensor(M["sgu_w"][:, g, :], M["sgu_w"][:, g, :], sgu_mask[:, :], ALU.mult)\
                       .then_inc(sgu_masked if g == SG - 1 else sgu_norm, 1)
                norm_rstd(norm)
                dve.wait_ge(sgu_col, 1)
                dve.tensor_copy(M["sgu_stat"][:, 0, :], side[:, 0, 0:4]).then_inc(sgu_col_taken, 1)
                o += 8
                dve.wait_ge(sgu_root, 1)
                dve.reciprocal(M["sgu_stat"][:, 3, :], M["sgu_stat"][:, 2, :]).then_inc(sgu_norm, 1)
                dve.wait_ge(sgu_norm, SG)
                for tb in range(4):
                    dve.tensor_scalar(M["sgu_v"][:, tb, :], M["sgu_v"][:, tb, :], M["sgu_stat"][:, 3, tb:tb + 1], None,
                                      ALU.mult).then_inc(sgu_v_norm, 1)
                for m in range(KT):
                    wait_made(dve, o)
                    dve.tensor_tensor(M["sgu_u"][:, m, :], bank(o), rstd[:, :], ALU.mult).then_inc(out_taken[o % BANKS], 1)
                    o += 1
                for g in range(SG):
                    y = M["sgu_y"][:, g % 2, :]
                    wait_made(dve, o)
                    if g >= 1:
                        dve.wait_ge(sgu_lo_made, g)
                    for tb in range(4):
                        ins = dve.scalar_tensor_tensor(out=y[:, P * tb:P * tb + P], in0=bank(o)[:, P * tb:P * tb + P],
                                                       scalar=col("b_norm_g", g), in1=M["sgu_bias"][:, g, :],
                                                       op0=ALU.mult, op1=ALU.add)
                    ins.then_inc(out_taken[o % BANKS], 1)
                    taken(o)
                    dve.wait_ge(sgu_u_made, g + 1)
                    dve.tensor_tensor(y, y, M["sgu_u"][:, g, :], ALU.mult).then_inc(sgu_y_made, 1)
                    dve.wait_ge(sgu_y_made, g + 1)
                    dve.wait_ge(sgu_hi_made, g + 1)
                    split_low(M["sgu_lo"][:, g, :], y, M["sgu_hi"][:, g, :], sgu_lo_made)
                    o += 1
                return o

            def short_conv(layer, norm):
                o = first_out["mix", layer]
                dve.memset(M["cnv_p"][:, :, 0:C_TAPS - 1], 0.0).then_inc(cnv_zeroed, 1)
                norm_rstd(norm)
                dve.wait_ge(cnv_zeroed, 1)
                for m in range(KT):
                    s = m % 2
                    g, c, p, b, xv = (M[n][:, s, :] for n in ("cnv_g", "cnv_c", "cnv_p", "cnv_b", "cnv_x"))
                    if m:
                        dve.wait_ge(cnv_lo_made, m)
                    wait_made(dve, o)
                    dve.tensor_tensor(g, bank(o), rstd[:, :], ALU.mult).then_inc(out_taken[o % BANKS], 1)
                    taken(o)
                    wait_made(dve, o + 1)
                    dve.tensor_tensor(xv, bank(o + 1), rstd[:, :], ALU.mult).then_inc(out_taken[(o + 1) % BANKS], 1)
                    taken(o + 1)
                    n0 = (C_TAPS + 1) * m
                    dve.tensor_tensor(p[:, C_TAPS - 1:], xv, g, ALU.mult).then_inc(cnv_step, 1)
                    dve.wait_ge(cnv_step, n0 + 1)
                    w = [col("c_conv_w", KT * j + m) for j in range(C_TAPS)]
                    dve.tensor_scalar(c, p[:, 0:T], w[0], None, ALU.mult).then_inc(cnv_step, 1)
                    for j in range(1, C_TAPS):
                        dve.wait_ge(cnv_step, n0 + 1 + j)
                        dve.scalar_tensor_tensor(out=c, in0=p[:, j:j + T], scalar=w[j], in1=c,
                                                 op0=ALU.mult, op1=ALU.add).then_inc(cnv_step, 1)
                    wait_made(dve, o + 2)
                    dve.tensor_tensor(b, bank(o + 2), rstd[:, :], ALU.mult).then_inc(out_taken[(o + 2) % BANKS], 1)
                    taken(o + 2)
                    dve.wait_ge(cnv_step, n0 + 1 + C_TAPS)
                    dve.tensor_tensor(c, c, b, ALU.mult).then_inc(cnv_y, 1)
                    dve.wait_ge(cnv_y, m + 1)
                    dve.wait_ge(cnv_hi_made, m + 1)
                    split_low(M["cnv_lo"][:, m, :], c, M["cnv_hi"][:, m, :], cnv_lo_made)
                    o += 3
                return o

            def hidden(o, j, half, made, turn=None):
                wait_made(dve, o, turn)
                if made:
                    dve.wait_ge(hid_lo_made, turn.value(made) if turn else made)
                dve.scalar_tensor_tensor(out=M["relu"][:, o % 4, :], in0=bank(o), scalar=0.0, in1=rstd[:, :],
                                         op0=ALU.max, op1=ALU.mult).then_inc(out_taken[o % BANKS], 1)
                dve.wait_ge(hid_hi_made, turn.value(made + 1) if turn else made + 1)
                if turn is None:
                    hi, lo = M["hid_hi"][:, half, j, :], M["hid_lo"][:, half, j, :]
                else:
                    hi, lo = (M[n][:, half, bass.ds(turn.it * SLOTS + j, 1), :].rearrange("p a t -> p (a t)")
                              for n in ("hid_hi", "hid_lo"))
                split_low(lo, M["hidden"][:, o % 4, :], hi, hid_lo_made)

            def mlp(layer, norm):
                o = first_out["mlp", layer]
                norm_rstd(norm)
                for j in range(8):
                    hidden(o + j, j, 0, FF2 * layer + j)
                o += 8
                turn = Turn()
                for group in range(1, UG + 1):
                    if group < UG:
                        with dve.Fori(0, 2) as it:
                            turn.it, turn.rate = it, SLOTS
                            for j in range(SLOTS):
                                hidden(o + j, j, group % 2, FF2 * layer + 8 * group + j, turn)
                        o += 8
                        dve.wait_ge(hid_lo_made, FF2 * layer + 8 * (group + 1))
                        with dve.Fori(0, 2) as it:
                            turn.it = it
                            for k in range(SLOTS):
                                add_to_x(o + k, k, turn)
                        o += 8
                taken(o - 1)
                return o

            def add_and_feed(o, norm, gain):
                for k in range(KT + 1):
                    if k < KT:
                        add_to_x(o + k, k)
                    if k:
                        feed(k - 1, norm)
                        if gain is not None:
                            feed_low(k - 1, norm, gain)

            dve.wait_ge(const_in, CONSTS)
            if start_x:
                dve.wait_ge(x_in, 16 * KT)
                for k in range(KT):
                    feed(k, NORM0)
                    feed_low(k, NORM0, ("norm_mix", 0))
            else:
                first_block_dve(dve, feed, feed_low)
            norm = NORM0
            for layer in range(LAYERS)[:upto]:
                o = (lambda l, n: recurrent(l // 3, l, n), spatial, short_conv)[layer % 3](layer, norm)
                assert o == mix_down(layer)
                add_and_feed(o, norm + 1, ("norm_mlp", layer))
                o = mlp(layer, norm + 1)
                assert o == mlp_down(layer)
                norm += 2
                last = layer == len(range(LAYERS)[:upto]) - 1
                add_and_feed(o, norm, None if last else ("norm_mix", layer + 1))
            norm_rstd(norm)
            for k in range(KT):
                dve.scalar_tensor_tensor(out=x[:, k, :], in0=x[:, k, :], scalar=col("last_g", k), in1=rstd[:, :],
                                         op0=ALU.mult, op1=ALU.mult).then_inc(scaled, 1)


def panels_by_column(w, k0, kt, m):
    return w[P * k0:P * (k0 + kt), P * m:P * (m + 1)].reshape(kt, P, P)


def packed(tiles):
    n = len(tiles)
    pad = -n % TP
    if pad:
        tiles = np.concatenate([tiles, np.zeros((pad, P, P), tiles.dtype)])
    return tiles.reshape(-1, TP, P, P).transpose(0, 2, 1, 3)


def moving(w, k0, kt, c0, cols):
    part = w[P * k0:P * (k0 + kt), c0:c0 + cols]
    return part.reshape(kt, P, cols // P, P).transpose(0, 2, 1, 3).reshape(-1, P, P)


def block_diagonal(gate_w, m, k):
    tile = np.zeros((P, P), gate_w.dtype)
    for h in range(gate_w.shape[0]):
        r0, r1 = max(80 * h, P * k), min(80 * h + 80, P * k + P)
        c0, c1 = max(80 * h, P * m), min(80 * h + 80, P * m + P)
        if r0 < r1 and c0 < c1:
            tile[r0 - P * k:r1 - P * k, c0 - P * m:c1 - P * m] = gate_w[h, r0 - 80 * h:r1 - 80 * h, c0 - 80 * h:c1 - 80 * h]
    return tile


def second_block_panels(g):
    out = []
    for layer in range(LAYERS):
        kind, j = layer % 3, layer // 3
        if kind == 0:
            w_in, w_out = g["a_w_in_2"][j], g["a_w_out_2"][j]
            for half in range(2):
                ms = range(HALF * half, HALF * half + HALF)
                for m in ms:
                    out.append(packed(panels_by_column(w_in, 0, KT, RT + m)))
                tiles = [block_diagonal(g[n][j], m, k) for m in ms for n in ("a_gate_a_w_2", "a_gate_x_w_2") for k in BD[m]]
                out.append(packed(np.stack(tiles)))
                for m in ms:
                    out.append(packed(panels_by_column(w_in, 0, KT, m)))
            tiles = [panels_by_column(w_out, 0, RT, m) for m in range(KT)]
            out.append(packed(np.concatenate(tiles)))
        elif kind == 1:
            w_in, w_out = g["b_w_in_2"][j], g["b_w_out_2"][j]
            for half in range(2):
                for k in range(0, KT, 2):
                    out.append(packed(moving(w_in, k, 2, D + 512 * half, 512)))
            for m in range(KT):
                out.append(packed(panels_by_column(w_in, 0, KT, m)))
            for m in range(KT):
                out.append(packed(panels_by_column(w_out, 0, KT, m)))
        else:
            w_in, w_out = g["c_w_in_2"][j], g["c_w_out_2"][j]
            for m in range(KT):
                for part in (1, 2, 0):
                    out.append(packed(panels_by_column(w_in, 0, KT, KT * part + m)))
            for m in range(KT):
                out.append(packed(panels_by_column(w_out, 0, KT, m)))
        w1, w2 = g["mlp_w1_2"][layer], g["mlp_w2_2"][layer]
        up = [packed(panels_by_column(w1, 0, KT, m)) for m in range(FF2)]
        for group in range(UG + 1):
            if group < UG:
                out += up[8 * group:8 * group + 8]
            if group:
                out += [packed(panels_by_column(w2, 8 * (group - 1), 8, m)) for m in range(KT)]
    return out


def features(a):
    return np.asarray(a).reshape(-1, P).T


def second_table(g):
    return {
        "norm_mix": features(g["norm_mix_g_2"]), "norm_mlp": features(g["norm_mlp_g_2"]),
        "last_g": features(g["final_norm_g_2"]), "a_conv_w": features(g["a_conv_w_2"]),
        "a_conv_b": features(g["a_conv_b_2"]), "a_gate_a_b": features(g["a_gate_a_b_2"]),
        "a_gate_x_b": features(g["a_gate_x_b_2"]), "a_lambda": features(g["a_lambda_2"]),
        "b_norm_g": features(g["b_norm_g_2"]), "c_conv_w": features(g["c_conv_w_2"]),
        "eps": np.full((P, 1), EPS, np.float32), "one": np.ones((P, 1), np.float32),
    }


def second_constants(g):
    w_s, bias = g["b_w_s_2"][0], g["b_s_bias_2"][0]
    s = np.arange(P)
    return {
        "ones": np.ones((P, P), np.float32),
        "sgu_mask": (s[:, None] <= s[None, :]).astype(np.float32),
        "sgu_w": w_s.transpose(2, 0, 1), "sgu_bias": np.broadcast_to(bias[None], (P, SG, P)),
    }


def input_columns(w_in):
    sizes = {"q": 384, "kv": 256, "rope": ROPE, "gq": 512, "gk": 512, "gv": 512, "gr": 512, "glow": 32, "gates": 2 * D}
    out, at = {}, 0
    for name, size in sizes.items():
        out[name] = w_in[:, at:at + size]
        at += size
    return out


PARTNER = np.array([16 * (r // 16) + (r + 8) % 16 for r in range(ROPE)])


def first_block_panels(g):
    w = input_columns(g["w_in"][0])
    zero = np.zeros((D, 16), w["q"].dtype)
    misc = np.concatenate([w["glow"][:, :16], zero, w["glow"][:, 16:], zero, w["rope"], w["rope"][:, PARTNER]], 1)
    out = [packed(panels_by_column(misc, 0, KT, 0))]
    out += [packed(panels_by_column(w["kv"], 0, KT, m)) for m in range(KVL)]
    out += [packed(panels_by_column(w["q"], 0, KT, m)) for m in range(QL)]
    out += [packed(moving(w["gv"], k, 2, 0, GH * P)) for k in range(0, KT, 2)]
    for h in range(GH):
        out += [packed(panels_by_column(w[n], 0, KT, h)) for n in ("gk", "gq", "gr")]
    uq = g["w_uq"][0].reshape(QL * P, HEADS, QK)
    uq = np.concatenate([uq, uq[:, :, NOPE + PARTNER]], 2).reshape(QL * P, HEADS * P)
    out.append(packed(np.concatenate([panels_by_column(uq, 0, QL, h) for h in range(HEADS)])))
    ukv = g["w_ukv"][0].reshape(KVL * P, HEADS, 2, 64)
    uk, uv = (ukv[:, :, i].reshape(KVL * P, HEADS * 64) for i in range(2))
    out.append(packed(np.concatenate([panels_by_column(uk, 0, KVL, m) for m in range(HEADS // 2)])))
    out.append(packed(moving(uv, 0, KVL, 0, HEADS * 64)))
    for m in range(KT):
        out += [packed(panels_by_column(w["gates"], 0, KT, i * KT + m)) for i in range(2)]
        out.append(packed(np.concatenate([panels_by_column(g[n][0], 0, 4, m) for n in ("w_br_mla", "w_br_gla")])))
    out += [packed(panels_by_column(g["w_out"][0], 0, KT, m)) for m in range(KT)]

    def up(group):
        return [packed(panels_by_column(g["w_up"][0], 0, KT, i * FF1 + j)) for j in FF1_GROUPS[group] for i in (1, 0)]

    def down(group):
        js = FF1_GROUPS[group]
        return [packed(np.concatenate([panels_by_column(g["w_down"][0], js[0], len(js), m) for m in range(KT)]))]

    return out + up(0) + up(1) + down(0) + up(2) + down(1) + down(2)


def first_table(g):
    return {
        "b_ada": features(g["b_ada"]), "norm1": features(g["norm1_g"]), "norm2": features(g["norm2_g"]),
        "q_norm": features(g["q_norm_g"]), "kv_norm": features(g["kv_norm_g"]), "b_decay": features(g["gla_b_decay"]),
        "gla_norm": features(g["gla_norm_g"]), "conv_w": features(g["conv_w"]), "conv_b": features(g["conv_b"]),
        "final1": features(g["final_g"]),
    }


def first_constants(g):
    t = np.arange(T)
    inv_freq = (10000.0 ** (-np.arange(0, 16, 2, dtype=np.float32) / 16)).astype(np.float32)
    place = [(t // GRID_W).astype(np.float32), (t % GRID_W).astype(np.float32)]
    rope = np.zeros((P, T), np.float32)
    for r in range(ROPE):
        angle = place[r // 16] * inv_freq[r % 8]
        rope[64 + r] = np.cos(angle)
        rope[96 + r] = np.sin(angle) * (-1 if r % 16 < 8 else 1)
    s, c = np.arange(P)[:, None], np.arange(P)[None, :]
    same = s // CHUNK == c // CHUNK
    decay_w = np.zeros((48, GH * P), g["gla_w_decay"].dtype)
    decay_w[0:16], decay_w[32:48] = g["gla_w_decay"][0, 0], g["gla_w_decay"][0, 1]
    tiles = lambda a: np.asarray(a).T.reshape(KT, P, -1).transpose(1, 0, 2)
    return {
        "x": tiles(g["x"][0]), "ctx": tiles(g["ctx"][0]),
        "cvec": tiles(np.stack([g["c"][0], g["c_ctx"]])),
        "identity": np.eye(P, dtype=np.float32), "rope": rope, "decay_w": decay_w,
        "intra_mask": np.stack([same & (s <= c), same & (s >= c)], 1).astype(np.float32),
        "reset": np.broadcast_to((np.arange(TC + 1) % CHUNK != 0).astype(np.float32), (P, TC + 1)),
        "ada": np.concatenate([packed(panels_by_column(g["w_ada"][0], 0, KT, m)) for m in range(6 * KT)]),
    }


def kernel(**inputs):
    import concourse.bacc as bacc
    from concourse.bass_utils import run_bass_kernel_spmd

    g = {name: np.asarray(a) for name, a in inputs.items()}
    columns = first_table(g) | second_table(g)
    names, width = {}, 0
    for name, part in columns.items():
        names[name] = width
        width += part.shape[1]
    names["width"] = width
    data = first_constants(g) | second_constants(g)
    data["table"] = np.concatenate(list(columns.values()), 1)
    data["weights"] = np.concatenate(first_block_panels(g) + second_block_panels(g))
    data = {name: np.ascontiguousarray(a) for name, a in data.items()}

    nc = bacc.Bacc("TRN2", target_bir_lowering=False, num_devices=1)
    io = {name: nc.dram_tensor(f"in_{name}", a.shape, F32, kind="ExternalInput").ap() for name, a in data.items()}
    io["out"] = nc.dram_tensor("out", (P, KT, T), F32, kind="ExternalOutput").ap()
    build(nc, io, names)
    result = run_bass_kernel_spmd(nc, [{f"in_{name}": a for name, a in data.items()}], core_ids=[0])
    out = result.results[0]["out"]
    return np.ascontiguousarray(out.transpose(1, 0, 2).reshape(D, T).T).reshape(1, T, D)
```

```python
from contextlib import ExitStack

import numpy as np

import concourse.bass as bass
from concourse import mybir

F32 = mybir.dt.float32
F32R = mybir.dt.float32r
ALU = mybir.AluOpType
ACT = mybir.ActivationFunctionType
AX = mybir.AxisListType

P = 128
D = 1024
KT = D // P
T = 512
C = 256
TC = T + C
EPS = 1e-6
SLOTS = 4
BANKS = 4
TP = 8

LAYERS = 4
RT = 1280 // P
HALF = RT // 2
FF2 = 4 * D // P
UG = FF2 // 8
A_TAPS = 4
C_TAPS = 3
SG = 8


def block_diagonal_inputs(m):
    first = (P * m // 80) * 80
    last = ((P * m + P - 1) // 80 + 1) * 80 - 1
    return list(range(first // P, last // P + 1))


BD = [block_diagonal_inputs(m) for m in range(RT)]
BD_HALF_PANELS = -(-2 * sum(len(BD[m]) for m in range(HALF)) // TP)

SPATIAL_ORDER = [("u", m) for m in range(3)]
for group in range(SG):
    SPATIAL_ORDER.append(("mixed", group))
    if group + 3 < SG:
        SPATIAL_ORDER.append(("u", group + 3))

QL, KVL = 384 // P, 256 // P
HEADS, NOPE, ROPE = 8, 64, 32
QK = NOPE + ROPE
MLA_SCALE = float(QK) ** -0.5
GH = 4
GLA_SCALE = float(P) ** -0.5
GATE_NORM = 16.0
CHUNK = 64
NCH = TC // CHUNK
FF1 = 2816 // P
FF1_GROUPS = [range(0, 8), range(8, 16), range(16, FF1)]
GRID_W, GRID_H = 64, T // 64
ADA_SLOTS = 4
ADA_FIRST = 2 * KT
LEAD = 16
KB = TC // P

OUT_Q = 0
OUT_AHEAD = OUT_Q + QL
AHEAD = [("q", 0), ("r", 0), ("r", 1)]
OUT_MISC = OUT_AHEAD + len(AHEAD)
OUT_KV = OUT_MISC + 2
OUT_GV = OUT_KV + 2 * KVL
OUT_QNORM = OUT_GV + 4
OUT_KVNORM = OUT_QNORM + 1
GLA_STEPS = 2 * GH


def gla_outputs():
    at, n = {part: OUT_AHEAD + i for i, part in enumerate(AHEAD)}, OUT_KVNORM + 2
    for name, i, count in gla_order():
        at[name, i] = n
        n += count
    return at, n


def gla_order():
    order = [("gate", 0, 2), ("k", 0, 2)]
    for u in range(GLA_STEPS):
        h, d = u // 2, u % 2
        order.append(("turned", u, 2))
        if u + 1 < GLA_STEPS:
            order.append(("gate", u + 1, 2))
        order += [("intra", u, 1), ("added", u, 4)]
        if h + 1 < GH:
            fill = [("q", h + 1, 1), ("r", h + 1, 1)] if d == 0 else [("k", h + 1, 2)]
            order += [part for part in fill if part[:2] not in AHEAD]
        if d == 1 and h + 1 < GH:
            order.append(("sum", h, 1))
    return order


OUT_GLA, OUT_QH = gla_outputs()
OUT_GLA["sum", GH - 1] = OUT_QH + HEADS
OUT_KH = OUT_QH + HEADS + 1
OUT_V = OUT_KH + HEADS
OUT_ATT = OUT_V + KB
OUT_ATT += OUT_ATT % 2
UNITS = 4 * HEADS


def out_scores(u):
    return OUT_ATT + 2 * u


OUT_MERGE = OUT_ATT + 2 * UNITS
OUT_MIX = OUT_MERGE + 4 * KT
OUT_FF = OUT_MIX + KT


def out_ff_up(group):
    return OUT_FF + sum(2 * len(FF1_GROUPS[g]) for g in range(group)) + KT * max(group - 1, 0)


def out_ff_down(group):
    return OUT_FF + sum(2 * len(FF1_GROUPS[g]) for g in range(min(group + 2, 3))) + KT * group


FIRST_OUTS = out_ff_down(2) + KT
FIRST_NORMS = 4


class Turn:

    def __init__(self):
        self.out = 0
        self.it = None
        self.rate = 0

    def value(self, count, per_turn=None):
        if self.it is None:
            return count
        return self.it * (self.rate if per_turn is None else per_turn) + count


def build(nc, io, names, upto=None, start_x=False):
    n_panels = io["weights"].shape[0]
    with ExitStack() as whole:
        def sem(name):
            return whole.enter_context(nc.semaphore(name))

        def sb(name, shape, dt=F32):
            return whole.enter_context(nc.sbuf_tensor(name, shape, dt))

        x = sb("x", [P, KT, T])
        h_hi = sb("h_hi", [P, KT, T], F32R)
        h_lo = sb("h_lo", [P, KT, T], F32R)
        w_raw = sb("w_raw", [P, SLOTS, TP * P])
        w_hi = sb("w_hi", [P, SLOTS, TP * P], F32R)
        w_lo = sb("w_lo", [P, SLOTS, TP * P], F32R)
        table = sb("table", [P, names["width"]])
        ones = sb("ones", [P, P])
        sgu_mask = sb("sgu_mask", [P, P])
        square = sb("square", [P, 2, T])
        square_sum = sb("square_sum", [P, T])
        root = sb("root", [P, T])
        rstd = sb("rstd", [P, T])

        def col(name, i=0):
            return table[:, names[name] + i:names[name] + i + 1]

        memory = {}
        def overlay(part, **tensors):
            with ExitStack() as stage:
                for name, (shape, dt) in tensors.items():
                    memory[name] = stage.enter_context(nc.sbuf_tensor(f"{part}_{name}", shape, dt))

        overlay("rec", rec_in=([P, 3, A_TAPS - 1 + T], F32), rec_x=([P, RT, T], F32),
                rec_hi=([P, RT, T], F32R), rec_lo=([P, RT, T], F32R),
                rec_a=([P, HALF, T], F32), rec_u=([P, HALF, T], F32), rec_gate=([P, HALF, T], F32),
                rec_cl=([P, 4, RT], F32))
        overlay("mlp", hid_hi=([P, 2, 8, T], F32R), hid_lo=([P, 2, 8, T], F32R),
                relu=([P, 4, T], F32), hidden=([P, 4, T], F32))
        overlay("sgu", sgu_v=([P, 4, D], F32), sgu_u=([P, KT, T], F32), sgu_w=([P, SG, P], F32),
                sgu_bias=([P, SG, P], F32), sgu_hi=([P, KT, T], F32R), sgu_lo=([P, KT, T], F32R),
                sgu_stat=([P, 4, 4], F32), sgu_sq=([P, D], F32), sgu_y=([P, 2, T], F32))
        overlay("conv", cnv_g=([P, 2, T], F32), cnv_x=([P, 2, T], F32), cnv_p=([P, 2, C_TAPS - 1 + T], F32),
                cnv_c=([P, 2, T], F32), cnv_b=([P, 2, T], F32),
                cnv_hi=([P, KT, T], F32R), cnv_lo=([P, KT, T], F32R))
        M = memory

        acc = whole.enter_context(nc.psum_tensor("acc", [P, BANKS, T], F32))
        stat = whole.enter_context(nc.psum_tensor("stat", [P, T], F32))
        side = whole.enter_context(nc.psum_tensor("side", [P, 3, T], F32))

        raw_in = [sem(f"raw_in{s}") for s in range(SLOTS)]
        hi_made = sem("hi_made")
        panel_made = sem("panel_made")
        panel_used = sem("panel_used")
        out_made = sem("out_made")
        out_taken = [sem(f"out_taken{b}") for b in range(BANKS)]
        const_in = sem("const_in")
        x_in = sem("x_in")
        squared = sem("squared")
        h_hi_made = sem("h_hi_made")
        summed = sem("summed")
        h_lo_made = sem("h_lo_made")
        stat_made = sem("stat_made")
        root_made = sem("root_made")
        rstd_made = sem("rstd_made")
        hid_hi_made = sem("hid_hi_made")
        hid_lo_made = sem("hid_lo_made")
        rec_zeroed = sem("rec_zeroed")
        rec_cl_exp = sem("rec_cl_exp")
        rec_cl_ln = sem("rec_cl_ln")
        rec_cl_made = sem("rec_cl_made")
        rec_conv = sem("rec_conv")
        rec_hi_made = sem("rec_hi_made")
        rec_lo_made = sem("rec_lo_made")
        rec_xi_made = sem("rec_xi_made")
        rec_tanh = sem("rec_tanh")
        rec_decay = sem("rec_decay")
        rec_ratio = sem("rec_ratio")
        rec_sqrt = sem("rec_sqrt")
        rec_scan = sem("rec_scan")
        rec_gelu = sem("rec_gelu")
        rec_y = sem("rec_y")
        sgu_in = sem("sgu_in")
        sgu_masked = sem("sgu_masked")
        sgu_col = sem("sgu_col")
        sgu_col_taken = sem("sgu_col_taken")
        sgu_sq_made = sem("sgu_sq_made")
        sgu_root = sem("sgu_root")
        sgu_norm = sem("sgu_norm")
        sgu_v_norm = sem("sgu_v_norm")
        sgu_u_made = sem("sgu_u_made")
        sgu_y_made = sem("sgu_y_made")
        sgu_hi_made = sem("sgu_hi_made")
        sgu_lo_made = sem("sgu_lo_made")
        cnv_zeroed = sem("cnv_zeroed")
        cnv_step = sem("cnv_step")
        cnv_y = sem("cnv_y")
        cnv_hi_made = sem("cnv_hi_made")
        cnv_lo_made = sem("cnv_lo_made")
        scaled = sem("scaled")
        result_out = sem("result_out")

        A_OUTS = 2 * (HALF + 2 * HALF + HALF) + KT
        B_OUTS = 8 + KT + KT + KT
        C_OUTS = 3 * KT + KT
        M_OUTS = FF2 + UG * KT
        first_out = {}
        n = 0
        if not start_x:
            n = FIRST_OUTS
        for layer in range(LAYERS):
            first_out["mix", layer] = n
            n += (A_OUTS, B_OUTS, C_OUTS)[layer % 3]
            first_out["mlp", layer] = n
            n += M_OUTS
        last_norm = n
        CONSTS = 48
        NORM0 = 0 if start_x else FIRST_NORMS
        PE_NORMS = 0 if start_x else 2
        H_SKIP = 0 if start_x else KT

        def bank(o):
            return acc[:, o % BANKS, :]

        def wait_made(eng, o, turn=None):
            eng.wait_ge(out_made, turn.value(o + 1) if turn else o + 1)

        def wait_taken(eng, o, turn=None):
            v = o // BANKS + 1
            eng.wait_ge(out_taken[o % BANKS], turn.value(v, turn.rate // BANKS) if turn else v)

        def mix_down(layer):
            return first_out["mlp", layer] - KT

        def mlp_down(layer):
            return first_out["mlp", layer] + M_OUTS - KT

        def rec_x_lo(inst, k):
            half = k // HALF
            return 2 * RT * inst + k + HALF * half + 1

        def rec_y_lo(inst, k):
            return 2 * RT * inst + k + HALF * (1 + k // HALF) + 1


        with ExitStack() as first:
            def fb(name, shape, dt=F32):
                return first.enter_context(nc.sbuf_tensor(name, shape, dt))

            mod = fb("mod", [P, 6 * KT, 2])
            gain1 = fb("gain1", [P, 2, KT])
            gain2 = fb("gain2", [P, KT])
            products = fb("products", [P, 6 * KT, 2])
            identity = fb("identity", [P, P])
            rope = fb("rope", [P, T])
            main = ExitStack()
            with nc.sbuf_tensor("ada", [P, ADA_SLOTS, D], F32) as ada:
                pass
            og_hi = main.enter_context(nc.sbuf_tensor("og_hi", [P, GH, T], F32R))
            og_lo = main.enter_context(nc.sbuf_tensor("og_lo", [P, GH, T], F32R))
            with ExitStack() as part:
                def fa(name, shape, dt=F32):
                    return part.enter_context(nc.sbuf_tensor(name, shape, dt))

                with ExitStack() as norm_part:
                    xc = norm_part.enter_context(nc.sbuf_tensor("xc", [P, KT, C], F32))
                    with nc.sbuf_tensor("ada_n", [P, 2, D], F32) as ada_n:
                        pass
                    n_full = norm_part.enter_context(nc.sbuf_tensor("n_full", [P, 2, T], F32))
                    n_scaled = norm_part.enter_context(nc.sbuf_tensor("n_scaled", [P, 2, T], F32))
                    cvec = norm_part.enter_context(nc.sbuf_tensor("cvec", [P, 2, D], F32))
                    spare = norm_part.enter_context(nc.sbuf_tensor("spare", [P, D], F32))
                    ada_more = norm_part.enter_context(nc.sbuf_tensor("ada_more", [P, ADA_FIRST - 2 - ADA_SLOTS, D], F32))
                    spare_b = norm_part.enter_context(nc.sbuf_tensor("spare_b", [P, D], F32))
                with nc.sbuf_tensor("low_square", [P, QL * T + KVL * TC], F32) as low_square:
                    pass
                zb = fa("zb", [P, TC])
                ln = fa("ln", [P, TC])
                b_cum = fa("b_cum", [P, TC])
                kd = fa("kd", [P, TC])
                qe = fa("qe", [P, T])
                ke = fa("ke", [P, T])
                kd_tok = fa("kd_tok", [P, KB, P])
                a_t = fa("a_t", [P, 4, P])
                state = fa("state", [P, T // CHUNK, P])
                state_c = fa("state_c", [P, 4, P])
                chunk_decay = fa("chunk_decay", [P, NCH])
                hc_hi = fa("hc_hi", [P, KT, C], F32R)
                hc_lo = fa("hc_lo", [P, KT, C], F32R)
                glow = fa("glow", [64, TC])
                v_tok = fa("v_tok", [P, KB, GH * P])
                gk = fa("gk", [P, 2, TC])
                decay_w = fa("decay_w", [48, GH * P])
                intra_mask = fa("intra_mask", [P, 2, P])
                reset = fa("reset", [P, TC + 1])
                gq = fa("gq", [P, 2, T])
                gr = fa("gr", [P, 2, T])
            with ExitStack() as part:
                om_hi = fa("om_hi", [P, 4, T], F32R)
                om_lo = fa("om_lo", [P, 4, T], F32R)
                with ExitStack() as att:
                    def ft(name, shape, dt=F32):
                        return att.enter_context(nc.sbuf_tensor(name, shape, dt))
                    q_t = ft("q_t", [P, HEADS, T])
                    k_t = ft("k_t", [P, HEADS, TC])
                    v_mla = ft("v_mla", [P, KB, T])
                    with nc.sbuf_tensor("kv_hi", [P, KVL, TC], F32R) as kv_hi:
                        pass
                    prob = ft("prob", [P, 2, TC])
                    att_stat = ft("att_stat", [P, 2, 8])
                with ExitStack() as att:
                    mg_hi = ft("mg_hi", [P, KT, T], F32R)
                    mg_lo = ft("mg_lo", [P, KT, T], F32R)
                    gate_m = ft("gate_m", [P, 2, T])
                    gate_g = ft("gate_g", [P, 2, T])
            main.close()
            with ExitStack() as part:
                f2_full = fa("f2_full", [P, 2, T])
                f2_scaled = fa("f2_scaled", [P, 2, T])
                ff_hi = fa("ff_hi", [P, 2, 8, T], F32R)
                ff_lo = fa("ff_lo", [P, 2, 8, T], F32R)
                ff_pad = fa("ff_pad", [P, 2, GRID_H + 2, GRID_W + 2])
                ff_conv = fa("ff_conv", [P, 2, T])
                ff_hid = fa("ff_hid", [P, 2, T])
        x_flat = x[:, :, :].rearrange("p k t -> p (k t)")
        z_kv = x_flat[:, 0:KVL * TC].rearrange("p (k t) -> p k t", k=KVL)
        z_q = x_flat[:, KVL * TC:KVL * TC + QL * T].rearrange("p (k t) -> p k t", k=QL)
        k_rope = x_flat[64:96, KVL * TC + QL * T:KVL * TC + QL * T + TC]
        p_t = x_flat[:, 0:KB * T].rearrange("p (b q) -> p b q", b=KB)
        o_norm = square_sum
        kv_lo = om_lo[:, :, :].rearrange("p k t -> p (k t)")[:, 0:KVL * TC].rearrange("p (k t) -> p k t", k=KVL)

        ada_slot = [ada[:, s, :] for s in range(ADA_SLOTS)]
        ada_slot += [ada_more[:, s, :] for s in range(ADA_FIRST - 2 - ADA_SLOTS)] + [ada_n[:, s, :] for s in range(2)]
        ada_in = [sem(f"ada_in{s}") for s in range(ADA_FIRST)]
        ada_used = sem("ada_used")
        ctx_in = sem("ctx_in")
        small_in = sem("small_in")
        mix_in = sem("mix_in")
        silu_made = sem("silu_made")
        dve_chain = sem("dve_chain")
        act_chain = sem("act_chain")
        gains_made = sem("gains_made")
        n_scaled_made = sem("n_scaled_made")
        side_made = sem("side_made")
        side_taken = sem("side_taken")
        gla_ln = sem("gla_ln")
        gla_b = sem("gla_b")
        gla_e = sem("gla_e")
        gla_d = sem("gla_d")
        gla_ed = sem("gla_ed")
        gla_qk = sem("gla_qk")
        gla_kd = sem("gla_kd")
        gla_s = sem("gla_s")
        gla_o = sem("gla_o")
        gla_sq = sem("gla_sq")
        gla_y = sem("gla_y")
        og_hi_made = sem("og_hi_made")
        og_lo_made = sem("og_lo_made")
        lr_sq = sem("lr_sq")
        lr_scaled = sem("lr_scaled")
        lr_hi = sem("lr_hi")
        lr_lo = sem("lr_lo")
        q_copied = sem("q_copied")
        k_spread = sem("k_spread")
        att_max = sem("att_max")
        att_prob = sem("att_prob")
        att_turned = sem("att_turned")
        turned_taken = sem("turned_taken")
        att_o = sem("att_o")
        om_hi_made = sem("om_hi_made")
        om_lo_made = sem("om_lo_made")
        mg_made = sem("mg_made")
        mg_hi_made = sem("mg_hi_made")
        mg_lo_made = sem("mg_lo_made")
        pads_made = sem("pads_made")
        ff_conved = sem("ff_conved")
        ff_gelu = sem("ff_gelu")
        ff_hi_made = sem("ff_hi_made")
        ff_lo_made = sem("ff_lo_made")
        x_normed = sem("x_normed")

        def sums(norm):
            return C if norm == 1 else T

        def rev(ap, d, a, b):
            return ap[:, a:b] if d == 0 else ap[:, a:b][:, ::-1]

        def chunk_cols(d, i):
            if i < 4:
                n = 8 + (i if d == 0 else 3 - i)
            else:
                n = i - 4 if d == 0 else 11 - i
            return n

        queries = [qe[:, :], ada[:, ADA_SLOTS - 1, D - T:D]]

        def ada_free(m):
            return ADA_FIRST + 2 + m - ADA_FIRST + 1 if m < ADA_FIRST + ADA_SLOTS else 2 * ADA_FIRST + m - ADA_FIRST - ADA_SLOTS + 1

        def first_block_sp(sp, load_panel):
            def load_ada(m):
                slot = m if m < ADA_FIRST else m % ADA_SLOTS
                if m >= ADA_FIRST:
                    sp.wait_ge(ada_used, ada_free(m))
                sp.dma_start(ada_slot[slot], io["ada"][m]).then_inc(ada_in[slot], 16)

            for m in range(ADA_FIRST):
                load_ada(m)
            sp.dma_start(xc[:, :, :], io["ctx"]).then_inc(ctx_in, 16)
            for n in range(SLOTS):
                load_panel(sp, n, n)
            for n in range(SLOTS, 2 * SLOTS):
                sp.wait_ge(panel_made, n - SLOTS + 1)
                load_panel(sp, n % SLOTS, n)
            for i, m in enumerate(range(ADA_FIRST, 6 * KT)):
                load_ada(m)
                if i % 4 == 3:
                    n = 2 * SLOTS + i // 4
                    sp.wait_ge(panel_made, n - SLOTS + 1)
                    load_panel(sp, n % SLOTS, n)

        def first_block_pe(pe, turn, next_tile, mm, begin_out, project, looped, tile, norm_sum, skip_to_panel):
            def both(parts_a, parts_b, wa, wb, ready=None):
                a, b = begin_out(), begin_out()
                n = len(parts_a)
                for k in range(n):
                    slot, cols = next_tile()
                    if ready:
                        ready(k)
                    (ah, al), (bh, bl) = parts_a[k], parts_b[k]
                    mm(a[:, 0:wa], w_hi[:, slot, cols], ah, k == 0, False)
                    mm(a[:, 0:wa], w_hi[:, slot, cols], al, False, False)
                    mm(b[:, 0:wb], w_hi[:, slot, cols], bh, k == 0, False)
                    mm(b[:, 0:wb], w_hi[:, slot, cols], bl, False, False)
                    ia = mm(a[:, 0:wa], w_lo[:, slot, cols], ah, False, k == n - 1)
                    if k == n - 1:
                        ia.then_inc(out_made, 1)
                    ib = mm(b[:, 0:wb], w_lo[:, slot, cols], bh, False, k == n - 1)
                ib.then_inc(out_made, 1)

            h_parts = [(h_hi[:, k, :], h_lo[:, k, :]) for k in range(KT)]
            hc_parts = [(hc_hi[:, k, :], hc_lo[:, k, :]) for k in range(KT)]
            for norm in range(2):
                w = sums(norm)
                for k in range(KT):
                    pe.wait_ge(squared, KT * norm + k + 1)
                    if norm and k == 0:
                        pe.wait_ge(root_made, 1)
                    pe.matmul(stat[:, 0:w], ones[:, :], square[:, k % 2, 0:w], start=(k == 0), stop=(k == KT - 1))\
                      .then_inc(summed, 1)
            for m in range(QL + len(AHEAD)):
                project(h_parts, (lambda k: pe.wait_ge(h_lo_made, k + 1)) if m == 0 else None)
            pe.wait_ge(h_lo_made, 2 * KT)
            both(h_parts, hc_parts, T, C)
            for m in range(KVL):
                both(h_parts, hc_parts, T, C)
            outs = [begin_out() for _ in range(4)] + [side[:, 1, :], side[:, 2, :]]
            for k in range(KT):
                if k % 2 == 0:
                    slot, _ = next_tile()
                    tile[0] += TP - 1
                cols = slice(T * (k % 2), T * (k % 2) + T)
                for tb in range(KB):
                    hi, lo = (h_hi, h_lo) if tb < 4 else (hc_hi, hc_lo)
                    tok = slice(P * (tb % 4), P * (tb % 4) + P)
                    mm(outs[tb], hi[:, k, tok], w_hi[:, slot, cols], k == 0, False)
                    mm(outs[tb], hi[:, k, tok], w_lo[:, slot, cols], False, False)
                    ins = mm(outs[tb], lo[:, k, tok], w_hi[:, slot, cols], False, k == KT - 1)
                    if k == KT - 1 and tb < 4:
                        ins.then_inc(out_made, 1)
            ins.then_inc(side_made, 1)
            assert turn.out == OUT_QNORM
            pe.wait_ge(lr_sq, 1)
            out = begin_out()
            for k in range(QL):
                ins = pe.matmul(out[:, :], ones[:, :], low_square[:, T * k:T * k + T], start=(k == 0), stop=(k == QL - 1))
            ins.then_inc(out_made, 1)
            for c0, c1 in ((0, T), (T, TC)):
                out = begin_out()
                for k in range(KVL):
                    at = QL * T + TC * k
                    ins = pe.matmul(out[:, 0:c1 - c0], ones[:, :], low_square[:, at + c0:at + c1], start=(k == 0),
                                    stop=(k == KVL - 1))
                ins.then_inc(out_made, 1)

            def gla_part(name, i):
                assert turn.out == OUT_GLA[name, i]
                if name == "k":
                    both(h_parts, hc_parts, T, C)
                if name in ("q", "r"):
                    project(h_parts)
                if name == "gate":
                    h, d = i // 2, i % 2
                    rows = slice(32 * d, 32 * d + 16)
                    if i == 0:
                        wait_taken(pe, OUT_MISC + 1)
                        pe.wait_ge(mix_in, 64)
                    for c0, c1 in ((0, T), (T, TC)):
                        out = begin_out()
                        pe.matmul(out[:, 0:c1 - c0], decay_w[rows, P * h:P * h + P], glow[rows, c0:c1], start=True,
                                  stop=True).then_inc(out_made, 1)
                if name == "turned":
                    pe.wait_ge(gla_kd, i + 1)
                    if i == 0:
                        pe.wait_ge(small_in, 32)
                    for b0, b1 in ((0, 4), (4, KB)):
                        out = begin_out()
                        for b in range(b0, b1):
                            ins = pe.transpose(out[:, P * (b - b0):P * (b - b0) + P], kd[:, P * b:P * b + P], identity[:, :])
                        ins.then_inc(out_made, 1)
                if name == "intra":
                    pe.wait_ge(gla_qk, i + 1)
                    out = begin_out()
                    for b in range(4):
                        ins = pe.matmul(out[:, P * b:P * b + P], ke[:, P * b:P * b + P], queries[i % 2][:, P * b:P * b + P],
                                        start=True, stop=True)
                    ins.then_inc(out_made, 1)
                if name == "added":
                    h, d = i // 2, i % 2
                    wait_taken(pe, OUT_GLA["turned", i])
                    wait_taken(pe, OUT_GLA["turned", i] + 1)
                    if i == 0:
                        wait_taken(pe, OUT_GV + 3)
                        pe.wait_ge(side_taken, 2)
                    for i0 in (0, 8):
                        pair = [begin_out(), begin_out()]
                        for i in range(i0, min(i0 + 8, NCH - 1)):
                            n = chunk_cols(d, i)
                            r = slice(CHUNK * (n % 2), CHUNK * (n % 2) + CHUNK)
                            j = (i - i0) // 2
                            ins = pe.matmul(pair[i % 2][:, P * j:P * j + P], kd_tok[r, n // 2, :],
                                            v_tok[r, n // 2, P * h:P * h + P], start=True, stop=True)
                            if i + 2 >= min(i0 + 8, NCH - 1):
                                ins.then_inc(out_made, 1)
                if name == "sum":
                    pe.wait_ge(gla_sq, i + 1)
                    out = begin_out()
                    pe.matmul(out[:, :], ones[:, :], square[:, i % 2, :], start=True, stop=True).then_inc(out_made, 1)

            def gla_output(u):
                h, d = u // 2, u % 2
                o = side[:, h % 2, :]
                wait_taken(pe, OUT_GLA["intra", u])
                if d == 0 and h >= 1:
                    pe.wait_ge(side_taken, 2)
                    if h >= 2:
                        pe.wait_ge(gla_y, h - 1)
                for b in range(4):
                    pe.matmul(o[:, P * b:P * b + P], v_tok[:, b, P * h:P * h + P], a_t[:, b, :], start=(d == 0 and b == 0),
                              stop=False, skip_group_check=True)
                pe.wait_ge(gla_s, u + 1)
                for i in range(T // CHUNK):
                    n = chunk_cols(d, i + 4)
                    cs = slice(CHUNK * n, CHUNK * n + CHUNK)
                    ins = pe.matmul(o[:, cs], state[:, i, :], queries[u % 2][:, cs], start=False,
                                    stop=(d == 1 and i == T // CHUNK - 1), skip_group_check=True)
                ins.then_inc(gla_o, 1)

            for part in ("gate", "k"):
                gla_part(part, 0)
            for u in range(GLA_STEPS):
                h, d = u // 2, u % 2
                gla_part("turned", u)
                if u + 1 < GLA_STEPS:
                    gla_part("gate", u + 1)
                gla_part("intra", u)
                gla_part("added", u)
                if h + 1 < GH:
                    gla_part("q" if d == 0 else "k", h + 1)
                gla_output(u)
                if d == 0 and h + 1 < GH and ("r", h + 1) not in AHEAD:
                    gla_part("r", h + 1)
                if d == 1 and h + 1 < GH:
                    gla_part("sum", h)

            assert turn.out == OUT_QH
            om = [t[:, :, :].rearrange("p k t -> p (k t)") for t in (om_hi, om_lo)]
            for h in range(HEADS):
                project([(om[0][:, T * k:T * k + T], om[1][:, T * k:T * k + T]) for k in range(QL)],
                        (lambda k: pe.wait_ge(lr_lo, k + 1)) if h == 0 else None)
            gla_part("sum", GH - 1)
            for pair in range(HEADS // 2):
                both([(kv_hi[:, k, 0:T], kv_lo[:, k, 0:T]) for k in range(KVL)],
                     [(kv_hi[:, k, T:TC], kv_lo[:, k, T:TC]) for k in range(KVL)], T, C,
                     (lambda k: pe.wait_ge(lr_lo, QL + k + 1)) if pair == 0 else None)
            slot, _ = next_tile()
            tile[0] += TP - 1
            for tb in range(KB):
                out = begin_out()
                for k in range(KVL):
                    tok = slice(P * tb, P * tb + P)
                    cols = slice(T * k, T * k + T)
                    mm(out, kv_hi[:, k, tok], w_hi[:, slot, cols], k == 0, False)
                    mm(out, kv_hi[:, k, tok], w_lo[:, slot, cols], False, False)
                    ins = mm(out, kv_lo[:, k, tok], w_hi[:, slot, cols], False, k == KVL - 1)
                ins.then_inc(out_made, 1)

            def scores(u):
                assert turn.out == out_scores(u)
                h, qb = u // 4, u % 4
                for c0, c1 in ((0, T), (T, TC)):
                    out = begin_out()
                    pe.matmul(out[:, 0:c1 - c0], q_t[0:QK, h, P * qb:P * qb + P], k_t[0:QK, h, c0:c1],
                              start=True, stop=True).then_inc(out_made, 1)

            def turn_probs(u):
                pe.wait_ge(att_prob, u + 1)
                if u:
                    pe.wait_ge(turned_taken, u)
                for b in range(KB):
                    out = side[:, 2, P * b:P * b + P] if b < 4 else stat[:, P * (b - 4):P * (b - 4) + P]
                    ins = pe.transpose(out, prob[:, u % 2, P * b:P * b + P], identity[:, :])
                ins.then_inc(att_turned, 1)

            def head_values(h):
                pe.wait_ge(turned_taken, 4 * h + 4)
                if h == 0:
                    wait_taken(pe, OUT_V + KB - 1)
                    pe.wait_ge(gla_y, GH)
                if h >= 2:
                    pe.wait_ge(om_lo_made, h - 1)
                rows = slice(64 * (h % 2), 64 * (h % 2) + 64)
                for b in range(KB):
                    ins = pe.matmul(side[rows, h % 2, :], v_mla[:, b, 64 * h:64 * h + 64], p_t[:, b, :],
                                    start=(b == 0), stop=(b == KB - 1))
                ins.then_inc(att_o, 1)

            assert turn.out == OUT_ATT
            wait_taken(pe, OUT_KH - 1)
            pe.wait_ge(k_spread, 1)
            wait_taken(pe, OUT_V - 1)
            scores(0)
            scores(1)
            for u in range(UNITS):
                if u + 2 < UNITS:
                    scores(u + 2)
                if u % 4 == 0 and u:
                    head_values(u // 4 - 1)
                if u == UNITS - 1:
                    project(h_parts)
                turn_probs(u)
            project(h_parts)
            head_values(HEADS - 1)

            assert turn.out == OUT_MERGE + 2
            for m in range(KT):
                if m:
                    project(h_parts)
                    project(h_parts)
                project([(om_hi[:, k, :], om_lo[:, k, :]) for k in range(4)],
                        (lambda k: pe.wait_ge(om_lo_made, 2 * k + 2)) if m == 0 else None)
                project([(og_hi[:, k, :], og_lo[:, k, :]) for k in range(4)],
                        (lambda k: pe.wait_ge(og_lo_made, k + 1)) if m == 0 else None)
            for m in range(KT):
                project([(mg_hi[:, k, :], mg_lo[:, k, :]) for k in range(KT)],
                        (lambda k: pe.wait_ge(mg_lo_made, k + 1)) if m == 0 else None)

            norm_sum(2)
            def up(group):
                outs = 2 * len(FF1_GROUPS[group])
                if group == 0:
                    for i in range(BANKS):
                        project(h_parts, (lambda k: pe.wait_ge(h_lo_made, 2 * KT + k + 1)) if i == 0 else None)
                    outs -= BANKS
                looped(h_parts, outs // BANKS)

            def down(group):
                n = len(FF1_GROUPS[group])
                parts = [(ff_hi[:, group % 2, k, :], ff_lo[:, group % 2, k, :]) for k in range(n)]
                if n == TP:
                    pe.wait_ge(ff_lo_made, FF1_GROUPS[group][-1] + 1)
                    looped(parts)
                    return
                for m in range(KT):
                    project(parts, (lambda k: pe.wait_ge(ff_lo_made, FF1_GROUPS[group][k] + 1)) if m == 0 else None)

            up(0)
            up(1)
            down(0)
            up(2)
            down(1)
            down(2)
            norm_sum(3)
            assert turn.out == FIRST_OUTS and tile[0] % TP == 0

        def first_block_act(act, feed):
            steps = [0]

            def link(ins):
                steps[0] += 1
                ins.then_inc(act_chain, 1)
                act.wait_ge(act_chain, steps[0])

            act.dma_start(cvec[:, :, :], io["cvec"]).then_inc(small_in, 16)
            for k in range(KT):
                act.dma_start(x[:, k, :], io["x"][:, k, :]).then_inc(x_in, 16)
            act.wait_ge(small_in, 16)
            act.activation(cvec[:, :, :], cvec[:, :, :], ACT.Silu).then_inc(silu_made, 1)
            act.dma_start(identity[:, :], io["identity"]).then_inc(small_in, 16)
            act.dma_start(rope[:, :], io["rope"]).then_inc(mix_in, 16)
            act.wait_ge(const_in, CONSTS)
            act.wait_ge(x_in, 16 * KT)

            def sq(k, norm, src):
                if KT * norm + k >= 2:
                    act.wait_ge(summed, KT * norm + k - 1)
                w = sums(norm)
                act.activation(square[:, k % 2, 0:w], src[:, k, 0:w], ACT.Square).then_inc(squared, 1)

            def root_of(norm):
                if norm < 2:
                    act.wait_ge(summed, KT * (norm + 1))
                else:
                    act.wait_ge(stat_made, norm + 1 - PE_NORMS)
                if norm:
                    act.wait_ge(rstd_made, norm)
                w = sums(norm)
                act.activation(root[:, 0:w], stat[:, 0:w], ACT.Sqrt, bias=col("eps"), scale=1.0 / D).then_inc(root_made, 1)

            def modulated(norm, n0, hi, scaled_, full, gain, shift):
                w = sums(norm)
                for k in range(KT):
                    act.wait_ge(n_scaled_made, n0 + k + 1)
                    if n0 + k >= 2:
                        act.wait_ge(h_lo_made, n0 + k - 1)
                    act.activation(full[:, k % 2, 0:w], scaled_[:, k % 2, 0:w], ACT.Identity, bias=shift(k), scale=gain(k))
                    act.activation(hi[:, k, :], scaled_[:, k % 2, 0:w], ACT.Identity, bias=shift(k),
                                   scale=gain(k)).then_inc(h_hi_made, 1)

            for k in range(KT):
                sq(k, 0, x)
            root_of(0)
            act.wait_ge(ctx_in, 16)
            for k in range(KT):
                sq(k, 1, xc)
            act.wait_ge(gains_made, 1)
            modulated(0, 0, h_hi, n_scaled, n_full, lambda k: gain1[:, 0, k:k + 1], lambda k: mod[:, k, 0:1])
            def take(o, out, func=ACT.Copy, width=T, **kw):
                wait_made(act, o)
                act.activation(out, bank(o)[:, 0:width], func, **kw).then_inc(out_taken[o % BANKS], 1)

            def gla_take(name, h):
                o = OUT_GLA[name, h]
                if name == "k":
                    if h >= 2:
                        act.wait_ge(gla_kd, 2 * h - 2)
                        act.wait_ge(gla_qk, 2 * h - 2)
                    take(o, gk[:, h % 2, 0:T])
                    take(o + 1, gk[:, h % 2, T:TC], width=C)
                if name == "q":
                    if h >= 2:
                        act.wait_ge(gla_qk, 2 * h - 2)
                    take(o, gq[:, h % 2, :], scale=GLA_SCALE)
                if name == "r":
                    if h >= 2:
                        act.wait_ge(gla_y, h - 1)
                    take(o, gr[:, h % 2, :], func=ACT.Silu)

            root_of(1)
            for m in range(QL):
                take(OUT_Q + m, z_q[:, m, :])
            act.wait_ge(gains_made, 2)
            modulated(1, KT, hc_hi, n_scaled, n_full, lambda k: gain1[:, 1, k:k + 1], lambda k: mod[:, k, 1:2])
            for name, h in AHEAD:
                gla_take(name, h)
            act.dma_start(decay_w[:, :], io["decay_w"]).then_inc(mix_in, 16)
            act.dma_start(intra_mask[:, :, :], io["intra_mask"]).then_inc(mix_in, 16)
            act.dma_start(reset[:, :], io["reset"]).then_inc(mix_in, 16)
            act.wait_ge(h_lo_made, 2 * KT)
            for m in range(KVL):
                take(OUT_KV + 2 * m, z_kv[:, m, 0:T])
                take(OUT_KV + 2 * m + 1, z_kv[:, m, T:TC], width=C)
            for o in [*range(OUT_Q, OUT_AHEAD), *range(OUT_KV, OUT_GV)]:
                wait_taken(act, o)
            for k in range(QL):
                act.activation(low_square[:, T * k:T * k + T], z_q[:, k, :], ACT.Square)
            for k in range(KVL):
                at = QL * T + TC * k
                ins = act.activation(low_square[:, at:at + TC], z_kv[:, k, :], ACT.Square)
            ins.then_inc(lr_sq, 1)
            for tb in range(4):
                take(OUT_GV + tb, v_tok[:, tb, :])
            take(OUT_QNORM, square_sum[:, :], func=ACT.Sqrt, bias=col("eps"), scale=1.0 / (QL * P))
            take(OUT_KVNORM, square[:, 0, :], func=ACT.Sqrt, bias=col("eps"), scale=1.0 / (KVL * P))
            take(OUT_KVNORM + 1, square[:, 1, 0:C], func=ACT.Sqrt, bias=col("eps"), scale=1.0 / (KVL * P), width=C)

            def log_gates(u):
                wait_taken(act, OUT_GLA["gate", u] + 1)
                if u:
                    act.wait_ge(gla_b, u)
                link(act.activation(ln[:, :], zb[:, :], ACT.Abs))
                link(act.activation(ln[:, :], ln[:, :], ACT.Exp, scale=-1.0))
                act.activation(ln[:, :], ln[:, :], ACT.Ln, bias=col("one")).then_inc(gla_ln, 1)

            def key_decays(u):
                act.wait_ge(gla_d, u + 1)
                act.activation(kd[:, :], kd[:, :], ACT.Exp, scale=1.0 / GATE_NORM).then_inc(gla_ed, 1)

            om = om_hi[:, :, :].rearrange("p k t -> p (k t)")
            log_gates(0)
            gla_take("k", 0)
            key_decays(0)
            def sum_decays(u):
                last = slice(CHUNK - 1, TC, CHUNK) if u % 2 == 0 else slice(0, TC, CHUNK)
                act.wait_ge(gla_b, u + 1)
                if u:
                    act.wait_ge(gla_s, u)
                act.activation(chunk_decay[:, :], b_cum[:, last], ACT.Exp, scale=1.0 / GATE_NORM)
                if u >= 2:
                    act.wait_ge(gla_o, u - 1)
                act.activation(queries[u % 2], b_cum[:, 0:T], ACT.Exp, scale=1.0 / GATE_NORM)
                if u:
                    wait_made(act, OUT_GLA["intra", u - 1])
                act.activation(ke[:, :], b_cum[:, 0:T], ACT.Exp, scale=-1.0 / GATE_NORM).then_inc(gla_e, 1)

            sum_decays(0)
            for u in range(GLA_STEPS):
                h, d = u // 2, u % 2
                o = OUT_GLA["turned", u]
                take(o, kd_tok[:, 0:4, :].rearrange("p b d -> p (b d)"))
                take(o + 1, kd_tok[:, 4:KB, :].rearrange("p b d -> p (b d)"), width=2 * P)
                if u + 1 < GLA_STEPS:
                    log_gates(u + 1)
                    key_decays(u + 1)
                    sum_decays(u + 1)
                else:
                    act.wait_ge(lr_scaled, 2)
                    for k in range(QL):
                        act.activation(om[:, T * k:T * k + T], z_q[:, k, :], ACT.Copy).then_inc(lr_hi, 1)
                if h + 1 < GH:
                    gla_take("q" if d == 0 else "k", h + 1)
                if d == 0 and 0 < h < GH - 1:
                    act.wait_ge(gla_y, h)
                    act.activation(og_hi[:, h - 1, :], o_norm[:, :], ACT.Copy).then_inc(og_hi_made, 1)
                if d == 0 and h + 1 < GH and ("r", h + 1) not in AHEAD:
                    gla_take("r", h + 1)
                if d == 1:
                    act.wait_ge(gla_o, 2 * h + 2)
                    act.activation(square[:, h % 2, :], side[:, h % 2, :], ACT.Square).then_inc(gla_sq, 1)
                    if h:
                        act.wait_ge(gla_y, h)
                    if h == GH - 1:
                        act.activation(og_hi[:, h - 1, :], o_norm[:, :], ACT.Copy).then_inc(og_hi_made, 1)
                    else:
                        take(OUT_GLA["sum", h], root[:, :], func=ACT.Sqrt, bias=col("eps"), scale=1.0 / P)
            for k in range(KVL):
                act.activation(kv_hi[:, k, :], z_kv[:, k, :], ACT.Copy).then_inc(lr_hi, 1)
            for h in range(HEADS):
                wait_made(act, OUT_QH + h)
                act.activation(q_t[0:64, h, :], bank(OUT_QH + h)[0:64, :], ACT.Copy).then_inc(q_copied, 1)
            take(OUT_GLA["sum", GH - 1], root[:, :], func=ACT.Sqrt, bias=col("eps"), scale=1.0 / P)
            for pair in range(HEADS // 2):
                for o, c0, c1 in ((OUT_KH + 2 * pair, 0, T), (OUT_KH + 2 * pair + 1, T, TC)):
                    wait_made(act, o)
                    act.activation(k_t[0:64, 2 * pair, c0:c1], bank(o)[0:64, 0:c1 - c0], ACT.Copy)
                    act.activation(k_t[0:64, 2 * pair + 1, c0:c1], bank(o)[64:P, 0:c1 - c0], ACT.Copy)\
                       .then_inc(out_taken[o % BANKS], 1)
            for tb in range(KB):
                take(OUT_V + tb, v_mla[:, tb, :])
            act.wait_ge(gla_y, GH)
            act.activation(og_hi[:, GH - 1, :], o_norm[:, :], ACT.Copy).then_inc(og_hi_made, 1)

            def exps(u):
                o = out_scores(u)
                act.wait_ge(att_max, u + 1)
                if u >= 2:
                    act.wait_ge(att_turned, u - 1)
                for i, (c0, c1) in enumerate(((0, T), (T, TC))):
                    act.activation(prob[:, u % 2, c0:c1], bank(o + i)[:, 0:c1 - c0], ACT.Exp, scale=MLA_SCALE,
                                   bias=att_stat[:, u % 2, 1:2], accum_out=att_stat[:, u % 2, 2 + i:3 + i])\
                       .then_inc(out_taken[(o + i) % BANKS], 1)

            def head_high(h):
                rows = slice(64 * (h % 2), 64 * (h % 2) + 64)
                act.wait_ge(att_o, h + 1)
                act.activation(om_hi[rows, h // 2, :], side[rows, h % 2, :], ACT.Copy).then_inc(om_hi_made, 1)

            exps(0)
            for u in range(UNITS):
                if u + 1 < UNITS:
                    exps(u + 1)
                h, qb = u // 4, u % 4
                if qb == 0 and h:
                    head_high(h - 1)
                act.wait_ge(att_turned, u + 1)
                act.activation(p_t[:, 0:4, P * qb:P * qb + P], side[:, 2, :].rearrange("p (b q) -> p b q", b=4),
                               ACT.Copy)
                act.activation(p_t[:, 4:KB, P * qb:P * qb + P], stat[:, 0:2 * P].rearrange("p (b q) -> p b q", b=2),
                               ACT.Copy).then_inc(turned_taken, 1)
            head_high(HEADS - 1)
            for k in range(KT):
                act.dma_start(x[:, k, :], io["x"][:, k, :]).then_inc(x_in, 16)
            for m in range(KT):
                o = OUT_MERGE + 4 * m
                if m >= 2:
                    act.wait_ge(mg_lo_made, m - 1)
                take(o, gate_m[:, m % 2, :], func=ACT.Sigmoid)
                take(o + 1, gate_g[:, m % 2, :], func=ACT.Sigmoid)
                act.wait_ge(mg_made, m + 1)
                act.activation(mg_hi[:, m, :], gate_m[:, m % 2, :], ACT.Copy).then_inc(mg_hi_made, 1)
            for k in range(KT):
                wait_taken(act, OUT_MIX + k)
                sq(k, 2, x)
            root_of(2)
            modulated(2, 2 * KT, h_hi, f2_scaled, f2_full, lambda k: gain2[:, k:k + 1], lambda k: mod[:, 3 * KT + k, 0:1])

            def up(group):
                for i, j in enumerate(FF1_GROUPS[group]):
                    o = out_ff_up(group) + 2 * i
                    wait_made(act, o)
                    if j >= 2:
                        act.wait_ge(ff_conved, j - 1)
                    else:
                        act.wait_ge(pads_made, 1)
                    act.activation(ff_pad[:, j % 2, 1:GRID_H + 1, 1:GRID_W + 1],
                                   bank(o).rearrange("p (r c) -> p r c", r=GRID_H), ACT.Copy).then_inc(out_taken[o % BANKS], 1)
                    act.wait_ge(ff_conved, j + 1)
                    act.activation(ff_conv[:, j % 2, :], ff_conv[:, j % 2, :], ACT.Gelu).then_inc(ff_gelu, 1)
                    wait_taken(act, o + 1)
                    act.activation(ff_hi[:, group % 2, i, :], ff_hid[:, j % 2, :], ACT.Copy).then_inc(ff_hi_made, 1)
            for g in range(3):
                up(g)
            o = out_ff_down(2)
            for k in range(KT):
                wait_taken(act, o + k)
                sq(k, 3, x)
            root_of(3)
            for k in range(KT):
                feed(k, NORM0, ("norm_mix", 0), lambda k: act.wait_ge(x_normed, k + 1), o)

        last_of = [slice(CHUNK - 1, CHUNK), slice(0, 1)]

        def first_block_dve(dve, feed, feed_low):
            steps = [0]

            def link(ins):
                steps[0] += 1
                ins.then_inc(dve_chain, 1)
                dve.wait_ge(dve_chain, steps[0])

            def take(ins, o):
                ins.then_inc(out_taken[o % BANKS], 1)
                wait_taken(dve, o)

            def own(ins, s, count):
                ins.then_inc(s, 1)
                dve.wait_ge(s, count)

            def add_up(k, norm):
                w = sums(norm)
                dve.wait_ge(squared, KT * norm + k + 1)
                if k == 0:
                    if norm > PE_NORMS:
                        dve.wait_ge(stat_made, norm - PE_NORMS)
                    dve.tensor_copy(square_sum[:, 0:w], square[:, 0, 0:w]).then_inc(summed, 1)
                else:
                    dve.wait_ge(summed, KT * norm + k)
                    dve.tensor_tensor(square_sum[:, 0:w], square_sum[:, 0:w], square[:, k % 2, 0:w], ALU.add)\
                       .then_inc(summed, 1)

            def rstd_of(norm):
                w = sums(norm)
                dve.wait_ge(root_made, norm + 1)
                own(dve.reciprocal(rstd[:, 0:w], root[:, 0:w]), rstd_made, norm + 1)

            def modulated(norm, n0, src, hi, lo, scaled_, full):
                w = sums(norm)
                for k in range(KT + 1):
                    if k < KT:
                        dve.tensor_tensor(scaled_[:, k % 2, 0:w], src[:, k, 0:w], rstd[:, 0:w], ALU.mult)\
                           .then_inc(n_scaled_made, 1)
                    if k:
                        dve.wait_ge(h_hi_made, n0 + k)
                        dve.tensor_tensor(lo[:, k - 1, :], full[:, (k - 1) % 2, 0:w], hi[:, k - 1, :].bitcast(F32),
                                          ALU.subtract).then_inc(h_lo_made, 1)

            made = [0]

            def ada_product(m, s):
                slot = m if m < ADA_FIRST else m % ADA_SLOTS
                if s == 0:
                    dve.wait_ge(ada_in[slot], 16 if m < ADA_FIRST else 16 * ((m - ADA_FIRST) // ADA_SLOTS + 2))
                out = ada_slot[slot]
                if s == 0 and m < ADA_FIRST:
                    out = (spare, spare_b)[m % 2][:, :]
                    if m >= 2:
                        dve.wait_ge(ada_used, m - 1)
                if s == 1:
                    dve.wait_ge(ada_used, m + 1)
                made[0] += 1
                dve.scalar_tensor_tensor(out=out, in0=ada_slot[slot], scalar=1.0, in1=cvec[:, s, :], op0=ALU.mult,
                                         op1=ALU.mult, accum_out=products[:, m, s:s + 1]).then_inc(ada_used, 1)

            def gains(s):
                dve.wait_ge(ada_used, made[0])
                link(dve.tensor_tensor(mod[:, 0:ADA_FIRST, s], products[:, 0:ADA_FIRST, s],
                                       table[:, names["b_ada"]:names["b_ada"] + ADA_FIRST], ALU.add))
                own(dve.scalar_tensor_tensor(out=gain1[:, s, :], in0=mod[:, KT:2 * KT, s], scalar=1.0,
                                             in1=table[:, names["norm1"]:names["norm1"] + KT],
                                             op0=ALU.add, op1=ALU.mult), gains_made, s + 1)

            dve.wait_ge(silu_made, 1)
            for m in range(ADA_FIRST):
                ada_product(m, 0)
            for m in range(ADA_FIRST - 2, ADA_FIRST):
                ada_product(m, 1)
            gains(0)
            rstd_of(0)
            modulated(0, 0, x, h_hi, h_lo, n_scaled, n_full)
            for m in range(ADA_FIRST - 2):
                ada_product(m, 1)
            gains(1)
            rstd_of(1)
            modulated(1, KT, xc, hc_hi, hc_lo, n_scaled, n_full)
            dve.wait_ge(h_lo_made, 2 * KT)

            for m in range(ADA_FIRST, ADA_FIRST + KT):
                ada_product(m, 0)
            dve.wait_ge(mix_in, 64)
            wait_made(dve, OUT_MISC)
            lat, con = bank(OUT_MISC), bank(OUT_MISC + 1)
            link(dve.tensor_copy(glow[:, 0:T], lat[0:64, :]))
            link(dve.tensor_tensor(square[64:96, 1, :], lat[96:P, :], rope[96:P, :], ALU.mult))
            take(dve.tensor_tensor(k_rope[:, 0:T], lat[64:96, :], rope[64:96, :], ALU.mult), OUT_MISC)
            link(dve.tensor_tensor(k_rope[:, 0:T], k_rope[:, 0:T], square[64:96, 1, :], ALU.add))
            wait_made(dve, OUT_MISC + 1)
            link(dve.tensor_copy(k_rope[:, T:TC], con[64:96, 0:C]))
            own(dve.tensor_copy(glow[:, T:TC], con[0:64, 0:C]), out_taken[(OUT_MISC + 1) % BANKS], 1)
            for m in range(ADA_FIRST + KT, 6 * KT):
                ada_product(m, 0)
            dve.wait_ge(ada_used, made[0])
            link(dve.tensor_tensor(mod[:, ADA_FIRST:, 0], products[:, ADA_FIRST:, 0],
                                   table[:, names["b_ada"] + ADA_FIRST:names["b_ada"] + 6 * KT], ALU.add))
            own(dve.scalar_tensor_tensor(out=gain2[:, :], in0=mod[:, 4 * KT:5 * KT, 0], scalar=1.0,
                                         in1=table[:, names["norm2"]:names["norm2"] + KT], op0=ALU.add, op1=ALU.mult),
                gains_made, 3)
            dve.wait_ge(side_made, 1)
            dve.tensor_copy(v_tok[:, 4, :], side[:, 1, :]).then_inc(side_taken, 1)
            dve.tensor_copy(v_tok[:, 5, :], side[:, 2, :]).then_inc(side_taken, 1)
            dve.wait_ge(side_taken, 2)
            def low_rank_keys():
                wait_taken(dve, OUT_KVNORM)
                wait_taken(dve, OUT_KVNORM + 1)
                link(dve.reciprocal(square[:, 0, :], square[:, 0, :]))
                link(dve.reciprocal(square[:, 1, 0:C], square[:, 1, 0:C]))
                for k in range(KVL):
                    dve.scalar_tensor_tensor(out=z_kv[:, k, 0:T], in0=z_kv[:, k, 0:T], scalar=col("kv_norm", k),
                                             in1=square[:, 0, :], op0=ALU.mult, op1=ALU.mult)
                    ins = dve.scalar_tensor_tensor(out=z_kv[:, k, T:TC], in0=z_kv[:, k, T:TC], scalar=col("kv_norm", k),
                                                   in1=square[:, 1, 0:C], op0=ALU.mult, op1=ALU.mult)
                own(ins, lr_scaled, 1)

            def low_rank_queries():
                wait_taken(dve, OUT_QNORM)
                link(dve.reciprocal(rstd[:, :], square_sum[:, :]))
                for k in range(QL):
                    ins = dve.scalar_tensor_tensor(out=z_q[:, k, :], in0=z_q[:, k, :], scalar=col("q_norm", k),
                                                   in1=rstd[:, :], op0=ALU.mult, op1=ALU.mult)
                own(ins, lr_scaled, 2)

            def shifted_gates(u):
                h, d = u // 2, u % 2
                bias, o = col("b_decay", GH * d + h), OUT_GLA["gate", u]
                wait_made(dve, o)
                take(dve.tensor_scalar(zb[:, 0:T], bank(o), bias, None, ALU.add), o)
                wait_made(dve, o + 1)
                take(dve.tensor_scalar(zb[:, T:TC], bank(o + 1)[:, 0:C], bias, None, ALU.add), o + 1)

            def decays(u):
                h, d = u // 2, u % 2
                dve.wait_ge(gla_ln, u + 1)
                if u:
                    dve.wait_ge(gla_e, u)
                link(dve.scalar_tensor_tensor(out=zb[:, :], in0=zb[:, :], scalar=0.0, in1=ln[:, :], op0=ALU.min,
                                              op1=ALU.subtract))
                own(dve.tensor_tensor_scan(rev(b_cum, d, 0, TC), rev(reset, d, d, TC + d), rev(zb, d, 0, TC), 0.0,
                                           ALU.mult, ALU.add), gla_b, u + 1)
                chunks = lambda t: t.rearrange("p (n c) -> p n c", c=CHUNK)
                own(dve.tensor_tensor(chunks(kd[:, :]), chunks(b_cum[:, :])[:, :, last_of[d]].to_broadcast([P, NCH, CHUNK]),
                                      chunks(b_cum[:, :]), ALU.subtract), gla_d, u + 1)

            def decayed_keys(u):
                h = u // 2
                wait_taken(dve, OUT_GLA["k", h])
                wait_taken(dve, OUT_GLA["k", h] + 1)
                dve.wait_ge(gla_ed, u + 1)
                own(dve.tensor_tensor(kd[:, :], kd[:, :], gk[:, h % 2, :], ALU.mult), gla_kd, u + 1)

            def head_output(h):
                wait_taken(dve, OUT_GLA["sum", h])
                link(dve.reciprocal(rstd[:, :], root[:, :]))
                dve.wait_ge(gla_o, 2 * h + 2)
                link(dve.scalar_tensor_tensor(out=o_norm[:, :], in0=side[:, h % 2, :], scalar=col("gla_norm"),
                                              in1=rstd[:, :], op0=ALU.mult, op1=ALU.mult))
                own(dve.tensor_tensor(o_norm[:, :], o_norm[:, :], gr[:, h % 2, :], ALU.mult), gla_y, h + 1)

            def head_output_low(h):
                dve.wait_ge(og_hi_made, h + 1)
                own(dve.tensor_tensor(og_lo[:, h, :], o_norm[:, :], og_hi[:, h, :].bitcast(F32), ALU.subtract),
                    og_lo_made, h + 1)

            shifted_gates(0)
            decays(0)
            decayed_keys(0)
            for u in range(GLA_STEPS):
                h, d = u // 2, u % 2
                dve.wait_ge(gla_e, u + 1)
                wait_taken(dve, OUT_GLA["q", h])
                link(dve.tensor_tensor(queries[u % 2], queries[u % 2], gq[:, h % 2, :], ALU.mult))
                own(dve.tensor_tensor(ke[:, :], ke[:, :], gk[:, h % 2, 0:T], ALU.mult), gla_qk, u + 1)
                if u + 1 < GLA_STEPS:
                    shifted_gates(u + 1)
                o = OUT_GLA["intra", u]
                wait_made(dve, o)
                take(dve.tensor_tensor(a_t[:, :, :], bank(o).rearrange("p (b c) -> p b c", b=4),
                                       intra_mask[:, d:d + 1, :].to_broadcast([P, 4, P]), ALU.mult), o)
                o = OUT_GLA["added", u]
                for i in range(NCH - 1):
                    n = chunk_cols(d, i)
                    source = o + i % 2 + 2 * (i // 8)
                    if i % 8 < 2:
                        wait_made(dve, o + 1 + 2 * (i // 8))
                    out = state_c[:, i, :] if i < 3 else state[:, i - 3, :]
                    new = bank(source)[:, P * (i % 8 // 2):P * (i % 8 // 2) + P]
                    if i == 0:
                        link(dve.tensor_copy(out, new))
                        continue
                    before = state_c[:, i - 1, :] if i < 4 else state[:, i - 4, :]
                    ins = dve.scalar_tensor_tensor(out=out, in0=before, scalar=chunk_decay[:, n:n + 1], in1=new,
                                                   op0=ALU.mult, op1=ALU.add)
                    if i % 8 >= 6 or i >= NCH - 3:
                        take(ins, source)
                    else:
                        link(ins)
                own(dve.tensor_copy(state_c[:, 3, 0:1], state[:, 7, 0:1]), gla_s, u + 1)
                if u + 1 < GLA_STEPS:
                    if d == 0 and 0 < h < GH - 1:
                        head_output(h - 1)
                    decays(u + 1)
                    if u == 0:
                        low_rank_keys()
                    if u == 1:
                        low_rank_queries()
                    if d == 0 and 0 < h < GH - 1:
                        head_output_low(h - 1)
                    decayed_keys(u + 1)
            om = [t[:, :, :].rearrange("p k t -> p (k t)") for t in (om_hi, om_lo)]
            for k in range(QL):
                dve.wait_ge(lr_hi, k + 1)
                if k == QL - 1:
                    dve.wait_ge(gla_o, GLA_STEPS)
                own(dve.tensor_tensor(om[1][:, T * k:T * k + T], z_q[:, k, :], om[0][:, T * k:T * k + T].bitcast(F32),
                                      ALU.subtract), lr_lo, k + 1)
            head_output(GH - 2)
            head_output_low(GH - 2)
            for h in range(HEADS):
                o = OUT_QH + h
                wait_made(dve, o)
                b = bank(o)
                link(dve.tensor_tensor(square[64:96, 0, :], b[96:P, :], rope[96:P, :], ALU.mult))
                link(dve.tensor_tensor(q_t[64:96, h, :], b[64:96, :], rope[64:96, :], ALU.mult))
                dve.wait_ge(q_copied, h + 1)
                take(dve.tensor_tensor(q_t[64:96, h, :], q_t[64:96, h, :], square[64:96, 0, :], ALU.add), o)
            wait_made(dve, OUT_KH - 1)
            for k in range(KVL):
                dve.wait_ge(lr_hi, QL + k + 1)
                own(dve.tensor_tensor(kv_lo[:, k, :], z_kv[:, k, :], kv_hi[:, k, :].bitcast(F32),
                                      ALU.subtract), lr_lo, QL + k + 1)
            for h in range(HEADS):
                ins = dve.tensor_copy(k_t[64:96, h, :], k_rope)
            own(ins, k_spread, 1)
            head_output(GH - 1)
            head_output_low(GH - 1)

            def probs(u):
                o, st = out_scores(u), att_stat[:, u % 2, :]
                wait_made(dve, o + 1)
                both_banks = acc[:, o % BANKS:o % BANKS + 2, :].rearrange("p b t -> p (b t)")[:, 0:TC]
                link(dve.tensor_reduce(st[:, 0:1], both_banks, AX.X, ALU.max))
                own(dve.tensor_scalar(st[:, 1:2], st[:, 0:1], -MLA_SCALE, None, ALU.mult), att_max, u + 1)

            def normalised(u):
                o, st = out_scores(u), att_stat[:, u % 2, :]
                wait_taken(dve, o)
                wait_taken(dve, o + 1)
                link(dve.tensor_tensor(st[:, 4:5], st[:, 2:3], st[:, 3:4], ALU.add))
                link(dve.reciprocal(st[:, 5:6], st[:, 4:5]))
                own(dve.tensor_scalar(prob[:, u % 2, :], prob[:, u % 2, :], st[:, 5:6], None, ALU.mult), att_prob, u + 1)

            def head_low(h):
                rows = slice(64 * (h % 2), 64 * (h % 2) + 64)
                dve.wait_ge(om_hi_made, h + 1)
                own(dve.tensor_tensor(om_lo[rows, h // 2, :], side[rows, h % 2, :], om_hi[rows, h // 2, :].bitcast(F32),
                                      ALU.subtract), om_lo_made, h + 1)

            wait_taken(dve, OUT_V - 1)
            probs(0)
            probs(1)
            for u in range(UNITS):
                h, qb = u // 4, u % 4
                normalised(u)
                if u + 2 < UNITS:
                    probs(u + 2)
                if qb == 0 and h:
                    head_low(h - 1)
            head_low(HEADS - 1)
            for m in range(KT):
                o = OUT_MERGE + 4 * m
                gm, gg = gate_m[:, m % 2, :], gate_g[:, m % 2, :]
                wait_taken(dve, o + 1)
                wait_made(dve, o + 2)
                take(dve.tensor_tensor(gm, gm, bank(o + 2), ALU.mult), o + 2)
                wait_made(dve, o + 3)
                take(dve.tensor_tensor(gg, gg, bank(o + 3), ALU.mult), o + 3)
                own(dve.tensor_tensor(gm, gm, gg, ALU.add), mg_made, m + 1)
                dve.wait_ge(mg_hi_made, m + 1)
                own(dve.tensor_tensor(mg_lo[:, m, :], gm, mg_hi[:, m, :].bitcast(F32), ALU.subtract), mg_lo_made, m + 1)
            dve.wait_ge(x_in, 16 * 2 * KT)

            def gated_add(o, k, gate):
                wait_made(dve, o)
                take(dve.scalar_tensor_tensor(out=x[:, k, :], in0=bank(o), scalar=mod[:, gate * KT + k, 0:1], in1=x[:, k, :],
                                              op0=ALU.mult, op1=ALU.add), o)

            for k in range(KT + 1):
                if k < KT:
                    gated_add(OUT_MIX + k, k, 2)
                if k:
                    add_up(k - 1, 2)
            rstd_of(2)
            modulated(2, 2 * KT, x, h_hi, h_lo, f2_scaled, f2_full)
            dve.memset(ff_pad[:, :, :, :], 0.0).then_inc(pads_made, 1)

            def up(group):
                for i, j in enumerate(FF1_GROUPS[group]):
                    o = out_ff_up(group) + 2 * i
                    pad, conv = ff_pad[:, j % 2, :, :], ff_conv[:, j % 2, :].rearrange("p (r c) -> p r c", r=GRID_H)
                    wait_taken(dve, o)
                    for tap in range(9):
                        r, c = tap // 3, tap % 3
                        src = pad[:, r:r + GRID_H, c:c + GRID_W]
                        w = col("conv_w", FF1 * tap + j)
                        if tap == 0:
                            ins = dve.tensor_scalar(conv, src, w, col("conv_b", j), ALU.mult, ALU.add)
                        else:
                            ins = dve.scalar_tensor_tensor(out=conv, in0=src, scalar=w, in1=conv, op0=ALU.mult, op1=ALU.add)
                        if tap < 8:
                            link(ins)
                    own(ins, ff_conved, j + 1)
                    dve.wait_ge(ff_gelu, j + 1)
                    wait_made(dve, o + 1)
                    ins = dve.tensor_tensor(ff_hid[:, j % 2, :], bank(o + 1), ff_conv[:, j % 2, :], ALU.mult)
                    take(ins, o + 1)
                    dve.wait_ge(ff_hi_made, j + 1)
                    own(dve.tensor_tensor(ff_lo[:, group % 2, i, :], ff_hid[:, j % 2, :], ff_hi[:, group % 2, i, :].bitcast(F32),
                                          ALU.subtract), ff_lo_made, j + 1)

            up(0)
            up(1)
            for k in range(KT):
                gated_add(out_ff_down(0) + k, k, 5)
            up(2)
            for k in range(KT):
                gated_add(out_ff_down(1) + k, k, 5)
            for k in range(KT + 1):
                if k < KT:
                    gated_add(out_ff_down(2) + k, k, 5)
                if k:
                    add_up(k - 1, 3)
            rstd_of(3)
            for k in range(KT + 1):
                if k < KT:
                    dve.scalar_tensor_tensor(out=x[:, k, :], in0=x[:, k, :], scalar=col("final1", k), in1=rstd[:, :],
                                             op0=ALU.mult, op1=ALU.mult).then_inc(x_normed, 1)
                if k:
                    dve.wait_ge(x_normed, k)
                    feed(k - 1, NORM0)
                    feed_low(k - 1, NORM0, ("norm_mix", 0))

        def load_panel(eng, slot, panel):
            eng.dma_start(w_raw[:, slot, :], io["weights"][panel].rearrange("p t c -> p (t c)")).then_inc(raw_in[slot], 16)

        block = whole.enter_context(nc.Block())

        @block.sync
        def _(sp):
            sp.dma_start(table[:, :], io["table"]).then_inc(const_in, 16)
            sp.dma_start(ones[:, :], io["ones"]).then_inc(const_in, 16)
            sp.dma_start(sgu_mask[:, :], io["sgu_mask"]).then_inc(const_in, 16)
            if start_x:
                for k in range(KT):
                    sp.dma_start(x[:, k, :], io["x"][:, k, :]).then_inc(x_in, 16)
            if start_x:
                for slot in range(SLOTS):
                    load_panel(sp, slot, slot)
            if not start_x:
                first_block_sp(sp, load_panel)
            lead = SLOTS if start_x else LEAD
            turns = (n_panels - lead) // SLOTS
            with sp.Fori(0, turns) as it:
                for slot in range(SLOTS):
                    sp.wait_ge(panel_made, it * SLOTS + (lead - SLOTS + slot + 1))
                    load_panel(sp, slot, it * SLOTS + (lead + slot))
            for n in range(lead + SLOTS * turns, n_panels):
                sp.wait_ge(panel_made, n - SLOTS + 1)
                load_panel(sp, n % SLOTS, n)
            for k in range(KT):
                sp.wait_ge(scaled, k + 1)
                sp.dma_start(io["out"][:, k, :], x[:, k, :]).then_inc(result_out, 16)
            sp.wait_ge(result_out, 16 * KT)

        @block.gpsimd
        def _(pool):
            def high(slot):
                pool.tensor_scalar(w_hi[:, slot, :], w_raw[:, slot, :], 1.0, 1.0, ALU.mult, ALU.mult).then_inc(hi_made, 1)

            def low_then_high(slot, made, landed, used):
                after = (slot + 1) % SLOTS
                if landed is not None:
                    pool.wait_ge(raw_in[after], landed)
                if used is not None:
                    pool.wait_ge(panel_used, used)
                pool.wait_ge(hi_made, made)
                pool.tensor_tensor(w_lo[:, slot, :], w_raw[:, slot, :], w_hi[:, slot, :].bitcast(F32),
                                   ALU.subtract).then_inc(panel_made, 1)
                if landed is not None:
                    high(after)

            pool.wait_ge(raw_in[0], 16)
            high(0)
            for n in range(SLOTS - 1):
                low_then_high(n, n + 1, 16, None)
            first = SLOTS - 1
            turns = (n_panels - 1 - first) // SLOTS
            with pool.Fori(0, turns) as it:
                for j in range(SLOTS):
                    low_then_high((first + j) % SLOTS, it * SLOTS + (first + j + 1), it * 16 + 32, it * SLOTS + (j + 1))
            for n in range(first + SLOTS * turns, n_panels):
                last = n == n_panels - 1
                low_then_high(n % SLOTS, n + 1, None if last else 16 * ((n + 1) // SLOTS + 1), None if last else n + 2 - SLOTS)

        @block.tensor
        def _(pe):
            turn = Turn()
            turn.out = first_out["mix", 0] if start_x else 0
            tile = [0]
            pending = [False]

            def next_tile():
                t = tile[0]
                tile[0] += 1
                slot = t // TP % SLOTS
                if t % TP == 0:
                    pe.wait_ge(panel_made, turn.value(t // TP + 1))
                    pending[0] = t >= TP
                return slot, slice(P * (t % TP), P * (t % TP) + P)

            def mm(out, lhs, rhs, start, stop, group=False):
                ins = pe.matmul(out, lhs, rhs, start=start, stop=stop, skip_group_check=group)
                if pending[0]:
                    ins.then_inc(panel_used, 1)
                    pending[0] = False
                return ins

            def skip_to_panel():
                while tile[0] % TP:
                    tile[0] += 1

            def begin_out():
                o = turn.out
                turn.out += 1
                if o >= BANKS:
                    v = o // BANKS
                    pe.wait_ge(out_taken[o % BANKS], turn.value(v, turn.rate // BANKS))
                return bank(o)

            def project(parts, ready=None):
                out = begin_out()
                for k, (hi, lo) in enumerate(parts):
                    slot, cols = next_tile()
                    if ready:
                        ready(k)
                    last = k == len(parts) - 1
                    mm(out, w_hi[:, slot, cols], hi, k == 0, False)
                    mm(out, w_hi[:, slot, cols], lo, False, False)
                    ins = mm(out, w_lo[:, slot, cols], hi, False, last)
                ins.then_inc(out_made, 1)

            h_parts = [(h_hi[:, k, :], h_lo[:, k, :]) for k in range(KT)]

            def looped(parts, turns=2):
                assert tile[0] % TP == 0 and len(parts) == TP
                with pe.Fori(0, turns) as it:
                    turn.it, turn.rate = it, SLOTS
                    for _ in range(SLOTS):
                        project(parts)
                turn.it = None
                turn.out += SLOTS * (turns - 1)
                tile[0] += SLOTS * TP * (turns - 1)

            def down_in_two(parts, ready):
                outs = []
                for ks in (range(0, HALF), range(HALF, len(parts))):
                    for i in range(BANKS):
                        if ks[0] == 0:
                            outs.append(begin_out())
                        out = outs[i]
                        for k in ks:
                            slot, cols = next_tile()
                            if i == 0:
                                ready(k)
                            hi, lo = parts[k]
                            last = k == len(parts) - 1
                            mm(out, w_hi[:, slot, cols], hi, k == 0, False)
                            mm(out, w_hi[:, slot, cols], lo, False, False)
                            ins = mm(out, w_lo[:, slot, cols], hi, False, last)
                        if last:
                            ins.then_inc(out_made, 1)
                for _ in range(BANKS, KT):
                    project(parts)

            def norm_sum(norm):
                pe.wait_ge(summed, KT * (norm + 1))
                if norm:
                    pe.wait_ge(root_made, norm)
                pe.matmul(stat[:, :], ones[:, :], square_sum[:, :], start=True, stop=True).then_inc(stat_made, 1)

            def ready_h(norm):
                return lambda k: pe.wait_ge(h_lo_made, KT * norm + k + 1 - H_SKIP)

            def recurrent(inst, norm):
                for half in range(2):
                    for m in range(HALF):
                        project(h_parts, ready_h(norm) if half == 0 and m == 0 else None)
                        if half == 0 and m == 0:
                            norm_sum(norm)
                    for m in range(HALF * half, HALF * half + HALF):
                        for gate in range(2):
                            project([(M["rec_hi"][:, k, :], M["rec_lo"][:, k, :]) for k in BD[m]],
                                    lambda i, m=m: pe.wait_ge(rec_lo_made, rec_x_lo(inst, BD[m][i])))
                    skip_to_panel()
                    for m in range(HALF):
                        project(h_parts)
                down_in_two([(M["rec_hi"][:, k, :], M["rec_lo"][:, k, :]) for k in range(RT)],
                            lambda k: pe.wait_ge(rec_lo_made, rec_y_lo(inst, k)))

            def spatial(norm):
                for half in range(2):
                    outs = [begin_out() for _ in range(4)]
                    for k in range(KT):
                        if k % 2 == 0:
                            slot, _ = next_tile()
                            tile[0] += TP - 1
                        if half == 0:
                            pe.wait_ge(h_lo_made, KT * norm + k + 1 - H_SKIP)
                        if half == 0 and k == KT // 2:
                            norm_sum(norm)
                        cols = slice(512 * (k % 2), 512 * (k % 2) + 512)
                        for tb in range(4):
                            tok = slice(P * tb, P * tb + P)
                            mm(outs[tb], h_hi[:, k, tok], w_hi[:, slot, cols], k == 0, False)
                            mm(outs[tb], h_hi[:, k, tok], w_lo[:, slot, cols], False, False)
                            ins = mm(outs[tb], h_lo[:, k, tok], w_hi[:, slot, cols], False, k == KT - 1)
                            if k == KT - 1:
                                ins.then_inc(out_made, 1)
                    if half == 0:
                        pe.wait_ge(rstd_made, norm + 1)
                        for tb in range(4):
                            ins = pe.matmul(side[:, 0, tb:tb + 1], rstd[0:1, P * tb:P * tb + P], ones[0:1, 0:1],
                                            start=True, stop=True)
                        ins.then_inc(sgu_col, 1)
                pe.wait_ge(sgu_masked, 1)
                for kind, g in SPATIAL_ORDER:
                    if kind == "u":
                        project(h_parts)
                        continue
                    out = begin_out()
                    if g == 0:
                        pe.wait_ge(sgu_v_norm, 4)
                    for tb in range(4):
                        ins = pe.matmul(out[:, P * tb:P * tb + P], M["sgu_v"][:, tb, P * g:P * g + P],
                                        M["sgu_w"][:, g, :], start=True, stop=True)
                    ins.then_inc(out_made, 1)
                down_in_two([(M["sgu_hi"][:, k, :], M["sgu_lo"][:, k, :]) for k in range(KT)],
                            lambda k: pe.wait_ge(sgu_lo_made, k + 1))

            def short_conv(norm):
                for m in range(KT):
                    for part in range(3):
                        project(h_parts, ready_h(norm) if m == 0 and part == 0 else None)
                        if m == 0 and part == 0:
                            norm_sum(norm)
                for m in range(KT):
                    project([(M["cnv_hi"][:, k, :], M["cnv_lo"][:, k, :]) for k in range(KT)],
                            (lambda k: pe.wait_ge(cnv_lo_made, k + 1)) if m == 0 else None)

            def mlp(layer, norm):
                for j in range(8):
                    project(h_parts, ready_h(norm) if j == 0 else None)
                    if j == 0:
                        norm_sum(norm)
                for group in range(1, UG + 1):
                    if group < UG:
                        looped(h_parts)
                    pe.wait_ge(hid_lo_made, FF2 * layer + 8 * group)
                    half = (group - 1) % 2
                    looped([(M["hid_hi"][:, half, k, :], M["hid_lo"][:, half, k, :]) for k in range(8)])

            pe.wait_ge(const_in, CONSTS)
            if not start_x:
                first_block_pe(pe, turn, next_tile, mm, begin_out, project, looped, tile, norm_sum, skip_to_panel)
            norm = NORM0
            for layer in range(LAYERS)[:upto]:
                assert turn.out == first_out["mix", layer]
                (lambda n: recurrent(layer // 3, n), spatial, short_conv)[layer % 3](norm)
                assert turn.out == first_out["mlp", layer]
                mlp(layer, norm + 1)
                norm += 2
            norm_sum(norm)

        @block.scalar
        def _(act):
            def feed(k, norm, gain, x_ready, h_free):
                x_ready(k)
                if KT * norm + k >= 2:
                    act.wait_ge(summed, KT * norm + k - 1)
                act.activation(square[:, k % 2, :], x[:, k, :], ACT.Square).then_inc(squared, 1)
                if gain is not None:
                    if k == 0 and h_free:
                        wait_made(act, h_free - 1)
                    act.activation(h_hi[:, k, :], x[:, k, :], ACT.Copy, scale=col(*gain_at(gain, k))).then_inc(h_hi_made, 1)

            def norm_root(norm):
                act.wait_ge(stat_made, norm + 1 - PE_NORMS)
                if norm:
                    act.wait_ge(rstd_made, norm)
                act.activation(root[:, :], stat[:, :], ACT.Sqrt, bias=col("eps"), scale=1.0 / D).then_inc(root_made, 1)

            def recurrent(inst, layer, norm):
                o = first_out["mix", layer]
                act.activation(M["rec_cl"][:, 0, :], table[:, names["a_lambda"] + RT * inst:names["a_lambda"] + RT * inst + RT],
                               ACT.Exp, scale=-1.0).then_inc(rec_cl_exp, 1)
                act.wait_ge(rec_cl_exp, inst + 1)
                act.activation(M["rec_cl"][:, 1, :], M["rec_cl"][:, 0, :], ACT.Ln, bias=col("one")).then_inc(rec_cl_ln, 1)
                norm_root(norm)
                for half in range(2):
                    ms = range(HALF * half, HALF * half + HALF)
                    for m in ms:
                        act.wait_ge(rec_conv, A_TAPS * (RT * inst + m + 1))
                        act.activation(M["rec_hi"][:, m, :], M["rec_x"][:, m, :], ACT.Copy).then_inc(rec_hi_made, 1)
                    o += HALF
                    for i, m in enumerate(ms):
                        if half == 1 or inst == 1:
                            act.wait_ge(rec_y, RT * inst + HALF * half)
                        wait_made(act, o)
                        act.activation(M["rec_a"][:, i, :], bank(o), ACT.Sigmoid,
                                       bias=col("a_gate_a_b", RT * inst + m)).then_inc(out_taken[o % BANKS], 1)
                        wait_made(act, o + 1)
                        act.activation(M["rec_u"][:, i, :], bank(o + 1), ACT.Sigmoid,
                                       bias=col("a_gate_x_b", RT * inst + m)).then_inc(out_taken[(o + 1) % BANKS], 1)
                        o += 2
                    act.wait_ge(rec_cl_made, 2 * inst + 2)
                    done = RT * inst + HALF * half
                    for i, m in enumerate(ms):
                        act.wait_ge(rec_xi_made, done + i + 1)
                        wait_taken(act, o - 2)
                        act.activation(M["rec_u"][:, i, :], M["rec_a"][:, i, :], ACT.Tanh,
                                       scale=M["rec_cl"][:, 2, m:m + 1]).then_inc(rec_tanh, 1)
                        act.wait_ge(rec_tanh, done + i + 1)
                        act.activation(M["rec_a"][:, i, :], M["rec_a"][:, i, :], ACT.Exp,
                                       scale=M["rec_cl"][:, 3, m:m + 1]).then_inc(rec_decay, 1)
                    for i, m in enumerate(ms):
                        act.wait_ge(rec_ratio, 3 * (done + i + 1))
                        act.activation(M["rec_u"][:, i, :], M["rec_u"][:, i, :], ACT.Sqrt, scale=2.0).then_inc(rec_sqrt, 1)
                    for i, m in enumerate(ms):
                        wait_taken(act, o + i)
                        act.activation(M["rec_gate"][:, i, :], M["rec_gate"][:, i, :], ACT.Gelu_apprx_tanh).then_inc(rec_gelu, 1)
                    o += HALF
                    for i, m in enumerate(ms):
                        act.wait_ge(rec_y, done + i + 1)
                        if i == 0:
                            wait_made(act, o - HALF - 1)
                        act.activation(M["rec_hi"][:, m, :], M["rec_u"][:, i, :], ACT.Copy).then_inc(rec_hi_made, 1)

            def spatial(layer, norm):
                o = first_out["mix", layer]
                act.dma_start(M["sgu_w"][:, :, :], io["sgu_w"]).then_inc(sgu_in, 16)
                act.dma_start(M["sgu_bias"][:, :, :], io["sgu_bias"]).then_inc(sgu_in, 16)
                norm_root(norm)
                act.wait_ge(sgu_col_taken, 1)
                for half in range(2):
                    for tb in range(4):
                        wait_made(act, o)
                        act.activation(M["sgu_v"][:, tb, 512 * half:512 * half + 512], bank(o), ACT.Gelu_apprx_tanh,
                                       scale=M["sgu_stat"][:, 0, tb:tb + 1]).then_inc(out_taken[o % BANKS], 1)
                        o += 1
                for tb in range(4):
                    wait_taken(act, o - 4 + tb)
                    if tb:
                        act.wait_ge(sgu_sq_made, tb)
                    act.activation(M["sgu_sq"][:, :], M["sgu_v"][:, tb, :], ACT.Square,
                                   accum_out=M["sgu_stat"][:, 1, tb:tb + 1]).then_inc(sgu_sq_made, 1)
                act.wait_ge(sgu_sq_made, 4)
                act.activation(M["sgu_stat"][:, 2, :], M["sgu_stat"][:, 1, :], ACT.Sqrt, bias=col("eps"),
                               scale=1.0 / D).then_inc(sgu_root, 1)
                for i, (kind, m) in enumerate(SPATIAL_ORDER):
                    if kind == "u":
                        wait_taken(act, o + i)
                        act.activation(M["sgu_u"][:, m, :], M["sgu_u"][:, m, :], ACT.Gelu_apprx_tanh).then_inc(sgu_u_made, 1)
                        continue
                    act.wait_ge(sgu_y_made, m + 1)
                    act.activation(M["sgu_hi"][:, m, :], M["sgu_y"][:, m % 2, :], ACT.Copy).then_inc(sgu_hi_made, 1)

            def short_conv(layer, norm):
                norm_root(norm)
                for m in range(KT):
                    act.wait_ge(cnv_y, m + 1)
                    act.activation(M["cnv_hi"][:, m, :], M["cnv_c"][:, m % 2, :], ACT.Copy).then_inc(cnv_hi_made, 1)

            def hidden(o, j, half, made, turn=None):
                wait_taken(act, o, turn)
                if made >= 4:
                    act.wait_ge(hid_lo_made, turn.value(made - 3) if turn else made - 3)
                act.activation(M["hidden"][:, o % 4, :], M["relu"][:, o % 4, :], ACT.Square)
                act.activation(M["hid_hi"][:, half, j, :] if turn is None else
                               M["hid_hi"][:, half, bass.ds(turn.it * SLOTS + j, 1), :].rearrange("p a t -> p (a t)"),
                               M["relu"][:, o % 4, :], ACT.Square).then_inc(hid_hi_made, 1)

            def mlp(layer, norm):
                o = first_out["mlp", layer]
                norm_root(norm)
                for j in range(8):
                    hidden(o + j, j, 0, FF2 * layer + j)
                o += 8
                turn = Turn()
                for group in range(1, UG):
                    with act.Fori(0, 2) as it:
                        turn.it, turn.rate = it, SLOTS
                        for j in range(SLOTS):
                            hidden(o + j, j, group % 2, FF2 * layer + 8 * group + j, turn)
                    o += 16

            def gain_at(gain, k):
                name, layer = gain
                return name, KT * layer + k

            if start_x:
                act.wait_ge(const_in, CONSTS)
                for k in range(KT):
                    feed(k, NORM0, ("norm_mix", 0), lambda k: act.wait_ge(x_in, 16 * KT), None)
            else:
                first_block_act(act, feed)
            norm = NORM0
            for layer in range(LAYERS)[:upto]:
                (lambda l, n: recurrent(l // 3, l, n), spatial, short_conv)[layer % 3](layer, norm)
                o = mix_down(layer)
                for k in range(KT):
                    feed(k, norm + 1, ("norm_mlp", layer), lambda k: wait_taken(act, o + k), o)
                mlp(layer, norm + 1)
                norm += 2
                o = mlp_down(layer)
                last = layer == len(range(LAYERS)[:upto]) - 1
                for k in range(KT):
                    feed(k, norm, None if last else ("norm_mix", layer + 1), lambda k: wait_taken(act, o + k), o)
            norm_root(norm)

        @block.vector
        def _(dve):
            def feed(k, norm, h=True):
                dve.wait_ge(squared, KT * norm + k + 1)
                if k == 0:
                    if norm > PE_NORMS:
                        dve.wait_ge(stat_made, norm - PE_NORMS)
                    dve.tensor_copy(square_sum[:, :], square[:, 0, :]).then_inc(summed, 1)
                else:
                    dve.wait_ge(summed, KT * norm + k)
                    dve.tensor_tensor(square_sum[:, :], square_sum[:, :], square[:, k % 2, :], ALU.add).then_inc(summed, 1)
                return h

            def feed_low(k, norm, gain):
                name, layer = gain
                dve.wait_ge(h_hi_made, KT * norm + k + 1 - H_SKIP)
                dve.scalar_tensor_tensor(out=h_lo[:, k, :], in0=x[:, k, :], scalar=col(name, KT * layer + k),
                                         in1=h_hi[:, k, :].bitcast(F32), op0=ALU.mult, op1=ALU.subtract).then_inc(h_lo_made, 1)

            def norm_rstd(norm):
                dve.wait_ge(root_made, norm + 1)
                dve.reciprocal(rstd[:, :], root[:, :]).then_inc(rstd_made, 1)
                dve.wait_ge(rstd_made, norm + 1)

            def add_to_x(o, k, turn=None):
                wait_made(dve, o, turn)
                tile = x[:, k, :] if turn is None else x[:, bass.ds(turn.it * SLOTS + k, 1), :].rearrange("p a t -> p (a t)")
                dve.tensor_tensor(tile, bank(o), tile, ALU.add).then_inc(out_taken[o % BANKS], 1)

            def taken(o, turn=None):
                wait_taken(dve, o, turn)

            def split_low(lo, whole_, hi, made_sem):
                dve.tensor_tensor(lo, whole_, hi.bitcast(F32), ALU.subtract).then_inc(made_sem, 1)

            def recurrent(inst, layer, norm):
                o = first_out["mix", layer]
                dve.memset(M["rec_in"][:, :, 0:A_TAPS - 1], 0.0).then_inc(rec_zeroed, 1)
                dve.wait_ge(rec_cl_ln, inst + 1)
                dve.tensor_scalar(M["rec_cl"][:, 2, :], M["rec_cl"][:, 1, :], 8.0, None, ALU.mult).then_inc(rec_cl_made, 1)
                dve.tensor_scalar(M["rec_cl"][:, 3, :], M["rec_cl"][:, 1, :], -8.0, None, ALU.mult).then_inc(rec_cl_made, 1)
                dve.wait_ge(rec_zeroed, inst + 1)
                norm_rstd(norm)
                steps = A_TAPS * RT * inst

                def low_x(m):
                    dve.wait_ge(rec_hi_made, rec_x_lo(inst, m))
                    split_low(M["rec_lo"][:, m, :], M["rec_x"][:, m, :], M["rec_hi"][:, m, :], rec_lo_made)

                for half in range(2):
                    ms = range(HALF * half, HALF * half + HALF)
                    done = RT * inst + HALF * half
                    for m in ms:
                        wait_made(dve, o)
                        if m >= 1:
                            dve.wait_ge(rec_conv, A_TAPS * (RT * inst + m))
                        xin = M["rec_in"][:, m % 3, :]
                        dve.tensor_tensor(xin[:, A_TAPS - 1:], bank(o), rstd[:, :], ALU.mult).then_inc(out_taken[o % BANKS], 1)
                        taken(o)
                        w = [col("a_conv_w", (A_TAPS * inst + j) * RT + m) for j in range(A_TAPS)]
                        dve.tensor_scalar(M["rec_x"][:, m, :], xin[:, 0:T], w[0], col("a_conv_b", RT * inst + m),
                                          ALU.mult, ALU.add).then_inc(rec_conv, 1)
                        for j in range(1, A_TAPS):
                            dve.wait_ge(rec_conv, A_TAPS * (RT * inst + m) + j)
                            dve.scalar_tensor_tensor(out=M["rec_x"][:, m, :], in0=xin[:, j:j + T], scalar=w[j],
                                                     in1=M["rec_x"][:, m, :], op0=ALU.mult, op1=ALU.add).then_inc(rec_conv, 1)
                        o += 1
                        if m > ms[0]:
                            low_x(m - 1)
                    low_x(ms[-1])
                    for i, m in enumerate(ms):
                        taken(o + 1)
                        dve.tensor_tensor(M["rec_x"][:, m, :], M["rec_x"][:, m, :], M["rec_u"][:, i, :],
                                          ALU.mult).then_inc(rec_xi_made, 1)
                        o += 2

                    def take_gate(i):
                        wait_made(dve, o + i)
                        if i == 0 and done:
                            dve.wait_ge(rec_y, done)
                        dve.tensor_tensor(M["rec_gate"][:, i, :], bank(o + i), rstd[:, :], ALU.mult)\
                           .then_inc(out_taken[(o + i) % BANKS], 1)

                    for i in range(HALF):
                        u, spare = M["rec_u"][:, i, :], M["rec_in"][:, i % 2, A_TAPS - 1:]
                        base = 3 * (done + i)
                        dve.wait_ge(rec_decay, done + i + 1)
                        if base:
                            dve.wait_ge(rec_ratio, base)
                        dve.tensor_scalar(spare, u, 1.0, None, ALU.add).then_inc(rec_ratio, 1)
                        dve.wait_ge(rec_ratio, base + 1)
                        dve.reciprocal(spare, spare).then_inc(rec_ratio, 1)
                        dve.wait_ge(rec_ratio, base + 2)
                        dve.tensor_tensor(u, u, spare, ALU.mult).then_inc(rec_ratio, 1)
                        if i >= 1:
                            take_gate(i - 1)
                    take_gate(HALF - 1)
                    for i, m in enumerate(ms):
                        u, a = M["rec_u"][:, i, :], M["rec_a"][:, i, :]
                        base = 2 * (done + i)
                        dve.wait_ge(rec_sqrt, done + i + 1)
                        dve.wait_ge(rec_xi_made, done + i + 1)
                        dve.tensor_tensor(M["rec_x"][:, m, :], u, M["rec_x"][:, m, :], ALU.mult).then_inc(rec_scan, 1)
                        dve.wait_ge(rec_scan, base + 1)
                        dve.tensor_tensor_scan(u, a, M["rec_x"][:, m, :], 0.0, ALU.mult, ALU.add).then_inc(rec_scan, 1)
                        dve.wait_ge(rec_scan, base + 2)
                        dve.wait_ge(rec_gelu, done + i + 1)
                        dve.tensor_tensor(u, u, M["rec_gate"][:, i, :], ALU.mult).then_inc(rec_y, 1)
                    o += HALF
                    for i, m in enumerate(ms):
                        dve.wait_ge(rec_y, done + i + 1)
                        dve.wait_ge(rec_hi_made, hi_count(inst, half, i))
                        split_low(M["rec_lo"][:, m, :], M["rec_u"][:, i, :], M["rec_hi"][:, m, :], rec_lo_made)
                return o

            def hi_count(inst, half, i):
                return 2 * RT * inst + 2 * HALF * half + HALF + i + 1

            def spatial(layer, norm):
                o = first_out["mix", layer]
                dve.wait_ge(sgu_in, 32)
                for g in range(SG):
                    dve.tensor_tensor(M["sgu_w"][:, g, :], M["sgu_w"][:, g, :], sgu_mask[:, :], ALU.mult)\
                       .then_inc(sgu_masked if g == SG - 1 else sgu_norm, 1)
                norm_rstd(norm)
                dve.wait_ge(sgu_col, 1)
                dve.tensor_copy(M["sgu_stat"][:, 0, :], side[:, 0, 0:4]).then_inc(sgu_col_taken, 1)
                o += 8
                dve.wait_ge(sgu_root, 1)
                dve.reciprocal(M["sgu_stat"][:, 3, :], M["sgu_stat"][:, 2, :]).then_inc(sgu_norm, 1)
                dve.wait_ge(sgu_norm, SG)
                for tb in range(4):
                    dve.tensor_scalar(M["sgu_v"][:, tb, :], M["sgu_v"][:, tb, :], M["sgu_stat"][:, 3, tb:tb + 1], None,
                                      ALU.mult).then_inc(sgu_v_norm, 1)
                for kind, g in SPATIAL_ORDER:
                    if kind == "u":
                        wait_made(dve, o)
                        dve.tensor_tensor(M["sgu_u"][:, g, :], bank(o), rstd[:, :], ALU.mult).then_inc(out_taken[o % BANKS], 1)
                        o += 1
                        continue
                    y = M["sgu_y"][:, g % 2, :]
                    wait_made(dve, o)
                    if g >= 1:
                        dve.wait_ge(sgu_lo_made, g)
                    for tb in range(4):
                        ins = dve.scalar_tensor_tensor(out=y[:, P * tb:P * tb + P], in0=bank(o)[:, P * tb:P * tb + P],
                                                       scalar=col("b_norm_g", g), in1=M["sgu_bias"][:, g, :],
                                                       op0=ALU.mult, op1=ALU.add)
                    ins.then_inc(out_taken[o % BANKS], 1)
                    taken(o)
                    dve.wait_ge(sgu_u_made, g + 1)
                    dve.tensor_tensor(y, y, M["sgu_u"][:, g, :], ALU.mult).then_inc(sgu_y_made, 1)
                    dve.wait_ge(sgu_y_made, g + 1)
                    dve.wait_ge(sgu_hi_made, g + 1)
                    split_low(M["sgu_lo"][:, g, :], y, M["sgu_hi"][:, g, :], sgu_lo_made)
                    o += 1
                return o

            def short_conv(layer, norm):
                o = first_out["mix", layer]
                dve.memset(M["cnv_p"][:, :, 0:C_TAPS - 1], 0.0).then_inc(cnv_zeroed, 1)
                norm_rstd(norm)
                dve.wait_ge(cnv_zeroed, 1)
                for m in range(KT):
                    s = m % 2
                    g, c, p, b, xv = (M[n][:, s, :] for n in ("cnv_g", "cnv_c", "cnv_p", "cnv_b", "cnv_x"))
                    if m:
                        dve.wait_ge(cnv_lo_made, m)
                    wait_made(dve, o)
                    dve.tensor_tensor(g, bank(o), rstd[:, :], ALU.mult).then_inc(out_taken[o % BANKS], 1)
                    taken(o)
                    wait_made(dve, o + 1)
                    dve.tensor_tensor(xv, bank(o + 1), rstd[:, :], ALU.mult).then_inc(out_taken[(o + 1) % BANKS], 1)
                    taken(o + 1)
                    n0 = (C_TAPS + 1) * m
                    dve.tensor_tensor(p[:, C_TAPS - 1:], xv, g, ALU.mult).then_inc(cnv_step, 1)
                    dve.wait_ge(cnv_step, n0 + 1)
                    w = [col("c_conv_w", KT * j + m) for j in range(C_TAPS)]
                    dve.tensor_scalar(c, p[:, 0:T], w[0], None, ALU.mult).then_inc(cnv_step, 1)
                    for j in range(1, C_TAPS):
                        dve.wait_ge(cnv_step, n0 + 1 + j)
                        dve.scalar_tensor_tensor(out=c, in0=p[:, j:j + T], scalar=w[j], in1=c,
                                                 op0=ALU.mult, op1=ALU.add).then_inc(cnv_step, 1)
                    wait_made(dve, o + 2)
                    dve.tensor_tensor(b, bank(o + 2), rstd[:, :], ALU.mult).then_inc(out_taken[(o + 2) % BANKS], 1)
                    taken(o + 2)
                    dve.wait_ge(cnv_step, n0 + 1 + C_TAPS)
                    dve.tensor_tensor(c, c, b, ALU.mult).then_inc(cnv_y, 1)
                    dve.wait_ge(cnv_y, m + 1)
                    dve.wait_ge(cnv_hi_made, m + 1)
                    split_low(M["cnv_lo"][:, m, :], c, M["cnv_hi"][:, m, :], cnv_lo_made)
                    o += 3
                return o

            def hidden(o, j, half, made, turn=None):
                wait_made(dve, o, turn)
                if made:
                    dve.wait_ge(hid_lo_made, turn.value(made) if turn else made)
                dve.scalar_tensor_tensor(out=M["relu"][:, o % 4, :], in0=bank(o), scalar=0.0, in1=rstd[:, :],
                                         op0=ALU.max, op1=ALU.mult).then_inc(out_taken[o % BANKS], 1)
                dve.wait_ge(hid_hi_made, turn.value(made + 1) if turn else made + 1)
                if turn is None:
                    hi, lo = M["hid_hi"][:, half, j, :], M["hid_lo"][:, half, j, :]
                else:
                    hi, lo = (M[n][:, half, bass.ds(turn.it * SLOTS + j, 1), :].rearrange("p a t -> p (a t)")
                              for n in ("hid_hi", "hid_lo"))
                split_low(lo, M["hidden"][:, o % 4, :], hi, hid_lo_made)

            def mlp(layer, norm):
                o = first_out["mlp", layer]
                norm_rstd(norm)
                for j in range(8):
                    hidden(o + j, j, 0, FF2 * layer + j)
                o += 8
                turn = Turn()
                for group in range(1, UG + 1):
                    if group < UG:
                        with dve.Fori(0, 2) as it:
                            turn.it, turn.rate = it, SLOTS
                            for j in range(SLOTS):
                                hidden(o + j, j, group % 2, FF2 * layer + 8 * group + j, turn)
                        o += 8
                        dve.wait_ge(hid_lo_made, FF2 * layer + 8 * (group + 1))
                        with dve.Fori(0, 2) as it:
                            turn.it = it
                            for k in range(SLOTS):
                                add_to_x(o + k, k, turn)
                        o += 8
                taken(o - 1)
                return o

            def add_and_feed(o, norm, gain):
                for k in range(KT + 1):
                    if k < KT:
                        add_to_x(o + k, k)
                    if k:
                        feed(k - 1, norm)
                        if gain is not None:
                            feed_low(k - 1, norm, gain)

            dve.wait_ge(const_in, CONSTS)
            if start_x:
                dve.wait_ge(x_in, 16 * KT)
                for k in range(KT):
                    feed(k, NORM0)
                    feed_low(k, NORM0, ("norm_mix", 0))
            else:
                first_block_dve(dve, feed, feed_low)
            norm = NORM0
            for layer in range(LAYERS)[:upto]:
                o = (lambda l, n: recurrent(l // 3, l, n), spatial, short_conv)[layer % 3](layer, norm)
                assert o == mix_down(layer)
                add_and_feed(o, norm + 1, ("norm_mlp", layer))
                o = mlp(layer, norm + 1)
                assert o == mlp_down(layer)
                norm += 2
                last = layer == len(range(LAYERS)[:upto]) - 1
                add_and_feed(o, norm, None if last else ("norm_mix", layer + 1))
            norm_rstd(norm)
            for k in range(KT):
                dve.scalar_tensor_tensor(out=x[:, k, :], in0=x[:, k, :], scalar=col("last_g", k), in1=rstd[:, :],
                                         op0=ALU.mult, op1=ALU.mult).then_inc(scaled, 1)


def panels_by_column(w, k0, kt, m):
    return w[P * k0:P * (k0 + kt), P * m:P * (m + 1)].reshape(kt, P, P)


def packed(tiles):
    n = len(tiles)
    pad = -n % TP
    if pad:
        tiles = np.concatenate([tiles, np.zeros((pad, P, P), tiles.dtype)])
    return tiles.reshape(-1, TP, P, P).transpose(0, 2, 1, 3)


def moving(w, k0, kt, c0, cols):
    part = w[P * k0:P * (k0 + kt), c0:c0 + cols]
    return part.reshape(kt, P, cols // P, P).transpose(0, 2, 1, 3).reshape(-1, P, P)


def block_diagonal(gate_w, m, k):
    tile = np.zeros((P, P), gate_w.dtype)
    for h in range(gate_w.shape[0]):
        r0, r1 = max(80 * h, P * k), min(80 * h + 80, P * k + P)
        c0, c1 = max(80 * h, P * m), min(80 * h + 80, P * m + P)
        if r0 < r1 and c0 < c1:
            tile[r0 - P * k:r1 - P * k, c0 - P * m:c1 - P * m] = gate_w[h, r0 - 80 * h:r1 - 80 * h, c0 - 80 * h:c1 - 80 * h]
    return tile


def down_tiles(w, kt):
    order = [(k0, k1 - k0, m) for k0, k1 in ((0, HALF), (HALF, kt)) for m in range(BANKS)]
    order += [(0, kt, m) for m in range(BANKS, KT)]
    return np.concatenate([panels_by_column(w, *part) for part in order])


def second_block_panels(g):
    out = []
    for layer in range(LAYERS):
        kind, j = layer % 3, layer // 3
        if kind == 0:
            w_in, w_out = g["a_w_in_2"][j], g["a_w_out_2"][j]
            for half in range(2):
                ms = range(HALF * half, HALF * half + HALF)
                for m in ms:
                    out.append(packed(panels_by_column(w_in, 0, KT, RT + m)))
                tiles = [block_diagonal(g[n][j], m, k) for m in ms for n in ("a_gate_a_w_2", "a_gate_x_w_2") for k in BD[m]]
                out.append(packed(np.stack(tiles)))
                for m in ms:
                    out.append(packed(panels_by_column(w_in, 0, KT, m)))
            out.append(packed(down_tiles(w_out, RT)))
        elif kind == 1:
            w_in, w_out = g["b_w_in_2"][j], g["b_w_out_2"][j]
            for half in range(2):
                for k in range(0, KT, 2):
                    out.append(packed(moving(w_in, k, 2, D + 512 * half, 512)))
            for m in range(KT):
                out.append(packed(panels_by_column(w_in, 0, KT, m)))
            out.append(packed(down_tiles(w_out, KT)))
        else:
            w_in, w_out = g["c_w_in_2"][j], g["c_w_out_2"][j]
            for m in range(KT):
                for part in (1, 2, 0):
                    out.append(packed(panels_by_column(w_in, 0, KT, KT * part + m)))
            for m in range(KT):
                out.append(packed(panels_by_column(w_out, 0, KT, m)))
        w1, w2 = g["mlp_w1_2"][layer], g["mlp_w2_2"][layer]
        up = [packed(panels_by_column(w1, 0, KT, m)) for m in range(FF2)]
        for group in range(UG + 1):
            if group < UG:
                out += up[8 * group:8 * group + 8]
            if group:
                out += [packed(panels_by_column(w2, 8 * (group - 1), 8, m)) for m in range(KT)]
    return out


def features(a):
    return np.asarray(a).reshape(-1, P).T


def second_table(g):
    return {
        "norm_mix": features(g["norm_mix_g_2"]), "norm_mlp": features(g["norm_mlp_g_2"]),
        "last_g": features(g["final_norm_g_2"]), "a_conv_w": features(g["a_conv_w_2"]),
        "a_conv_b": features(g["a_conv_b_2"]), "a_gate_a_b": features(g["a_gate_a_b_2"]),
        "a_gate_x_b": features(g["a_gate_x_b_2"]), "a_lambda": features(g["a_lambda_2"]),
        "b_norm_g": features(g["b_norm_g_2"]), "c_conv_w": features(g["c_conv_w_2"]),
        "eps": np.full((P, 1), EPS, np.float32), "one": np.ones((P, 1), np.float32),
    }


def second_constants(g):
    w_s, bias = g["b_w_s_2"][0], g["b_s_bias_2"][0]
    s = np.arange(P)
    return {
        "ones": np.ones((P, P), np.float32),
        "sgu_mask": (s[:, None] <= s[None, :]).astype(np.float32),
        "sgu_w": w_s.transpose(2, 0, 1), "sgu_bias": np.broadcast_to(bias[None], (P, SG, P)),
    }


def input_columns(w_in):
    sizes = {"q": 384, "kv": 256, "rope": ROPE, "gq": 512, "gk": 512, "gv": 512, "gr": 512, "glow": 32, "gates": 2 * D}
    out, at = {}, 0
    for name, size in sizes.items():
        out[name] = w_in[:, at:at + size]
        at += size
    return out


PARTNER = np.array([16 * (r // 16) + (r + 8) % 16 for r in range(ROPE)])


def first_block_panels(g):
    w = input_columns(g["w_in"][0])
    zero = np.zeros((D, 16), w["q"].dtype)
    misc = np.concatenate([w["glow"][:, :16], zero, w["glow"][:, 16:], zero, w["rope"], w["rope"][:, PARTNER]], 1)
    out = [packed(panels_by_column(w["q"], 0, KT, m)) for m in range(QL)]
    out += [packed(panels_by_column(w["g" + name], 0, KT, h)) for name, h in AHEAD]
    out.append(packed(panels_by_column(misc, 0, KT, 0)))
    out += [packed(panels_by_column(w["kv"], 0, KT, m)) for m in range(KVL)]
    out += [packed(moving(w["gv"], k, 2, 0, GH * P)) for k in range(0, KT, 2)]
    out += [packed(panels_by_column(w["g" + name], 0, KT, h)) for name, h, _ in gla_order() if name in ("k", "q", "r")]
    uq = g["w_uq"][0].reshape(QL * P, HEADS, QK)
    uq = np.concatenate([uq, uq[:, :, NOPE + PARTNER]], 2).reshape(QL * P, HEADS * P)
    out.append(packed(np.concatenate([panels_by_column(uq, 0, QL, h) for h in range(HEADS)])))
    ukv = g["w_ukv"][0].reshape(KVL * P, HEADS, 2, 64)
    uk, uv = (ukv[:, :, i].reshape(KVL * P, HEADS * 64) for i in range(2))
    out.append(packed(np.concatenate([panels_by_column(uk, 0, KVL, m) for m in range(HEADS // 2)])))
    out.append(packed(moving(uv, 0, KVL, 0, HEADS * 64)))
    for m in range(KT):
        out += [packed(panels_by_column(w["gates"], 0, KT, i * KT + m)) for i in range(2)]
        out.append(packed(np.concatenate([panels_by_column(g[n][0], 0, 4, m) for n in ("w_br_mla", "w_br_gla")])))
    out += [packed(panels_by_column(g["w_out"][0], 0, KT, m)) for m in range(KT)]

    def up(group):
        return [packed(panels_by_column(g["w_up"][0], 0, KT, i * FF1 + j)) for j in FF1_GROUPS[group] for i in (1, 0)]

    def down(group):
        js = FF1_GROUPS[group]
        return [packed(np.concatenate([panels_by_column(g["w_down"][0], js[0], len(js), m) for m in range(KT)]))]

    return out + up(0) + up(1) + down(0) + up(2) + down(1) + down(2)


def first_table(g):
    return {
        "b_ada": features(g["b_ada"]), "norm1": features(g["norm1_g"]), "norm2": features(g["norm2_g"]),
        "q_norm": features(g["q_norm_g"]), "kv_norm": features(g["kv_norm_g"]), "b_decay": features(g["gla_b_decay"]),
        "gla_norm": features(g["gla_norm_g"]), "conv_w": features(g["conv_w"]), "conv_b": features(g["conv_b"]),
        "final1": features(g["final_g"]),
    }


def first_constants(g):
    t = np.arange(T)
    inv_freq = (10000.0 ** (-np.arange(0, 16, 2, dtype=np.float32) / 16)).astype(np.float32)
    place = [(t // GRID_W).astype(np.float32), (t % GRID_W).astype(np.float32)]
    rope = np.zeros((P, T), np.float32)
    for r in range(ROPE):
        angle = place[r // 16] * inv_freq[r % 8]
        rope[64 + r] = np.cos(angle)
        rope[96 + r] = np.sin(angle) * (-1 if r % 16 < 8 else 1)
    s, c = np.arange(P)[:, None], np.arange(P)[None, :]
    same = s // CHUNK == c // CHUNK
    decay_w = np.zeros((48, GH * P), g["gla_w_decay"].dtype)
    decay_w[0:16], decay_w[32:48] = g["gla_w_decay"][0, 0], g["gla_w_decay"][0, 1]
    tiles = lambda a: np.asarray(a).T.reshape(KT, P, -1).transpose(1, 0, 2)
    return {
        "x": tiles(g["x"][0]), "ctx": tiles(g["ctx"][0]),
        "cvec": np.broadcast_to(np.stack([g["c"][0], g["c_ctx"]]), (P, 2, D)),
        "identity": np.eye(P, dtype=np.float32), "rope": rope, "decay_w": decay_w,
        "intra_mask": np.stack([same & (s <= c), same & (s >= c)], 1).astype(np.float32),
        "reset": np.broadcast_to((np.arange(TC + 1) % CHUNK != 0).astype(np.float32), (P, TC + 1)),
        "ada": np.asarray(g["w_ada"][0]).T.reshape(6 * KT, P, D),
    }


def kernel(**inputs):
    import concourse.bacc as bacc
    from concourse.bass_utils import run_bass_kernel_spmd

    g = {name: np.asarray(a) for name, a in inputs.items()}
    columns = first_table(g) | second_table(g)
    names, width = {}, 0
    for name, part in columns.items():
        names[name] = width
        width += part.shape[1]
    names["width"] = width
    data = first_constants(g) | second_constants(g)
    data["table"] = np.concatenate(list(columns.values()), 1)
    data["weights"] = np.concatenate(first_block_panels(g) + second_block_panels(g))
    data = {name: np.ascontiguousarray(a) for name, a in data.items()}

    nc = bacc.Bacc("TRN2", target_bir_lowering=False, num_devices=1)
    io = {name: nc.dram_tensor(f"in_{name}", a.shape, F32, kind="ExternalInput").ap() for name, a in data.items()}
    io["out"] = nc.dram_tensor("out", (P, KT, T), F32, kind="ExternalOutput").ap()
    build(nc, io, names)
    result = run_bass_kernel_spmd(nc, [{f"in_{name}": a for name, a in data.items()}], core_ids=[0])
    out = result.results[0]["out"]
    return np.ascontiguousarray(out.transpose(1, 0, 2).reshape(D, T).T).reshape(1, T, D)
```
